# Optimizing a Trainium2 kernel written in Bass

```python
import math
import jax, jax.numpy as jnp
from jax import lax
import numpy as np

D_MODEL = 1024
BATCH = 1
SEQ = 256
DEPTH = 1

GRID_W = 64
CTX_LEN = 256
N_DA_HEADS = 4
DA_HEAD_DIM = 64
DA_V_DIM = 2 * DA_HEAD_DIM
QK_WIDTH = N_DA_HEADS * 2 * DA_HEAD_DIM
ATTN_WIDTH = N_DA_HEADS * DA_V_DIM
N_FOURIER_GROUPS = 4
FOURIER_GROUP_DIM = 128
FOURIER_WIDTH = N_FOURIER_GROUPS * FOURIER_GROUP_DIM
MIX_WIDTH = ATTN_WIDTH + FOURIER_WIDTH
IN_PROJ_WIDTH = 2 * QK_WIDTH + ATTN_WIDTH + FOURIER_WIDTH
ROPE_THETA = 10000.0
ROPE_AXIS_DIM = DA_HEAD_DIM // 2
Q_BLOCK = 128
N_GROUPS = 4
EXPERTS_PER_GROUP = 8
N_EXPERTS = N_GROUPS * EXPERTS_PER_GROUP
TOP_K = 2
D_EXPERT = 512
MOE_BLOCK = 128
N_MOD = 6
EPS = 1e-6


def rms_norm(x, g):
    xf = x.astype(jnp.float32)
    y = xf * lax.rsqrt(jnp.mean(xf * xf, axis=-1, keepdims=True) + EPS)
    return (y * g.astype(jnp.float32)).astype(x.dtype)

def modulate(h, shift, scale):
    return h * (1 + scale) + shift

def axial_rope_tables(rows, dtype):
    r, col = jnp.meshgrid(jnp.arange(rows), jnp.arange(GRID_W), indexing='ij')
    pos = jnp.stack([r.reshape(-1), col.reshape(-1)], axis=-1).astype(jnp.float32)
    inv_freq = ROPE_THETA ** (-jnp.arange(0, ROPE_AXIS_DIM, 2, dtype=jnp.float32) / ROPE_AXIS_DIM)
    ang = pos[:, :, None] * inv_freq
    ang = jnp.concatenate([ang, ang], axis=-1)
    return jnp.cos(ang).astype(dtype), jnp.sin(ang).astype(dtype)

def apply_axial_rope(x, cos, sin):
    xr = x.reshape(*x.shape[:-1], 2, ROPE_AXIS_DIM)
    x1, x2 = jnp.split(xr, 2, axis=-1)
    rot = jnp.concatenate([-x2, x1], axis=-1)
    c = cos[None, :, None, None]
    s = sin[None, :, None, None]
    return (xr * c + rot * s).reshape(x.shape)

def diff_lambda(lq1, lk1, lq2, lk2, lambda_init):
    f = lambda a: a.astype(jnp.float32)
    return jnp.exp(jnp.sum(f(lq1) * f(lk1))) - jnp.exp(jnp.sum(f(lq2) * f(lk2))) + lambda_init

def diff_attention(q, k, v, lam, g_subln, lambda_init):
    b, n = q.shape[:2]
    nb = n // Q_BLOCK
    qb = jnp.moveaxis(q.reshape(b, nb, Q_BLOCK, *q.shape[2:]), 1, 0)
    scale = DA_HEAD_DIM ** -0.5

    def block(qi):
        s = jnp.einsum('bqhmd,bkhmd->bhmqk', qi, k, preferred_element_type=jnp.float32) * scale
        p = jax.nn.softmax(s, axis=-1)
        a = p[:, :, 0] - lam * p[:, :, 1]
        return jnp.einsum('bhqk,bkhv->bqhv', a.astype(v.dtype), v)

    o = lax.map(block, qb)
    o = jnp.moveaxis(o, 0, 1).reshape(b, n, N_DA_HEADS, DA_V_DIM)
    o = rms_norm(o, g_subln) * (1.0 - lambda_init)
    return o.reshape(b, n, ATTN_WIDTH)

def fourier_mix(f, w_fourier):
    b, n, _ = f.shape
    fg = f.reshape(b, n, N_FOURIER_GROUPS, FOURIER_GROUP_DIM).astype(jnp.float32)
    fr = jnp.fft.fft2(fg, axes=(1, 3), norm='ortho').real.astype(f.dtype)
    return jnp.einsum('bngc,gcd->bngd', fr, w_fourier).reshape(b, n, FOURIER_WIDTH)

def hier_moe(h, w_rg, b_rg, w_re, b_re, w_gate, w_up, w_down):
    t, d = h.shape
    hf = h.astype(jnp.float32)
    g_logits = hf @ w_rg.astype(jnp.float32) + b_rg.astype(jnp.float32)
    grp = jnp.argmax(g_logits, axis=-1)
    p_grp = jnp.take_along_axis(jax.nn.softmax(g_logits, axis=-1), grp[:, None], axis=-1)
    e_logits = (hf @ w_re.astype(jnp.float32) + b_re.astype(jnp.float32)).reshape(t, N_GROUPS, EXPERTS_PER_GROUP)
    e_in = jnp.take_along_axis(e_logits, grp[:, None, None], axis=1)[:, 0]
    top_val, top_idx = lax.top_k(e_in, TOP_K)
    gate = p_grp * jax.nn.softmax(top_val, axis=-1)
    expert = grp[:, None] * EXPERTS_PER_GROUP + top_idx

    n_assign = t * TOP_K
    e_flat = expert.reshape(n_assign).astype(jnp.int32)
    tok_flat = jnp.repeat(jnp.arange(t, dtype=jnp.int32), TOP_K)
    w_flat = gate.reshape(n_assign)
    order = jnp.argsort(e_flat)
    e_sorted = e_flat[order]
    counts = jnp.bincount(e_flat, length=N_EXPERTS).astype(jnp.int32)
    starts = jnp.cumsum(counts) - counts
    padded = (counts + MOE_BLOCK - 1) // MOE_BLOCK * MOE_BLOCK
    pad_ends = jnp.cumsum(padded)
    pad_starts = pad_ends - padded
    dest = pad_starts[e_sorted] + jnp.arange(n_assign, dtype=jnp.int32) - starts[e_sorted]
    n_blocks = -(-n_assign // MOE_BLOCK) + N_EXPERTS
    buf_tok = jnp.full((n_blocks * MOE_BLOCK,), t, jnp.int32).at[dest].set(tok_flat[order])
    buf_w = jnp.zeros((n_blocks * MOE_BLOCK,), h.dtype).at[dest].set(w_flat[order].astype(h.dtype))
    block_expert = jnp.minimum(
        jnp.searchsorted(pad_ends, jnp.arange(n_blocks, dtype=jnp.int32) * MOE_BLOCK, side='right'),
        N_EXPERTS - 1)
    h_pad = jnp.concatenate([h, jnp.zeros((1, d), h.dtype)], axis=0)

    def expert_block(args):
        tok, wt, e = args
        xb = h_pad[tok]
        y = (jax.nn.silu(xb @ w_gate[e]) * (xb @ w_up[e])) @ w_down[e]
        return y * wt[:, None]

    ys = lax.map(expert_block, (buf_tok.reshape(n_blocks, MOE_BLOCK),
                                buf_w.reshape(n_blocks, MOE_BLOCK), block_expert))
    out = jnp.zeros((t + 1, d), ys.dtype).at[buf_tok].add(ys.reshape(-1, d))
    return out[:t]

def first_inputs(seed: int = 0) -> dict:
    key = jax.random.key(seed)
    ks = jax.random.split(key, 24)
    f32 = jnp.float32
    nrm = lambda k, shape, std: jax.random.normal(k, shape, f32) * std
    L = DEPTH
    return {
        'x': nrm(ks[0], (BATCH, SEQ, D_MODEL), 1.0),
        'c': nrm(ks[1], (BATCH, D_MODEL), 1.0),
        'ctx': nrm(ks[2], (BATCH, CTX_LEN, D_MODEL), 1.0),
        'c_ctx': nrm(ks[3], (D_MODEL,), 1.0),
        'w_ada': nrm(ks[4], (L, D_MODEL, N_MOD * D_MODEL), 0.5 * D_MODEL ** -0.5),
        'b_ada': nrm(ks[5], (L, N_MOD * D_MODEL), 0.02),
        'g_mix_norm': 1.0 + nrm(ks[6], (L, D_MODEL), 0.02),
        'g_ffn_norm': 1.0 + nrm(ks[7], (L, D_MODEL), 0.02),
        'w_in': nrm(ks[8], (L, D_MODEL, IN_PROJ_WIDTH), D_MODEL ** -0.5),
        'lambda_q1': nrm(ks[9], (L, DA_HEAD_DIM), 0.1),
        'lambda_k1': nrm(ks[10], (L, DA_HEAD_DIM), 0.1),
        'lambda_q2': nrm(ks[11], (L, DA_HEAD_DIM), 0.1),
        'lambda_k2': nrm(ks[12], (L, DA_HEAD_DIM), 0.1),
        'g_subln': 1.0 + nrm(ks[13], (L, DA_V_DIM), 0.02),
        'w_fourier': nrm(ks[14], (L, N_FOURIER_GROUPS, FOURIER_GROUP_DIM, FOURIER_GROUP_DIM), FOURIER_GROUP_DIM ** -0.5),
        'w_out': nrm(ks[15], (L, MIX_WIDTH, D_MODEL), MIX_WIDTH ** -0.5),
        'w_router_group': nrm(ks[16], (L, D_MODEL, N_GROUPS), D_MODEL ** -0.5),
        'b_router_group': nrm(ks[17], (L, N_GROUPS), 0.01),
        'w_router_expert': nrm(ks[18], (L, D_MODEL, N_EXPERTS), D_MODEL ** -0.5),
        'b_router_expert': nrm(ks[19], (L, N_EXPERTS), 0.01),
        'w_gate': nrm(ks[20], (L, N_EXPERTS, D_MODEL, D_EXPERT), D_MODEL ** -0.5),
        'w_up': nrm(ks[21], (L, N_EXPERTS, D_MODEL, D_EXPERT), D_MODEL ** -0.5),
        'w_down': nrm(ks[22], (L, N_EXPERTS, D_EXPERT, D_MODEL), D_EXPERT ** -0.5),
        'g_final': 1.0 + nrm(ks[23], (D_MODEL,), 0.02),
    }

def first_block(x, c, ctx, c_ctx, w_ada, b_ada, g_mix_norm, g_ffn_norm, w_in,
              lambda_q1, lambda_k1, lambda_q2, lambda_k2, g_subln, w_fourier, w_out,
              w_router_group, b_router_group, w_router_expert, b_router_expert,
              w_gate, w_up, w_down, g_final):
    b, s, d = x.shape
    n_ctx = ctx.shape[1]
    ROWS = s // GRID_W
    cos, sin = axial_rope_tables(ROWS, x.dtype)
    o_k = QK_WIDTH
    o_v = 2 * QK_WIDTH
    o_f = 2 * QK_WIDTH + ATTN_WIDTH
    xl, xc = x, ctx
    for l in range(DEPTH):
        last = l == DEPTH - 1
        lambda_init = 0.8 - 0.6 * math.exp(-0.3 * l)
        lam = diff_lambda(lambda_q1[l], lambda_k1[l], lambda_q2[l], lambda_k2[l], lambda_init)
        mod_l = (jax.nn.silu(c) @ w_ada[l] + b_ada[l]).reshape(b, N_MOD, 1, d)
        mod_c = (jax.nn.silu(c_ctx) @ w_ada[l] + b_ada[l]).reshape(N_MOD, d)
        sh1, sc1, gt1, sh2, sc2, gt2 = (mod_l[:, i] for i in range(N_MOD))
        csh1, csc1, cgt1, csh2, csc2, cgt2 = (mod_c[i] for i in range(N_MOD))
        wl = w_in[l]
        moe_args = (w_router_group[l], b_router_group[l], w_router_expert[l], b_router_expert[l],
                    w_gate[l], w_up[l], w_down[l])

        hl = modulate(rms_norm(xl, g_mix_norm[l]), sh1, sc1)
        pl = hl @ wl
        ql = apply_axial_rope(pl[..., :o_k].reshape(b, s, N_DA_HEADS, 2, DA_HEAD_DIM), cos, sin)
        kl = apply_axial_rope(pl[..., o_k:o_v].reshape(b, s, N_DA_HEADS, 2, DA_HEAD_DIM), cos, sin)
        vl = pl[..., o_v:o_f].reshape(b, s, N_DA_HEADS, DA_V_DIM)
        fl = pl[..., o_f:]

        hc = modulate(rms_norm(xc, g_mix_norm[l]), csh1, csc1)
        pc_kv = hc @ wl[:, o_k:o_f]
        kc = pc_kv[..., :QK_WIDTH].reshape(b, n_ctx, N_DA_HEADS, 2, DA_HEAD_DIM)
        vc = pc_kv[..., QK_WIDTH:].reshape(b, n_ctx, N_DA_HEADS, DA_V_DIM)

        k_all = jnp.concatenate([kc, kl], axis=1)
        v_all = jnp.concatenate([vc, vl], axis=1)
        mix_l = jnp.concatenate([diff_attention(ql, k_all, v_all, lam, g_subln[l], lambda_init),
                                 fourier_mix(fl, w_fourier[l])], axis=-1)
        xl = xl + gt1 * (mix_l @ w_out[l])
        h2l = modulate(rms_norm(xl, g_ffn_norm[l]), sh2, sc2)

        if last:
            xl = xl + gt2 * hier_moe(h2l.reshape(b * s, d), *moe_args).reshape(b, s, d)
        else:
            qc = (hc @ wl[:, :o_k]).reshape(b, n_ctx, N_DA_HEADS, 2, DA_HEAD_DIM)
            fc = hc @ wl[:, o_f:]
            mix_c = jnp.concatenate([diff_attention(qc, kc, vc, lam, g_subln[l], lambda_init),
                                     fourier_mix(fc, w_fourier[l])], axis=-1)
            xc = xc + cgt1 * (mix_c @ w_out[l])
            h2c = modulate(rms_norm(xc, g_ffn_norm[l]), csh2, csc2)
            y = hier_moe(jnp.concatenate([h2l.reshape(b * s, d), h2c.reshape(b * n_ctx, d)], axis=0), *moe_args)
            xl = xl + gt2 * y[:b * s].reshape(b, s, d)
            xc = xc + cgt2 * y[b * s:].reshape(b, n_ctx, d)
    return rms_norm(xl, g_final)


DEPTH_2 = 2

N_MIXERS = 4
D_FF = 2816
REL_BUCKETS = 32
REL_MAX_DIST = 2048
REL_HEADS = 8
A_HEADS = 8
A_HEAD_DIM = D_MODEL // A_HEADS
IDX_HEADS = 8
IDX_DIM = 64
TOPK_MAX = 256
A_SPLITS = (D_MODEL, 2 * D_MODEL, 3 * D_MODEL,
            3 * D_MODEL + IDX_HEADS * IDX_DIM,
            3 * D_MODEL + IDX_HEADS * IDX_DIM + IDX_DIM)
A_IN = 3 * D_MODEL + IDX_HEADS * IDX_DIM + IDX_DIM + IDX_HEADS
B_CHUNK = 128
B_HALF = 3 * D_MODEL
B_GROUPS = 8
C_KERNEL = 31
D_PAIRS = ((128, 1), (512, 4), (2048, 16))
D_NGROUPS = len(D_PAIRS)
D_HEADS = 8
D_HEAD_DIM = 64
D_BLOCK = 128
D_SPAN = D_BLOCK * max(dil for _, dil in D_PAIRS)
D_IN = 3 * D_NGROUPS * D_HEADS * D_HEAD_DIM
D_OUT = D_HEADS * D_HEAD_DIM

def n_uses(m):
    return (DEPTH_2 - m + N_MIXERS - 1) // N_MIXERS


def rmsnorm(x, g):
    xf = x.astype(jnp.float32)
    y = xf * lax.rsqrt(jnp.mean(xf * xf, axis=-1, keepdims=True) + EPS)
    return (y * g.astype(jnp.float32)).astype(x.dtype)

def layernorm(x, g, b):
    xf = x.astype(jnp.float32)
    mu = jnp.mean(xf, axis=-1, keepdims=True)
    var = jnp.mean(jnp.square(xf - mu), axis=-1, keepdims=True)
    y = (xf - mu) * lax.rsqrt(var + EPS)
    return (y * g.astype(jnp.float32) + b.astype(jnp.float32)).astype(x.dtype)

def swiglu(x, w_in, w_out):
    gate, up = jnp.split(x @ w_in, 2, axis=-1)
    return (jax.nn.silu(gate) * up) @ w_out

def rel_bucket(dist):
    max_exact = REL_BUCKETS // 2
    d = jnp.maximum(dist, 0)
    df = jnp.maximum(d, 1).astype(jnp.float32)
    large = max_exact + (jnp.log(df / max_exact) / math.log(REL_MAX_DIST / max_exact)
                         * (REL_BUCKETS - max_exact)).astype(jnp.int32)
    large = jnp.minimum(large, REL_BUCKETS - 1)
    return jnp.where(d < max_exact, d, large)

def mixer_a(h, w_in, w_out, rel_table):
    B_, S, _ = h.shape
    q, k, v, qi, ki, wi = jnp.split(h @ w_in, A_SPLITS, axis=-1)
    q = q.reshape(B_, S, A_HEADS, A_HEAD_DIM)
    k = k.reshape(B_, S, A_HEADS, A_HEAD_DIM)
    v = v.reshape(B_, S, A_HEADS, A_HEAD_DIM)
    qi = qi.reshape(B_, S, IDX_HEADS, IDX_DIM)
    wi = wi * (IDX_HEADS ** -0.5)
    top_k = min(TOPK_MAX, S // 4)
    nb = S // Q_BLOCK
    key_pos = jnp.arange(S)
    scale = A_HEAD_DIM ** -0.5
    gather = jax.vmap(lambda arr, ix: arr[ix])

    def block(i):
        start = i * Q_BLOCK
        q_pos = start + jnp.arange(Q_BLOCK)
        qb = lax.dynamic_slice_in_dim(q, start, Q_BLOCK, axis=1)
        qib = lax.dynamic_slice_in_dim(qi, start, Q_BLOCK, axis=1)
        wib = lax.dynamic_slice_in_dim(wi, start, Q_BLOCK, axis=1)
        rel = jax.nn.relu(jnp.einsum('bthd,bsd->bths', qib, ki).astype(jnp.float32) * (IDX_DIM ** -0.5))
        score = jnp.einsum('bth,bths->bts', wib.astype(jnp.float32), rel)
        causal = key_pos[None, :] <= q_pos[:, None]
        score = jnp.where(causal[None], score, -jnp.inf)
        _, idx = lax.top_k(score, top_k)
        valid = idx <= q_pos[None, :, None]
        kg = gather(k, idx)
        vg = gather(v, idx)
        bias = rel_table[rel_bucket(q_pos[None, :, None] - idx)]
        logits = (jnp.einsum('bthe,btkhe->bhtk', qb, kg).astype(jnp.float32) * scale
                  + jnp.transpose(bias, (0, 3, 1, 2)).astype(jnp.float32))
        logits = jnp.where(valid[:, None], logits, -jnp.inf)
        p = jax.nn.softmax(logits, axis=-1)
        o = jnp.einsum('bhtk,btkhe->bthe', p, vg)
        return o.reshape(B_, Q_BLOCK, D_MODEL)

    out = lax.map(block, jnp.arange(nb))
    out = jnp.transpose(out, (1, 0, 2, 3)).reshape(B_, S, D_MODEL).astype(h.dtype)
    return out @ w_out

def mixer_b(h, w_in, b_in, ln_g, ln_b, w_sp, b_sp, w_out):
    B_, S, _ = h.shape
    z = jax.nn.gelu(h @ w_in + b_in)
    u, v = jnp.split(z, 2, axis=-1)
    v = layernorm(v, ln_g, ln_b)
    nc = S // B_CHUNK
    v = v.reshape(B_, nc, B_CHUNK, B_GROUPS, B_HALF // B_GROUPS)
    tri = jnp.tril(jnp.ones((B_CHUNK, B_CHUNK), dtype=bool))
    w = jnp.where(tri[None], w_sp, jnp.zeros((), w_sp.dtype))
    sv = jnp.einsum('gts,bcsgd->bctgd', w, v) + jnp.transpose(b_sp)[None, None, :, :, None]
    y = u * sv.reshape(B_, S, B_HALF)
    return y @ w_out

def mixer_c(h, w_pw1, b_pw1, w_dw, b_dw, ln_g, ln_b, w_pw2, b_pw2):
    a, g = jnp.split(h @ w_pw1 + b_pw1, 2, axis=-1)
    y = a * jax.nn.sigmoid(g)
    y = lax.conv_general_dilated(y, w_dw[:, None, :], window_strides=(1,),
                                 padding=((C_KERNEL - 1, 0),),
                                 dimension_numbers=('NWC', 'WIO', 'NWC'),
                                 feature_group_count=D_MODEL) + b_dw
    y = jax.nn.silu(layernorm(y, ln_g, ln_b))
    return y @ w_pw2 + b_pw2

def dilated_group(q, k, v, window, dil, rel_table):
    B_, Sp, H, E = q.shape
    n = Sp // dil
    nb = n // D_BLOCK

    def to_sub(t):
        t = jnp.swapaxes(t.reshape(B_, n, dil, H, E), 1, 2)
        return t.reshape(B_, dil, nb, D_BLOCK, H, E)

    def band(t):
        prev = jnp.pad(t, ((0, 0), (0, 0), (1, 0), (0, 0), (0, 0), (0, 0)))[:, :, :-1]
        return jnp.concatenate([prev, t], axis=3)

    qs = to_sub(q)
    kb = band(to_sub(k))
    vb = band(to_sub(v))
    steps = window // dil
    p_loc = jnp.arange(D_BLOCK)[:, None]
    j_loc = jnp.arange(2 * D_BLOCK)[None, :]
    m = p_loc + D_BLOCK - j_loc
    in_win = (m >= 0) & (m <= steps)
    first = (jnp.arange(nb) == 0)[:, None, None] & (j_loc < D_BLOCK)[None]
    mask = in_win[None] & ~first
    bias = jnp.transpose(rel_table[rel_bucket(m * dil)], (2, 0, 1)).astype(jnp.float32)
    logits = jnp.einsum('brnqhe,brnkhe->brnhqk', qs, kb).astype(jnp.float32) * (E ** -0.5) + bias
    logits = jnp.where(mask[None, None, :, None], logits, -jnp.inf)
    mx = jnp.max(logits, axis=-1, keepdims=True)
    e = jnp.exp(logits - mx)
    l = jnp.sum(e, axis=-1, keepdims=True)
    o = jnp.einsum('brnhqk,brnkhe->brnqhe', e / l, vb)
    lse = jnp.swapaxes((mx + jnp.log(l))[..., 0], -1, -2)

    def from_sub(t):
        rest = t.shape[4:]
        t = t.reshape((B_, dil, n) + rest)
        return jnp.swapaxes(t, 1, 2).reshape((B_, Sp) + rest)

    return from_sub(o), from_sub(lse)

def mixer_d(h, w_in, w_out, rel_table):
    B_, S, _ = h.shape
    Sp = -(-S // D_SPAN) * D_SPAN
    proj = jnp.pad(h @ w_in, ((0, 0), (0, Sp - S), (0, 0)))
    proj = proj.reshape(B_, Sp, 3, D_NGROUPS, D_HEADS, D_HEAD_DIM)
    outs, lses = [], []
    for g, (window, dil) in enumerate(D_PAIRS):
        o, lse = dilated_group(proj[:, :, 0, g], proj[:, :, 1, g], proj[:, :, 2, g],
                               window, dil, rel_table)
        outs.append(o)
        lses.append(lse)
    alpha = jax.nn.softmax(jnp.stack(lses, 0), axis=0)
    y = jnp.sum(alpha[..., None] * jnp.stack(outs, 0), axis=0)
    y = y[:, :S].reshape(B_, S, D_OUT).astype(h.dtype)
    return y @ w_out

def second_inputs(seed: int = 0) -> dict:
    key = jax.random.key(seed)
    ks = jax.random.split(key, 32)
    nrm = lambda k, shape, s: jax.random.normal(k, shape, jnp.float32) * s
    nA, nB, nC, nD = n_uses(0), n_uses(1), n_uses(2), n_uses(3)
    D = D_MODEL
    return {
        "x": nrm(ks[0], (BATCH, SEQ, D), 1.0),
        "norm_g": 1.0 + nrm(ks[1], (DEPTH_2, 3, D), 0.05),
        "final_g": 1.0 + nrm(ks[2], (D,), 0.05),
        "ffn_w_in": nrm(ks[3], (DEPTH_2, 2, D, 2 * D_FF), D ** -0.5),
        "ffn_w_out": nrm(ks[4], (DEPTH_2, 2, D_FF, D), D_FF ** -0.5),
        "rel_table": nrm(ks[5], (REL_BUCKETS, REL_HEADS), 0.5),
        "a_w_in": nrm(ks[6], (nA, D, A_IN), D ** -0.5),
        "a_w_out": nrm(ks[7], (nA, D, D), D ** -0.5),
        "b_w_in": nrm(ks[8], (nB, D, 2 * B_HALF), D ** -0.5),
        "b_b_in": nrm(ks[9], (nB, 2 * B_HALF), 0.02),
        "b_ln_g": 1.0 + nrm(ks[10], (nB, B_HALF), 0.05),
        "b_ln_b": nrm(ks[11], (nB, B_HALF), 0.02),
        "b_w_sp": nrm(ks[12], (nB, B_GROUPS, B_CHUNK, B_CHUNK), B_CHUNK ** -0.5),
        "b_b_sp": 1.0 + nrm(ks[13], (nB, B_GROUPS, B_CHUNK), 0.05),
        "b_w_out": nrm(ks[14], (nB, B_HALF, D), B_HALF ** -0.5),
        "c_w_pw1": nrm(ks[15], (nC, D, 2 * D), D ** -0.5),
        "c_b_pw1": nrm(ks[16], (nC, 2 * D), 0.02),
        "c_w_dw": nrm(ks[17], (nC, C_KERNEL, D), C_KERNEL ** -0.5),
        "c_b_dw": nrm(ks[18], (nC, D), 0.02),
        "c_ln_g": 1.0 + nrm(ks[19], (nC, D), 0.05),
        "c_ln_b": nrm(ks[20], (nC, D), 0.02),
        "c_w_pw2": nrm(ks[21], (nC, D, D), D ** -0.5),
        "c_b_pw2": nrm(ks[22], (nC, D), 0.02),
        "d_w_in": nrm(ks[23], (nD, D, D_IN), D ** -0.5),
        "d_w_out": nrm(ks[24], (nD, D_OUT, D), D_OUT ** -0.5),
    }

def second_block(x, norm_g, final_g, ffn_w_in, ffn_w_out, rel_table,
              a_w_in, a_w_out,
              b_w_in, b_b_in, b_ln_g, b_ln_b, b_w_sp, b_b_sp, b_w_out,
              c_w_pw1, c_b_pw1, c_w_dw, c_b_dw, c_ln_g, c_ln_b, c_w_pw2, c_b_pw2,
              d_w_in, d_w_out):
    h = x
    for i in range(DEPTH_2):
        kind, j = i % N_MIXERS, i // N_MIXERS
        h = h + 0.5 * swiglu(rmsnorm(h, norm_g[i, 0]), ffn_w_in[i, 0], ffn_w_out[i, 0])
        hn = rmsnorm(h, norm_g[i, 1])
        if kind == 0:
            y = mixer_a(hn, a_w_in[j], a_w_out[j], rel_table)
        elif kind == 1:
            y = mixer_b(hn, b_w_in[j], b_b_in[j], b_ln_g[j], b_ln_b[j], b_w_sp[j], b_b_sp[j], b_w_out[j])
        elif kind == 2:
            y = mixer_c(hn, c_w_pw1[j], c_b_pw1[j], c_w_dw[j], c_b_dw[j], c_ln_g[j], c_ln_b[j],
                        c_w_pw2[j], c_b_pw2[j])
        else:
            y = mixer_d(hn, d_w_in[j], d_w_out[j], rel_table)
        h = h + y
        h = h + 0.5 * swiglu(rmsnorm(h, norm_g[i, 2]), ffn_w_in[i, 1], ffn_w_out[i, 1])
    return rmsnorm(h, final_g)


def setup_inputs(seed=0):
    out = dict(first_inputs(seed))
    for name, value in second_inputs(seed + 1).items():
        if name != "x":
            out[name + "_2"] = value
    return out


def reference(
    x, c, ctx, c_ctx, w_ada, b_ada, g_mix_norm, g_ffn_norm, w_in, lambda_q1, lambda_k1,
    lambda_q2, lambda_k2, g_subln, w_fourier, w_out, w_router_group, b_router_group,
    w_router_expert, b_router_expert, w_gate, w_up, w_down, g_final, norm_g_2, final_g_2,
    ffn_w_in_2, ffn_w_out_2, rel_table_2, a_w_in_2, a_w_out_2, b_w_in_2, b_b_in_2, b_ln_g_2,
    b_ln_b_2, b_w_sp_2, b_b_sp_2, b_w_out_2, c_w_pw1_2, c_b_pw1_2, c_w_dw_2, c_b_dw_2, c_ln_g_2,
    c_ln_b_2, c_w_pw2_2, c_b_pw2_2, d_w_in_2, d_w_out_2,
):
    x = first_block(
        x, c, ctx, c_ctx, w_ada, b_ada, g_mix_norm, g_ffn_norm, w_in, lambda_q1, lambda_k1,
        lambda_q2, lambda_k2, g_subln, w_fourier, w_out, w_router_group, b_router_group,
        w_router_expert, b_router_expert, w_gate, w_up, w_down, g_final,
    )
    return second_block(
        x, norm_g_2, final_g_2, ffn_w_in_2, ffn_w_out_2, rel_table_2, a_w_in_2, a_w_out_2,
        b_w_in_2, b_b_in_2, b_ln_g_2, b_ln_b_2, b_w_sp_2, b_b_sp_2, b_w_out_2, c_w_pw1_2,
        c_b_pw1_2, c_w_dw_2, c_b_dw_2, c_ln_g_2, c_ln_b_2, c_w_pw2_2, c_b_pw2_2, d_w_in_2,
        d_w_out_2,
    )


_drawn_inputs = setup_inputs


def setup_inputs(seed=0):
    import zlib

    import numpy as np

    out = dict(_drawn_inputs(seed))
    spreads = {}
    factors = {'g_mix_norm': 2.755,
     'lambda_q1': 3.524,
     'lambda_k1': 5.768,
     'g_subln': 3.322,
     'b_router_group': 5.204,
     'b_router_expert': 5.559,
     'b_b_in_2': 3.993,
     'b_ln_g_2': 3.439,
     'b_ln_b_2': 8.0,
     'g_ffn_norm': 3.057,
     'b_b_sp_2': 3.297}
    for name, (base, spread) in spreads.items():
        noise = np.random.default_rng([zlib.crc32(name.encode()), seed]).standard_normal(out[name].shape)
        drawn = base * np.exp(spread * noise) if base else spread * noise
        out[name] = __import__('jax').numpy.asarray(drawn.astype(out[name].dtype))
    for name, factor in factors.items():
        out[name] = (out[name] * factor).astype(out[name].dtype)
    return out
```

```python
import math
from contextlib import ExitStack

import numpy as np

import concourse.bass as bass
from concourse import mybir

ALU = mybir.AluOpType
ACT = mybir.ActivationFunctionType
F32 = mybir.dt.float32
AX_X = mybir.AxisListType.X

P = 128
D = 1024
KT = D // P
T = 256
TT = T // P
CTX = 256
EPS = 1e-6
UW = 256
RING = 12
HEADS1, HD1 = 4, 64
NE, DE = 32, 512
FF = 2816
FFC = FF // UW
MOEC = NE * DE // UW
HEADS2 = 8
TOPK = 64
BH = 3072
BT = BH // P
BGROUPS = 8
LAMBDA_INIT = 0.8 - 0.6 * math.exp(-0.3 * 0)
FAR = -1.0e38
TAKEN = -3.0e38

CONSTS = {}
_at = 0
for _name, _w in (("ident", P), ("ones", P), ("rot", P), ("flip", P), ("cos", T), ("sin", T),
                  ("dft_cos", TT * T), ("dft_sin", TT * T), ("dft_ccos", P), ("dft_csin", P),
                  ("causal", TT * T), ("buckets", 512), ("groups", 8)):
    CONSTS[_name] = (_at, _at + _w)
    _at += _w
NCONST = _at

U_ADA1 = 0
U_IN = U_ADA1 + 8
U_ADA2 = U_IN + 8
U_OUT = U_ADA2 + 16
U_MOE = U_OUT + 4
U_F = [U_MOE + 3 * MOEC]
U_A = U_F[0] + 3 * FFC
U_AOUT = U_A + 15
U_F.append(U_AOUT + 4)
U_F.append(U_F[1] + 3 * FFC)
U_B = U_F[2] + 3 * FFC
U_BOUT = U_B + 24
U_F.append(U_BOUT + 12)
C_MOE = 0
C_F = [MOEC + i * FFC for i in range(4)]
LOOP = 4


def gate_unit(u0, ch):
    return u0 if ch == 0 else u0 + 2 + 3 * (ch - 1)


def down_unit(u0, ch, n):
    return u0 + 4 + 3 * ch if ch < n - 1 else u0 + 3 * n - 1


def constants():
    c = np.zeros((P, NCONST), np.float64)

    def put(name, a):
        lo, _ = CONSTS[name]
        c[:a.shape[0], lo:lo + a.shape[1]] = a

    p = np.arange(P)
    put("ident", np.eye(P))
    put("ones", np.ones((P, P)))
    put("flip", np.eye(P)[::-1])
    rot = np.zeros((P, P))
    for i in range(P):
        if i % 32 < 16:
            rot[i + 16, i] = -1.0
        else:
            rot[i - 16, i] = 1.0
    put("rot", rot)
    tok = np.arange(T)
    inv = (np.float32(10000.0) ** (-np.arange(0, 32, 2, dtype=np.float32) / np.float32(32))).astype(np.float32)
    pos = np.stack([tok // 64, tok % 64]).astype(np.float32)
    ang = (pos[(p % 64) // 32] * inv[(p % 32) % 16][:, None]).astype(np.float32)
    put("cos", np.cos(ang.astype(np.float64)))
    put("sin", np.sin(ang.astype(np.float64)))
    n = np.outer(tok, tok) % T
    cn, sn = np.cos(2 * np.pi * n / T), np.sin(2 * np.pi * n / T)
    for t in range(TT):
        lo = CONSTS["dft_cos"][0] + t * T
        c[:, lo:lo + T] = cn[t * P:(t + 1) * P]
        lo = CONSTS["dft_sin"][0] + t * T
        c[:, lo:lo + T] = sn[t * P:(t + 1) * P]
    m = np.outer(p, p) % P
    put("dft_ccos", np.cos(2 * np.pi * m / P) / math.sqrt(T * P))
    put("dft_csin", -np.sin(2 * np.pi * m / P) / math.sqrt(T * P))
    for t in range(TT):
        lo = CONSTS["causal"][0] + t * T
        c[:, lo:lo + T] = np.where(tok[None, :] <= (t * P + p)[:, None], 0.0, FAR)
    dist = np.maximum(T - 1 - np.arange(512), 0)
    large = 16 + (np.log(np.maximum(dist, 1).astype(np.float32) / np.float32(16)) / np.float32(math.log(2048 / 16))
                  * np.float32(16)).astype(np.int32)
    bucket = np.where(dist < 16, dist, np.minimum(large, 31))
    put("buckets", (np.arange(32)[:, None] == bucket[None, :]).astype(np.float64))
    put("groups", np.tile(np.arange(8)[None, :] - 99.0, (P, 1)))
    return c.astype(np.float32)


def build(nc, x, c, ctx, c_ctx, w_ada, b_ada, g_mix_norm, g_ffn_norm, w_in, lambda_q1, lambda_k1,
          lambda_q2, lambda_k2, g_subln, w_fourier, w_out, w_router_group, b_router_group,
          w_router_expert, b_router_expert, w_gate, w_up, w_down, g_final, norm_g_2, final_g_2,
          ffn_w_in_2, ffn_w_out_2, rel_table_2, a_w_in_2, a_w_out_2, b_w_in_2, b_b_in_2, b_ln_g_2,
          b_ln_b_2, b_w_sp_2, b_b_sp_2, b_w_out_2, consts, out):
    stack = ExitStack()
    with stack:
        def sb(name, shape):
            return stack.enter_context(nc.sbuf_tensor(name, shape, F32))

        def sem(name):
            return stack.enter_context(nc.semaphore(name))

        ring = sb("ring", [P, RING, KT * UW])
        xT = sb("xT", [P, KT, T])
        hT = sb("hT", [P, KT, T])
        scr = sb("scr", [P, KT * T])
        gated = sb("gated", [P, 6 * 512])
        con = sb("con", [P, NCONST])
        cols = sb("cols", [P, 2 * P])
        small = sb("small", [P, 352])
        arena = sb("arena", [P, 18432])
        acc = stack.enter_context(nc.psum_tensor("acc", [P, KT, T], F32))
        wk = stack.enter_context(nc.psum_tensor("wk", [P, 4, 512], F32))
        accf = acc[:, :, :].rearrange("p k t -> p (k t)")

        def const(name):
            lo, hi = CONSTS[name]
            return con[:, lo:hi]

        ident, ones, rot, flip = const("ident"), const("ones"), const("rot"), const("flip")
        cosT, sinT = const("cos"), const("sin")
        dft_cos = const("dft_cos").rearrange("p (t n) -> p t n", t=TT)
        dft_sin = const("dft_sin").rearrange("p (t n) -> p t n", t=TT)
        dft_ccos, dft_csin = const("dft_ccos"), const("dft_csin")
        causal = const("causal").rearrange("p (t n) -> p t n", t=TT)
        buckets = const("buckets")
        groups = const("groups")

        used = [0]

        def area(n, at=None):
            if at is None:
                at = used[0]
                used[0] += n
            assert at + n <= 18432, (at, n)
            return arena[:, at:at + n]

        rows1 = scr[:, 0:P]
        rows2 = scr[:, P:2 * P]
        rows3 = scr[:, 2 * P:2 * P + 64]
        ada_b = cols[:, 0:48]
        g_mix = cols[:, 48:56]
        g_ffn = cols[:, 56:64]
        g_fin = cols[:, 64:72]
        norm2 = cols[:, 72:120]
        g_fin2 = cols[:, 120:128]
        c_cols = cols[:, 128:144]
        bu_cols = cols[:, 144:168]
        lng_cols = cols[:, 168:192]
        lnb_cols = cols[:, 192:216]
        sub_col = cols[:, 216:217]
        lam_cols = cols[:, 217:221]
        NR2 = 16 + 24 + 24 + 24 + 1
        s_at = [0]

        def sm(n):
            a = small[:, s_at[0]:s_at[0] + n]
            s_at[0] += n
            assert s_at[0] <= 352
            return a

        csil = sm(16).rearrange("p (k j) -> p k j", j=2)
        mod = sm(96).rearrange("p (m j) -> p m j", j=2)
        a_mix = sm(16).rearrange("p (j k) -> p j k", j=2)
        a_ffn = sm(8)
        eps_col = sm(1)
        lam_prod = sm(2)
        lam_exp = sm(2)
        neg_lam = sm(1)
        sub_g = sm(1)
        std = sb("std", [P, T])
        rstd = sb("rstd", [P, T])

        weights_in = [sem(f"weights_in{i}") for i in range(RING)]
        unit_done = sem("unit_done")
        consts_in, rows_in, x_in, ctx_in = sem("consts_in"), sem("rows_in"), sem("x_in"), sem("ctx_in")
        side_in = sem("side_in")
        dve_step, act_step = sem("dve_step"), sem("act_step")
        const_set = sem("const_set")
        vec_ps, cols_ready, csil_ready = sem("vec_ps"), sem("cols_ready"), sem("csil_ready")
        reldist_sb, reldist_out = sem("reldist_sb"), sem("reldist_out")
        x_ps, ctx_ps, x_ready, ctx_ready = sem("x_ps"), sem("ctx_ps"), sem("x_ready"), sem("ctx_ready")
        lamp_ready, lam_ps, lame_ready, lam_ready = (sem("lamp_ready"), sem("lam_ps"), sem("lame_ready"),
                                                     sem("lam_ready"))
        mod_ready = sem("mod_ready")
        sq_ready, ss_ready, std_ready = sem("sq_ready"), sem("ss_ready"), sem("std_ready")
        h_scaled, h_shifted = sem("h_scaled"), sem("h_shifted")
        grp_ps, grp_out = sem("grp_ps"), sem("grp_out")
        rope_ps, rope_cos, rope_done = sem("rope_ps"), sem("rope_cos"), sem("rope_done")
        sc_ps, max_ready, exp_ready, attn_ready = (sem("sc_ps"), sem("max_ready"), sem("exp_ready"),
                                                   sem("attn_ready"))
        at_ps, at_ready, pv_ps, pv_ready = sem("at_ps"), sem("at_ready"), sem("pv_ps"), sem("pv_ready")
        sub_sq, sub_ss, sub_std, sub_done = sem("sub_sq"), sem("sub_ss"), sem("sub_std"), sem("sub_done")
        resid_ready = sem("resid_ready")
        rt_ps, rt_sb, rt_max, rt_exp, rt_g = sem("rt_ps"), sem("rt_sb"), sem("rt_max"), sem("rt_exp"), sem("rt_g")
        gt_ps, gt_sb, gt_out, gates_in = sem("gt_ps"), sem("gt_sb"), sem("gt_out"), sem("gates_in")
        silu_ready, silw_ready, hidden_ready = sem("silu_ready"), sem("silw_ready"), sem("hidden_ready")
        tail_in, row_ready = sem("tail_in"), sem("row_ready")
        bias_in = sem("bias_in")
        rel_ready, rel_used, mask_ready = sem("rel_ready"), sem("rel_used"), sem("mask_ready")
        a_ps, a_max, a_exp, a_norm = sem("a_ps"), sem("a_max"), sem("a_exp"), sem("a_norm")
        apt_ps, apt_ready, apv_ps, apv_ready = (sem("apt_ps"), sem("apt_ready"), sem("apv_ps"),
                                                sem("apv_ready"))
        wsp_in, wsp_masked, wsp_ps, wsp_ready = (sem("wsp_in"), sem("wsp_masked"), sem("wsp_ps"),
                                                 sem("wsp_ready"))
        w1_ps, w1_ready, binrow_in = sem("w1_ps"), sem("w1_ready"), sem("binrow_in")
        ln_mean, ln_var, ln_std, ln_ready = sem("ln_mean"), sem("ln_var"), sem("ln_std"), sem("ln_ready")
        sp_ps, sp_done = sem("sp_ps"), sem("sp_done")
        fin_ps, fin_sb, out_done = sem("fin_ps"), sem("fin_sb"), sem("out_done")

        reldist_dram = nc.dram_tensor("reldist_dram", (HEADS2, 512), F32, kind="Internal").ap()
        gates_dram = nc.dram_tensor("gates_dram", (NE, T), F32, kind="Internal").ap()

        base1 = area(8192)
        x_rows, c_rows = base1[:, 0:2048], base1[:, 2048:4096]
        cT = base1[:, 4096:6144].rearrange("p (k t) -> p k t", k=KT)
        hcT = base1[:, 6144:8192].rearrange("p (k t) -> p k t", k=KT)
        x_rows = x_rows.rearrange("p (a d) -> p a d", a=TT)
        c_rows = c_rows.rearrange("p (a d) -> p a d", a=TT)
        prob = base1[:, 0:2048].rearrange("p (b m k) -> p b m k", b=2, m=2)
        attn = base1[:, 2048:3072].rearrange("p (b k) -> p b k", b=2)
        attnT = base1[:, 3072:5120].rearrange("p (b k t) -> p b k t", b=2, k=4)
        heads_o = base1[:, 5120:6144].rearrange("p (h t) -> p h t", h=4)
        dft_sb = base1[:, 6144:8192].rearrange("p (g a n) -> p g a n", g=4, a=2)
        mixT = area(2048).rearrange("p (k t) -> p k t", k=KT)
        raw = mixT
        qT = area(1024).rearrange("p (k t) -> p k t", k=4)
        kT = area(2048).rearrange("p (k t) -> p k t", k=4)
        vv = area(2048).rearrange("p (k f) -> p k f", k=4)
        ff = area(1024).rearrange("p (k f) -> p k f", k=2)
        frT = area(1024).rearrange("p (g n) -> p g n", g=4)
        wfo = area(512).rearrange("p (g n) -> p g n", g=4)
        wrt = area(8 * 36).rearrange("p (k n) -> p k n", k=KT)
        brt = area(36)
        gates = arena[:, 0:NE * T].rearrange("p (e t) -> p e t", e=NE)
        lg = arena[:, 8192:8264].rearrange("p (t n) -> p t n", t=2)
        rt = arena[:, 8264:8264 + 512]
        gT = arena[:, 8800:9056]
        gate_row = arena[:, 9088:9600].rearrange("p (b t) -> p b t", b=2)
        used[0] = 0
        qA = area(2048).rearrange("p (k t) -> p k t", k=8)
        kA = area(2048).rearrange("p (k t) -> p k t", k=8)
        vA = area(2048).rearrange("p (k f) -> p k f", k=2)
        qiA = area(1024).rearrange("p (k t) -> p k t", k=4)
        kiA = area(256)
        wiA = area(16).rearrange("p (t h) -> p t h", t=2)
        bias = area(3072).rearrange("p (h j) -> p h j", h=8)
        score = area(512).rearrange("p (t k) -> p t k", t=2)
        amask = area(512).rearrange("p (t k) -> p t k", t=2)
        relb = area(1024).rearrange("p (b k) -> p b k", b=2)
        lgA = area(1024).rearrange("p (b t k) -> p b t k", b=2, t=2)
        prA = area(1024).rearrange("p (b t k) -> p b t k", b=2, t=2)
        ptA = area(1024).rearrange("p (b k t) -> p b k t", b=2, k=2)
        mixA = area(2048).rearrange("p (k t) -> p k t", k=8)
        top8 = area(16).rearrange("p (t k) -> p t k", t=2)
        stA = area(64)
        used[0] = 0
        uB = area(6144).rearrange("p (k t) -> p k t", k=BT)
        vB = area(6144).rearrange("p (t f) -> p t f", t=2)
        wspT = area(1024).rearrange("p (g t) -> p g t", g=8)
        bspb = area(1024).rearrange("p (g t) -> p g t", g=8)
        wsum = area(1024).rearrange("p (g t) -> p g t", g=8)
        wsp = area(1024).rearrange("p (g t) -> p g t", g=8)
        binrow = arena[0:1, 15360:15360 + BH]
        stB = sm(64)
        affB = gated[:, 0:BT * P].rearrange("p (k t) -> p k t", k=BT)
        sqB = scr
        sil = gated[:, 0:1024].rearrange("p (b m t) -> p b m t", b=2, m=2)
        silw = gated[:, 1024:2048].rearrange("p (b m t) -> p b m t", b=2, m=2)
        hid = gated[:, 2048:3072].rearrange("p (b m t) -> p b m t", b=2, m=2)

        spb = scr[:, 0:512].rearrange("p (j t k) -> p j t k", j=2, t=2)
        ropea = scr[:, 0:1024].rearrange("p (b k t) -> p b k t", b=2, k=2)
        ropeb = scr[:, 1024:2048].rearrange("p (b k t) -> p b k t", b=2, k=2)
        stdh, rstdh = gated[:, 0:1024], gated[:, 1024:2048]
        nmax, nbias, sums, rsum = (sm(16).rearrange("p (s m) -> p s m", m=2) for _ in range(4))
        reltab = sb("reltab", [32, HEADS2])
        reldist = scr[0:HEADS2, 512:1024]

        rows2d = lambda v: v.rearrange("(r q) -> r q", q=P)
        ROWS = [(rows1[0:48, :], rows2d(b_ada[0])), (rows1[48:56, :], rows2d(g_mix_norm[0])),
                (rows1[56:64, :], rows2d(g_ffn_norm[0])), (rows1[64:72, :], rows2d(g_final)),
                (rows1[72:120, :], norm_g_2.rearrange("l n (r q) -> (l n r) q", q=P)),
                (rows1[120:128, :], rows2d(final_g_2)),
                (rows2[0:8, :], rows2d(c[0])), (rows2[8:16, :], rows2d(c_ctx)),
                (rows2[16:40, :], rows2d(b_b_in_2[0, 0:BH])), (rows2[40:64, :], rows2d(b_ln_g_2[0])),
                (rows2[64:88, :], rows2d(b_ln_b_2[0])), (rows2[88:89, :], g_subln),
                (rows3[0:1, :], lambda_q1), (rows3[1:2, :], lambda_q2),
                (rows3[2:3, :], lambda_k1), (rows3[3:4, :], lambda_k2), (reltab[:, :], rel_table_2)]
        N_ROWS = len(ROWS)
        SIDE = [(wfo, w_fourier[0].rearrange("g c d -> c g d")),
                (wrt[:, :, 0:4], w_router_group[0].rearrange("(k p) n -> p k n", p=P)),
                (wrt[:, :, 4:36], w_router_expert[0].rearrange("(k p) n -> p k n", p=P)),
                (brt[0:1, 0:4], b_router_group), (brt[0:1, 4:36], b_router_expert)]
        N_SIDE = len(SIDE)

        ada_v = w_ada[0].rearrange("(k p) (u f) -> u p k f", p=P, f=UW)
        in_v = w_in[0].rearrange("(k p) (u f) -> u p k f", p=P, f=UW)
        out_v = w_out[0].rearrange("(k p) (u f) -> u p k f", p=P, f=UW)
        gate_v = w_gate[0].rearrange("e (k p) (u f) -> u e p k f", p=P, f=UW)
        up_v = w_up[0].rearrange("e (k p) (u f) -> u e p k f", p=P, f=UW)
        down_v = w_down[0].rearrange("e (u k p) f -> u e p k f", p=P, k=2)
        ffin_v = [ffn_w_in_2[i // 2, i % 2].rearrange("(k p) (u f) -> u p k f", p=P, f=UW) for i in range(4)]
        ffout_v = [ffn_w_out_2[i // 2, i % 2].rearrange("(u k p) f -> u p k f", p=P, k=2) for i in range(4)]
        aout_v = a_w_out_2[0].rearrange("(k p) (u f) -> u p k f", p=P, f=UW)
        ain_v = a_w_in_2[0].rearrange("(k p) f -> p k f", p=P)
        bin_v = b_w_in_2[0].rearrange("(k p) (u f) -> u p k f", p=P, f=UW)
        bout_v = b_w_out_2[0].rearrange("(u k p) f -> u p k f", p=P, k=2)
        A_UNITS = [3072, 3328, 3584] + [UW * u for u in range(12)]

        def slot_cols(u, w=UW):
            return ring[:, u % RING, 0:KT * w].rearrange("p (k f) -> p k f", k=KT)

        def slot_rows(u):
            return ring[:, u % RING, :].rearrange("p (k f) -> p k f", k=2)

        block = stack.enter_context(nc.Block())

        def swiglu_steps(n):
            return (n - 2) // LOOP, list(range(2 + (n - 2) // LOOP * LOOP, n))

        @block.sync
        def _(sp):
            def fetch(u, dst, src, i=None):
                if u >= RING:
                    need = u - RING + 1
                    sp.wait_ge(unit_done, need if i is None else i * (3 * LOOP) + need)
                sp.dma_start(dst, src).then_inc(weights_in[u % RING], 16)

            def swiglu(u0, n, gate, up, down):
                fetch(u0, slot_cols(u0), gate(0, 0, None))
                fetch(u0 + 1, slot_cols(u0 + 1), up(0, 0, None))

                def step(s, s_static, i):
                    u = u0 + 2 + 3 * (s_static - 1)
                    fetch(u, slot_cols(u), gate(s_static, s, i), i)
                    fetch(u + 1, slot_cols(u + 1), up(s_static, s, i), i)
                    fetch(u + 2, slot_rows(u + 2), down(s_static - 1, s, i), i)
                step(1, 1, None)
                turns, rest = swiglu_steps(n)
                with sp.Fori(0, turns) as i:
                    for j in range(LOOP):
                        step(j, 2 + j, i)
                for s in rest:
                    step(s, s, None)
                u = u0 + 3 * n - 1
                fetch(u, slot_rows(u), down(n - 1, n, None))

            for a in range(8):
                fetch(U_ADA1 + a, slot_cols(U_ADA1 + a), ada_v[a])
            for a in range(8):
                fetch(U_IN + a, slot_cols(U_IN + a), in_v[a])
            for a in range(16):
                fetch(U_ADA2 + a, slot_cols(U_ADA2 + a), ada_v[8 + a])
            for a in range(4):
                fetch(U_OUT + a, slot_cols(U_OUT + a), out_v[a])

            def expert(view):
                def at(ch, _, i):
                    return view[ch % 2, ch // 2 if i is None else i * (LOOP // 2) + ch // 2]
                return at
            swiglu(U_MOE, MOEC, expert(gate_v), expert(up_v), expert(down_v))

            def dense(view, off):
                def at(ch, _, i):
                    return view[off + ch if i is None else i * LOOP + (off + ch)]
                return at

            def feed(n):
                swiglu(U_F[n], FFC, dense(ffin_v[n], 0), dense(ffin_v[n], FFC), dense(ffout_v[n], 0))
            feed(0)
            for a, lo in enumerate(A_UNITS):
                u = U_A + a
                if a == 2:
                    need = u - RING + 1
                    sp.wait_ge(unit_done, need)
                    tail = slot_cols(u, 136)
                    sp.dma_start(tail[:, :, 0:64], ain_v[:, :, lo:lo + 64]).then_inc(weights_in[u % RING], 16)
                    sp.dma_start(tail[:, :, 64:136], ain_v[:, :, lo:lo + 72]).then_inc(tail_in, 16)
                else:
                    fetch(u, slot_cols(u), ain_v[:, :, lo:lo + UW])
            for a in range(4):
                fetch(U_AOUT + a, slot_cols(U_AOUT + a), aout_v[a])
            feed(1)
            feed(2)
            for a in range(24):
                fetch(U_B + a, slot_cols(U_B + a), bin_v[(a + 12) % 24])
            for a in range(12):
                fetch(U_BOUT + a, slot_rows(U_BOUT + a), bout_v[a])
            feed(3)
            for t in range(TT):
                sp.wait_ge(fin_sb, t + 1)
                sp.dma_start(out[0, t * P:(t + 1) * P, :], scr[:, t * D:(t + 1) * D]).then_inc(out_done, 16)
            sp.wait_ge(out_done, 16 * TT)

        @block.tensor
        def _(pe):
            mm = nc.tensor.matmul

            def arrived(u, i=None):
                n = 16 * (u // RING + 1)
                pe.wait_ge(weights_in[u % RING], n if i is None else i * 16 + n)

            def project(dst, w, src):
                for m in range(2):
                    for k in range(KT):
                        last = mm(dst[:, m * T:(m + 1) * T], w[:, k, m * P:(m + 1) * P], src[:, k, :],
                                  start=(k == 0), stop=(k == KT - 1))
                return last

            def project_rows(dst, w, src):
                for t in range(TT):
                    for k in range(KT):
                        last = mm(dst[:, t * UW:(t + 1) * UW], src[:, k, t * P:(t + 1) * P], w[:, k, :],
                                  start=(k == 0), stop=(k == KT - 1))
                return last

            def norm(n, bank):
                pe.wait_ge(sq_ready, n + 1)
                sq = scr[:, :].rearrange("p (k t) -> p k t", k=KT)
                for k in range(KT):
                    last = mm(wk[:, bank, 0:T], ones, sq[:, k, :], start=(k == 0), stop=(k == KT - 1))
                last.then_inc(ss_ready, 1)

            pe.wait_ge(consts_in, 16)
            pe.wait_ge(rows_in, 16 * N_ROWS)
            nc.tensor.transpose(wk[:, 0, 0:P], rows1, ident)
            nc.tensor.transpose(wk[:, 0, P:P + NR2], rows2[0:NR2, :], ident[0:NR2, 0:NR2])
            nc.tensor.transpose(wk[0:64, 0, 256:260], rows3[0:4, :], ident[0:4, 0:4])
            mm(wk[0:HEADS2, 1, :], reltab[:, :], buckets[0:32, :], start=True, stop=True).then_inc(vec_ps, 1)
            pe.wait_ge(x_in, 16)
            for t in range(TT):
                for k in range(KT):
                    last = nc.tensor.transpose(acc[:, k, t * P:(t + 1) * P], x_rows[:, t, k * P:(k + 1) * P], ident)
            last.then_inc(x_ps, 1)
            pe.wait_ge(ctx_in, 16)
            pe.wait_ge(cols_ready, 3)
            pe.wait_ge(reldist_sb, 1)
            wkf = wk[:, :, :].rearrange("p b (c t) -> p (b c) t", t=T)
            for t in range(TT):
                for k in range(KT):
                    last = nc.tensor.transpose(wkf[:, k, t * P:(t + 1) * P], c_rows[:, t, k * P:(k + 1) * P], ident)
            last.then_inc(ctx_ps, 1)

            def ada(u, m0):
                arrived(u)
                for m in range(2):
                    for k in range(KT):
                        last = mm(accf[:, 1024 + 2 * (m0 + m):1024 + 2 * (m0 + m) + 2],
                                  slot_cols(u)[:, k, m * P:(m + 1) * P], csil[:, k, :],
                                  start=(k == 0), stop=(k == KT - 1))
                return last.then_inc(unit_done, 1)

            pe.wait_ge(csil_ready, 1)
            pe.wait_ge(x_ready, 1)
            pe.wait_ge(ctx_ready, 1)
            for a in range(8):
                ada(U_ADA1 + a, 2 * a)
            pe.wait_ge(lamp_ready, 1)
            mm(wk[:, 2, 0:2], ones[0:64, :], lam_prod[0:64, :], start=True, stop=True).then_inc(lam_ps, 1)
            norm(0, 0)
            norm(1, 1)

            g = [0]

            def group(fill, ends_unit=False):
                n = g[0]
                if n >= 4:
                    pe.wait_ge(grp_out, n - 3)
                fill(wk[:, n % 4, :]).then_inc(unit_done if ends_unit else grp_ps, 1)
                g[0] += 1

            pe.wait_ge(h_shifted, 2)
            pe.wait_ge(std_ready, 2)
            pe.wait_ge(lam_ready, 1)

            def unit_groups(u, fills):
                arrived(u)
                for fill in fills[:-1]:
                    group(fill)
                group(fills[-1], ends_unit=True)

            for a in range(2):
                w = slot_cols(U_IN + a)
                unit_groups(U_IN + a, [lambda b: project(b, w, hT)])
            for a in range(2, 4):
                w = slot_cols(U_IN + a)
                unit_groups(U_IN + a, [lambda b: project(b, w, hT), lambda b: project(b, w, hcT)])
            for a in range(4, 6):
                w = slot_cols(U_IN + a)
                unit_groups(U_IN + a, [lambda b: project_rows(b, w, hT), lambda b: project_rows(b, w, hcT)])
            for a in range(6, 8):
                w = slot_cols(U_IN + a)
                unit_groups(U_IN + a, [lambda b: project_rows(b, w, hT)])

            for r in range(4):
                if r == 0:
                    pe.wait_ge(mod_ready, 1)
                pe.wait_ge(grp_out, (1, 2, 3, 5)[r])
                mm(accf[:, r * 512:(r + 1) * 512], rot, raw[:, 2 * r:2 * r + 2, :].rearrange("p k t -> p (k t)"),
                   start=True, stop=True).then_inc(rope_ps, 1)

            def over_tokens(b, gr):
                for a, table in enumerate((dft_cos, dft_sin)):
                    for t in range(TT):
                        last = mm(b[:, a * T:(a + 1) * T], ff[:, t, gr * P:(gr + 1) * P], table[:, t, :],
                                  start=(t == 0), stop=(t == TT - 1))
                return last

            def over_channels(b, pair):
                for j in range(2):
                    gr = 2 * pair + j
                    mm(b[:, j * T:(j + 1) * T], dft_ccos, dft_sb[:, gr, 0, :], start=True, stop=False)
                    last = mm(b[:, j * T:(j + 1) * T], dft_csin, dft_sb[:, gr, 1, :], start=False, stop=True)
                return last

            def own_matrix(b, pair):
                for j in range(2):
                    gr = 2 * pair + j
                    last = mm(b[:, j * T:(j + 1) * T], wfo[:, gr, :], frT[:, gr, :], start=True, stop=True)
                return last

            pe.wait_ge(grp_out, 12)
            for gr in range(4):
                group(lambda b: over_tokens(b, gr))
            pe.wait_ge(grp_out, 16)
            for pair in range(2):
                group(lambda b: over_channels(b, pair))
            pe.wait_ge(grp_out, 18)
            pe.wait_ge(side_in, 16 * N_SIDE)
            for pair in range(2):
                group(lambda b: own_matrix(b, pair))

            pe.wait_ge(rope_done, 4)

            def scores(s):
                h, t = divmod(s, TT)
                if s < 2:
                    pe.wait_ge(grp_out, 20)
                else:
                    pe.wait_ge(exp_ready, s - 1)
                for m in range(2):
                    last = mm(wk[:, 2 * (s % 2) + m, :], qT[64 * m:64 * m + 64, h, t * P:(t + 1) * P],
                              kT[64 * m:64 * m + 64, h, :], start=True, stop=True)
                last.then_inc(sc_ps, 1)

            def turn(s):
                pe.wait_ge(attn_ready, s + 1)
                if s >= 2:
                    pe.wait_ge(at_ready, s - 1)
                for k in range(4):
                    last = nc.tensor.transpose(accf[:, (s % 2) * 512 + k * P:(s % 2) * 512 + (k + 1) * P],
                                               attn[:, s % 2, k * P:(k + 1) * P], ident)
                last.then_inc(at_ps, 1)

            def values(h):
                pe.wait_ge(at_ready, 2 * h + 2)
                if h >= 1:
                    pe.wait_ge(pv_ready, h)
                o = accf[:, 1536 + (h % 2) * T:1536 + (h % 2 + 1) * T]
                for k in range(4):
                    last = mm(o, vv[:, k, h * P:(h + 1) * P], attnT[:, h % 2, k, :], start=(k == 0), stop=(k == 3))
                last.then_inc(pv_ps, 1)

            scores(0)
            for s in range(8):
                if s + 1 < 8:
                    scores(s + 1)
                for a in (2 * s, 2 * s + 1):
                    last = ada(U_ADA2 + a, 16 + 2 * a)
                    if a == 15:
                        pass
                turn(s)
                if s % 2 == 1 and s >= 3:
                    values(s // 2 - 1)
            values(3)
            pe.wait_ge(sub_sq, 1)
            for j in range(2):
                last = mm(wk[:, j, :], ones, scr[:, j * 512:(j + 1) * 512], start=True, stop=True)
            last.then_inc(sub_ss, 1)

            pe.wait_ge(sub_done, 1)
            pe.wait_ge(grp_out, 20)
            for a in range(4):
                arrived(U_OUT + a)
                last = project(accf[:, a * 512:(a + 1) * 512], slot_cols(U_OUT + a), mixT)
                last.then_inc(unit_done, 1)
            norm(2, 0)

            pe.wait_ge(h_shifted, 3)
            pe.wait_ge(side_in, 16 * N_SIDE)
            for t in range(TT):
                o = wk[:, 1, 64 * t:64 * t + 36]
                for k in range(KT):
                    mm(o, hT[:, k, t * P:(t + 1) * P], wrt[:, k, :], start=(k == 0), stop=False)
                last = mm(o, ones[0:1, :], brt[0:1, :], start=False, stop=True)
            last.then_inc(rt_ps, 1)
            pe.wait_ge(rt_g, 1)
            for t in range(TT):
                last = nc.tensor.transpose(wk[0:NE, 2, t * P:(t + 1) * P], rt[:, 256 + 32 * t:256 + 32 * t + 32], ident)
            last.then_inc(gt_ps, 1)
            pe.wait_ge(gt_sb, 1)

            def swiglu(u0, c0, n):
                def gate_up(u, ch, i):
                    for j in range(2):
                        arrived(u + j, i)
                        if j == 0:
                            if i is not None:
                                pe.wait_ge(hidden_ready, i * LOOP + (c0 + ch - 1))
                            elif c0 + ch >= 2:
                                pe.wait_ge(hidden_ready, c0 + ch - 1)
                        last = project(wk[:, 2 * (ch % 2) + j, :], slot_cols(u + j), hT)
                        last.then_inc(unit_done, 1)

                def down(u, ch, i):
                    arrived(u, i)
                    pe.wait_ge(hidden_ready, c0 + ch + 1 if i is None else i * LOOP + (c0 + ch + 1))
                    for k in range(2):
                        for m in range(KT):
                            last = mm(acc[:, m, :], slot_rows(u)[:, k, m * P:(m + 1) * P], hid[:, ch % 2, k, :],
                                      start=(ch == 0 and k == 0 and m % 2 == 0), stop=True, skip_group_check=True)
                    last.then_inc(unit_done, 1)

                gate_up(u0, 0, None)

                def step(s, i):
                    u = u0 + 2 + 3 * (s - 1)
                    gate_up(u, s, i)
                    down(u + 2, s - 1, i)
                step(1, None)
                turns, rest = swiglu_steps(n)
                with pe.Fori(0, turns) as i:
                    for j in range(LOOP):
                        step(2 + j, i)
                for s in rest:
                    step(s, None)
                down(u0 + 3 * n - 1, n - 1, None)

            swiglu(U_MOE, C_MOE, MOEC)
            norm(3, 0)
            norm(4, 0)

            def feed(n, nn):
                pe.wait_ge(h_scaled, nn + 1)
                swiglu(U_F[n], C_F[n], FFC)
            feed(0, 4)

            norm(5, 0)
            pe.wait_ge(h_scaled, 6)
            g0 = 20
            def aunit(a, rows=False):
                u = U_A + a
                arrived(u)
                w = slot_cols(u)
                group(lambda b: (project_rows if rows else project)(b, w, hT), ends_unit=True)

            aunit(0)
            aunit(1)

            def tail(b):
                u = U_A + 2
                arrived(u)
                pe.wait_ge(tail_in, 16)
                w = slot_cols(u, 136)
                for k in range(KT):
                    mm(b[:, 0:T], w[:, k, 0:P], hT[:, k, :], start=(k == 0), stop=(k == KT - 1))
                for t in range(TT):
                    for k in range(KT):
                        last = mm(b[:, T + 8 * t:T + 8 * t + 8], hT[:, k, t * P:(t + 1) * P], w[:, k, P:P + 8],
                                  start=(k == 0), stop=(k == KT - 1))
                return last
            group(tail, ends_unit=True)
            aunit(3)

            def index_scores(b, t, pair, odd):
                for j in range(2):
                    h = 4 * pair + 2 * j + odd
                    last = mm(b[:, j * T:(j + 1) * T], qiA[64 * odd:64 * odd + 64, h // 2, t * P:(t + 1) * P],
                              kiA[64 * odd:64 * odd + 64, :], start=True, stop=True)
                return last
            pe.wait_ge(grp_out, g0 + 3)
            for t in range(TT):
                for pair in range(2):
                    for odd in range(2):
                        group(lambda b: index_scores(b, t, pair, odd))
            for a in range(4, 11):
                aunit(a)
            for a in range(11, 15):
                aunit(a, rows=True)

            def a_scores(h):
                if h < 2:
                    pe.wait_ge(grp_out, g0 + 23)
                else:
                    pe.wait_ge(a_max, h - 1)
                if h == 0:
                    pe.wait_ge(bias_in, 16)
                for t in range(TT):
                    o = wk[:, h % 2, t * T:(t + 1) * T]
                    mm(o, qA[:, h, t * P:(t + 1) * P], kA[:, h, :], start=True, stop=False)
                    last = mm(o, flip, bias[:, h, P * (1 - t):P * (1 - t) + T], start=False, stop=True)
                last.then_inc(a_ps, 1)

            def a_turn(h):
                pe.wait_ge(a_norm, h + 1)
                if h >= 2:
                    pe.wait_ge(apt_ready, h - 1)
                for k in range(2):
                    for t in range(TT):
                        last = nc.tensor.transpose(wk[:, 2 + h % 2, k * T + t * P:k * T + (t + 1) * P],
                                                   prA[:, h % 2, t, k * P:(k + 1) * P], ident)
                last.then_inc(apt_ps, 1)

            def a_values(h):
                pe.wait_ge(apt_ready, h + 1)
                if h >= 2:
                    pe.wait_ge(apv_ready, h - 1)
                o = accf[:, (h % 2) * 512:(h % 2) * 512 + T]
                for k in range(2):
                    last = mm(o, vA[:, k, h * P:(h + 1) * P], ptA[:, h % 2, k, :], start=(k == 0), stop=(k == 1))
                last.then_inc(apv_ps, 1)

            a_scores(0)
            for h in range(HEADS2):
                if h + 1 < HEADS2:
                    a_scores(h + 1)
                a_turn(h)
                if h >= 1:
                    a_values(h - 1)
            a_values(HEADS2 - 1)
            pe.wait_ge(apv_ready, HEADS2)
            for a in range(4):
                arrived(U_AOUT + a)
                last = project(accf[:, a * 512:(a + 1) * 512], slot_cols(U_AOUT + a), mixA)
                last.then_inc(unit_done, 1)

            norm(6, 0)
            feed(1, 6)
            norm(7, 0)
            feed(2, 7)

            pe.wait_ge(wsp_masked, 1)
            for gr in range(BGROUPS):
                last = nc.tensor.transpose(wkf[:, 4 + gr // 2, (gr % 2) * P:(gr % 2 + 1) * P], wsp[:, gr, :], ident)
            last.then_inc(wsp_ps, 1)
            norm(8, 0)
            pe.wait_ge(h_scaled, 9)
            pe.wait_ge(wsp_ready, 1)
            for j in range(2):
                last = mm(wk[:, j, :], ones, wspT[:, 4 * j:4 * j + 4, :].rearrange("p g t -> p (g t)"),
                          start=True, stop=True)
            last.then_inc(w1_ps, 1)
            pe.wait_ge(w1_ready, 1)
            pe.wait_ge(binrow_in, 16)
            gb = g[0]
            for a in range(12):
                u = U_B + a
                arrived(u)
                w = slot_cols(u)

                def with_bias(b):
                    for t in range(TT):
                        o = b[:, t * UW:(t + 1) * UW]
                        for k in range(KT):
                            mm(o, hT[:, k, t * P:(t + 1) * P], w[:, k, :], start=(k == 0), stop=False)
                        last = mm(o, ones[0:1, :], binrow[0:1, a * UW:(a + 1) * UW], start=False, stop=True)
                    return last
                group(with_bias, ends_unit=True)
            for a in range(12, 24):
                arrived(U_B + a)
                w = slot_cols(U_B + a)
                group(lambda b: project(b, w, hT), ends_unit=True)
            pe.wait_ge(ln_ready, 2)
            pe.wait_ge(grp_out, g[0])
            for q in range(BT // 2):
                if q >= 4:
                    pe.wait_ge(sp_done, q - 3)
                for j in range(2):
                    f = 2 * q + j
                    for t in range(TT):
                        last = mm(wk[:, q % 4, j * T + t * P:j * T + (t + 1) * P], vB[:, t, f * P:(f + 1) * P],
                                  wspT[:, f // 3, :], start=True, stop=True)
                last.then_inc(sp_ps, 1)
            for a in range(12):
                arrived(U_BOUT + a)
                pe.wait_ge(sp_done, a + 1)
                for k in range(2):
                    for m in range(KT):
                        last = mm(acc[:, m, :], slot_rows(U_BOUT + a)[:, k, m * P:(m + 1) * P], uB[:, 2 * a + k, :],
                                  start=(a == 0 and k == 0 and m % 2 == 0), stop=True, skip_group_check=True)
                last.then_inc(unit_done, 1)

            norm(9, 0)
            feed(3, 9)
            norm(10, 0)
            pe.wait_ge(h_scaled, 11)
            for t in range(TT):
                for k in range(KT):
                    last = nc.tensor.transpose(accf[:, t * D + k * P:t * D + (k + 1) * P],
                                               hT[:, k, t * P:(t + 1) * P], ident)
                last.then_inc(fin_ps, 1)

        @block.scalar
        def _(act):
            chain = [0]

            def link(ins):
                chain[0] += 1
                ins.then_inc(act_step, 1)
                act.wait_ge(act_step, chain[0])

            A = nc.scalar.activation
            act.dma_start(con[:, :], consts).then_inc(consts_in, 16)
            for dst, src in ROWS:
                act.dma_start(dst, src).then_inc(rows_in, 16)
            act.dma_start(x_rows, x[0].rearrange("(t p) d -> p t d", p=P)).then_inc(x_in, 16)
            act.dma_start(c_rows, ctx[0].rearrange("(t p) d -> p t d", p=P)).then_inc(ctx_in, 16)
            for dst, src in SIDE:
                act.dma_start(dst, src).then_inc(side_in, 16)

            act.wait_ge(vec_ps, 1)
            A(cols[:, 0:P], wk[:, 0, 0:P], ACT.Copy).then_inc(cols_ready, 1)
            A(cols[:, P:P + NR2], wk[:, 0, P:P + NR2], ACT.Copy).then_inc(cols_ready, 1)
            A(lam_cols[0:64, :], wk[0:64, 0, 256:260], ACT.Copy).then_inc(cols_ready, 1)
            A(reldist[:, :], wk[0:HEADS2, 1, :], ACT.Copy).then_inc(reldist_sb, 1)
            act.wait_ge(reldist_sb, 1)
            act.dma_start(reldist_dram, reldist[:, :]).then_inc(reldist_out, 16)
            act.wait_ge(cols_ready, 3)
            A(csil, c_cols.rearrange("p (j k) -> p k j", j=2), ACT.Silu).then_inc(csil_ready, 1)
            act.wait_ge(ctx_ps, 1)
            A(cT.rearrange("p k t -> p (k t)"), wk[:, :, :].rearrange("p b n -> p (b n)"), ACT.Copy).then_inc(ctx_ready, 1)
            act.wait_ge(ctx_ready, 1)

            def norm(n, src, bank, shift=None):
                A(scr[:, :], src.rearrange("p k t -> p (k t)"), ACT.Square).then_inc(sq_ready, 1)
                act.wait_ge(ss_ready, n + 1)
                A(std[:, 0:T], wk[:, bank, 0:T], ACT.Sqrt, bias=eps_col, scale=1.0 / D).then_inc(std_ready, 1)

            def shift(n, dst, j, m0):
                act.wait_ge(h_scaled, n + 1)
                for k in range(KT):
                    last = A(dst[:, k, :], dst[:, k, :], ACT.Identity, bias=mod[:, m0 + k, j:j + 1])
                last.then_inc(h_shifted, 1)

            act.wait_ge(const_set, 1)
            act.wait_ge(reldist_out, 16)
            norm(0, cT, 0)
            act.wait_ge(h_scaled, 1)
            act.wait_ge(x_ready, 1)
            norm(1, xT, 1)
            act.wait_ge(mod_ready, 1)
            shift(0, hcT, 1, 0)
            shift(1, hT, 0, 0)
            act.wait_ge(lam_ps, 1)
            A(lam_exp, wk[:, 2, 0:2], ACT.Exp).then_inc(lame_ready, 1)

            g, loose = [0], [0]

            def bank(unit=None):
                if unit is None:
                    loose[0] += 1
                    act.wait_ge(grp_ps, loose[0])
                else:
                    act.wait_ge(unit_done, unit + 1)
                g[0] += 1
                return wk[:, (g[0] - 1) % 4, :]

            def take(dst, unit=None, two=False, scale=1.0):
                b = bank(unit)
                A(dst, b.rearrange("p (k t) -> p k t", k=2) if two else b, ACT.Copy, scale=scale).then_inc(grp_out, 1)

            def half(a, n=2):
                return a.rearrange("p k t -> p (k t)") if len(a.shape) == 3 else a
            take(half(raw[:, 0:2, :]), U_IN)
            take(half(raw[:, 2:4, :]), U_IN + 1)
            for j in range(2):
                take(half(raw[:, 4 + 2 * j:6 + 2 * j, :]))
                take(kT[:, 2 * j:2 * j + 2, 0:CTX], U_IN + 2 + j, two=True)
            for j in range(2):
                take(vv[:, 2:4, j * UW:(j + 1) * UW], two=True)
                take(vv[:, 0:2, j * UW:(j + 1) * UW], U_IN + 4 + j, two=True)
            for j in range(2):
                take(ff[:, :, j * UW:(j + 1) * UW], U_IN + 6 + j, two=True)
            for gr in range(4):
                take(dft_sb[:, gr, :, :].rearrange("p a n -> p (a n)"))
            for pair in range(2):
                take(half(frT[:, 2 * pair:2 * pair + 2, :]))
            act.wait_ge(rope_done, 4)
            for pair in range(2):
                take(half(mixT[:, 4 + 2 * pair:6 + 2 * pair, :]))

            def exps(s):
                act.wait_ge(max_ready, s + 1)
                if s >= 2:
                    act.wait_ge(attn_ready, s - 1)
                for m in range(2):
                    last = A(prob[:, s % 2, m, :], wk[:, 2 * (s % 2) + m, :], ACT.Exp, bias=nbias[:, s, m:m + 1],
                             scale=HD1 ** -0.5, accum_out=sums[:, s, m:m + 1])
                last.then_inc(exp_ready, 1)

            def turned(s):
                h, t = divmod(s, TT)
                act.wait_ge(at_ps, s + 1)
                if h >= 2:
                    act.wait_ge(pv_ps, h - 1)
                A(attnT[:, h % 2, :, t * P:(t + 1) * P],
                  accf[:, (s % 2) * 512:(s % 2) * 512 + 512].rearrange("p (k t) -> p k t", k=4),
                  ACT.Copy).then_inc(at_ready, 1)

            def head_out(h):
                act.wait_ge(pv_ps, h + 1)
                A(heads_o[:, h, :], accf[:, 1536 + (h % 2) * T:1536 + (h % 2 + 1) * T], ACT.Copy).then_inc(pv_ready, 1)

            exps(0)
            for s in range(8):
                if s + 1 < 8:
                    exps(s + 1)
                turned(s)
                if s % 2 == 1 and s >= 3:
                    head_out(s // 2 - 1)
            head_out(3)
            act.wait_ge(pv_ready, 4)
            A(scr[:, 0:1024], heads_o.rearrange("p h t -> p (h t)"), ACT.Square).then_inc(sub_sq, 1)
            act.wait_ge(sub_ss, 1)
            A(stdh[:, :], wk[:, 0:2, :].rearrange("p b n -> p (b n)"), ACT.Sqrt, bias=eps_col,
              scale=1.0 / P).then_inc(sub_std, 1)

            act.wait_ge(resid_ready, 1)
            norm(2, xT, 0)
            act.wait_ge(mod_ready, 2)
            shift(2, hT, 0, 24)
            act.wait_ge(rt_ps, 1)
            A(lg, wk[:, 1, 0:128].rearrange("p (t n) -> p t n", t=2)[:, :, 0:36], ACT.Copy).then_inc(rt_sb, 1)
            act.wait_ge(rt_max, 1)
            for t in range(TT):
                A(rt[:, 400 + 4 * t:404 + 4 * t], lg[:, t, 0:4], ACT.Exp, bias=rt[:, 336 + t:337 + t],
                  accum_out=rt[:, 338 + t:339 + t])
                A(rt[:, 80 * t + 40:80 * t + 72], rt[:, 80 * t:80 * t + 32], ACT.Exp, bias=rt[:, 340 + t:341 + t])
                last = A(rt[:, 342 + t:343 + t], rt[:, 321 + 8 * t:322 + 8 * t], ACT.Exp, bias=rt[:, 340 + t:341 + t])
            last.then_inc(rt_exp, 1)
            act.wait_ge(gt_ps, 1)
            A(gT[0:NE, :], wk[0:NE, 2, 0:T], ACT.Copy).then_inc(gt_sb, 1)
            act.wait_ge(gt_sb, 1)
            act.dma_start(gates_dram, gT[0:NE, :]).then_inc(gt_out, 16)
            act.wait_ge(gt_out, 16)
            for q in range(4):
                act.dma_start(gates[:, 8 * q:8 * q + 8, :],
                              gates_dram[8 * q:8 * q + 8, :].rearrange("(o e) t -> o e t", o=1)
                              .to_broadcast([P, 8, T])).then_inc(gates_in, 16)

            def swiglu(u0, c0, n, weighted):
                def silu(ch, i):
                    def at(v):
                        return v if i is None else i * LOOP + v
                    u = gate_unit(u0, ch)
                    act.wait_ge(unit_done, u + 1 if i is None else i * (3 * LOOP) + (u + 1))
                    if ch >= 2:
                        act.wait_ge(silw_ready if weighted else hidden_ready, at(c0 + ch - 1))
                    A(sil[:, ch % 2, :, :].rearrange("p m t -> p (m t)"), wk[:, 2 * (ch % 2), :],
                      ACT.Silu).then_inc(silu_ready, 1)
                silu(0, None)
                silu(1, None)
                turns, rest = swiglu_steps(n)
                with act.Fori(0, turns) as i:
                    for j in range(LOOP):
                        silu(2 + j, i)
                for s in rest:
                    silu(s, None)

            swiglu(U_MOE, C_MOE, MOEC, True)
            act.wait_ge(resid_ready, 2)
            norm(3, xT, 0)
            act.wait_ge(h_scaled, 4)
            norm(4, xT, 0)
            swiglu(U_F[0], C_F[0], FFC, False)

            act.wait_ge(resid_ready, 3)
            norm(5, xT, 0)
            act.wait_ge(reldist_out, 16)
            act.dma_start(bias, bass.AP(reldist_dram.tensor, 0, [[1, P], [512, HEADS2], [1, 384]])).then_inc(bias_in, 16)
            take(half(qiA[:, 0:2, :]), U_A)
            take(half(qiA[:, 2:4, :]), U_A + 1)
            b = bank(U_A + 2)
            A(kiA, b[:, 0:T], ACT.Copy)
            A(wiA, b[:, T:T + 16].rearrange("p (t h) -> p t h", t=2), ACT.Copy, scale=8 ** -0.5).then_inc(grp_out, 1)
            take(half(qA[:, 0:2, :]), U_A + 3, scale=P ** -0.5)
            for r in range(8):
                if r >= 2:
                    act.wait_ge(rel_used, r - 1)
                A(relb[:, r % 2, :], bank(), ACT.Relu, scale=64 ** -0.5).then_inc(grp_out, 1)
            for a in range(1, 4):
                take(half(qA[:, 2 * a:2 * a + 2, :]), U_A + 3 + a, scale=P ** -0.5)
            for a in range(4):
                take(half(kA[:, 2 * a:2 * a + 2, :]), U_A + 7 + a)
            for a in range(4):
                take(vA[:, :, a * UW:(a + 1) * UW], U_A + 11 + a, two=True)

            def a_exps(h):
                act.wait_ge(a_max, h + 1)
                if h >= 2:
                    act.wait_ge(apt_ps, h - 1)
                for t in range(TT):
                    last = A(prA[:, h % 2, t, :], lgA[:, h % 2, t, :], ACT.Exp, bias=stA[:, 2 * h + t:2 * h + t + 1],
                             accum_out=stA[:, 16 + 2 * h + t:17 + 2 * h + t])
                last.then_inc(a_exp, 1)

            def a_turned(h):
                act.wait_ge(apt_ps, h + 1)
                if h >= 2:
                    act.wait_ge(apv_ps, h - 1)
                A(ptA[:, h % 2, :, :].rearrange("p k t -> p (k t)"), wk[:, 2 + h % 2, :], ACT.Copy).then_inc(apt_ready, 1)

            def a_out(h):
                act.wait_ge(apv_ps, h + 1)
                A(mixA[:, h, :], accf[:, (h % 2) * 512:(h % 2) * 512 + T], ACT.Copy).then_inc(apv_ready, 1)

            a_exps(0)
            for h in range(HEADS2):
                if h + 1 < HEADS2:
                    a_exps(h + 1)
                a_turned(h)
                if h >= 1:
                    a_out(h - 1)
            a_out(HEADS2 - 1)
            act.wait_ge(resid_ready, 4)
            norm(6, xT, 0)
            swiglu(U_F[1], C_F[1], FFC, False)
            act.wait_ge(resid_ready, 5)
            act.dma_start(wsp, b_w_sp_2[0].rearrange("g t s -> t g s")).then_inc(wsp_in, 16)
            act.dma_start(bspb, b_b_sp_2[0].rearrange("(o g) t -> o g t", o=1).to_broadcast([P, BGROUPS, P])).then_inc(wsp_in, 16)
            norm(7, xT, 0)
            swiglu(U_F[2], C_F[2], FFC, False)

            act.wait_ge(wsp_ps, 1)
            A(wspT.rearrange("p g t -> p (g t)"), wk[:, 2:4, :].rearrange("p b n -> p (b n)"), ACT.Copy).then_inc(wsp_ready, 1)
            act.dma_start(binrow, b_b_in_2[:, BH:2 * BH]).then_inc(binrow_in, 16)
            act.wait_ge(resid_ready, 6)
            norm(8, xT, 0)
            act.wait_ge(w1_ps, 1)
            A(wsum.rearrange("p g t -> p (g t)"), wk[:, 0:2, :].rearrange("p b n -> p (b n)"), ACT.Copy).then_inc(w1_ready, 1)
            for a in range(12):
                b = bank(U_B + a)
                for t in range(TT):
                    last = A(vB[:, t, a * UW:(a + 1) * UW], b[:, t * UW:(t + 1) * UW], ACT.Gelu_apprx_tanh,
                             accum_out=stB[:, 12 * t + a:12 * t + a + 1])
                last.then_inc(grp_out, 1)
            for a in range(12):
                b = bank(U_B + 12 + a)
                for m in range(2):
                    last = A(uB[:, 2 * a + m, :], b[:, m * T:(m + 1) * T], ACT.Gelu_apprx_tanh,
                             bias=bu_cols[:, 2 * a + m:2 * a + m + 1])
                last.then_inc(grp_out, 1)
                if a == 0:
                    act.wait_ge(ln_mean, 1)
                if a in (0, 2, 4, 6):
                    q = a // 2
                    t, hf = divmod(q, 2)
                    if q:
                        act.wait_ge(ln_var, q)
                    A(sqB[:, 0:BH // 2], vB[:, t, hf * (BH // 2):(hf + 1) * (BH // 2)], ACT.Square,
                      bias=stB[:, 26 + t:27 + t], accum_out=stB[:, 28 + q:29 + q]).then_inc(ln_var, 1)
            act.wait_ge(ln_mean, 2)
            A(stB[:, 34:36], stB[:, 32:34], ACT.Sqrt, bias=eps_col, scale=1.0 / BH).then_inc(ln_std, 1)

            act.wait_ge(resid_ready, 7)
            norm(9, xT, 0)
            swiglu(U_F[3], C_F[3], FFC, False)
            act.wait_ge(resid_ready, 8)
            norm(10, xT, 0)
            act.wait_ge(fin_ps, 1)
            A(scr[:, 0:D], accf[:, 0:D], ACT.Copy).then_inc(fin_sb, 1)
            act.wait_ge(fin_ps, 2)
            A(scr[:, D:2 * D], accf[:, D:2 * D], ACT.Copy).then_inc(fin_sb, 1)

        @block.gpsimd
        def _(pool):
            for r in range(4):
                pool.wait_ge(grp_out, (1, 2, 3, 5)[r])
                if r == 0:
                    pool.wait_ge(ss_ready, 2)
                if r >= 2:
                    pool.wait_ge(rope_done, r - 1)
                nc.gpsimd.tensor_tensor(ropeb[:, r % 2, :, :], raw[:, 2 * r:2 * r + 2, :],
                                        cosT.rearrange("p (o t) -> p o t", o=1).to_broadcast([P, 2, T]),
                                        ALU.mult).then_inc(rope_cos, 1)

            def weigh(ch, e_static, i):
                def at(v):
                    return v if i is None else i * LOOP + v
                e = e_static if i is None else i * (LOOP // 2) + e_static
                g = gate_row[:, ch % 2, :]
                nc.gpsimd.tensor_copy(g, gates[:, e, :]).then_inc(row_ready, 1)
                pool.wait_ge(row_ready, at(ch + 1))
                pool.wait_ge(silu_ready, at(ch + 1))
                if ch >= 2:
                    pool.wait_ge(hidden_ready, at(ch - 1))
                for m in range(2):
                    last = nc.gpsimd.tensor_tensor(silw[:, ch % 2, m, :], sil[:, ch % 2, m, :], g, ALU.mult)
                last.then_inc(silw_ready, 1)
            pool.wait_ge(gates_in, 64)
            weigh(0, 0, None)
            weigh(1, 0, None)
            turns, rest = swiglu_steps(MOEC)
            with pool.Fori(0, turns) as i:
                for j in range(LOOP):
                    weigh(2 + j, (2 + j) // 2, i)
            for s in rest:
                weigh(s, s // 2, None)

            pool.wait_ge(wsp_in, 32)
            nc.gpsimd.affine_select(out=wsp, in_=wsp, compare_op=ALU.is_ge, fill=0.0, base=0,
                                    pattern=[[0, BGROUPS], [-1, P]], channel_multiplier=1).then_inc(wsp_masked, 1)

        @block.vector
        def _(dve):
            chain = [0]

            def link(ins):
                chain[0] += 1
                ins.then_inc(dve_step, 1)
                dve.wait_ge(dve_step, chain[0])

            V = nc.vector
            V.memset(eps_col, EPS).then_inc(const_set, 1)
            dve.wait_ge(x_ps, 1)
            V.tensor_copy(xT[:, :, :], acc[:, :, :]).then_inc(x_ready, 1)
            dve.wait_ge(cols_ready, 3)
            V.tensor_tensor(lam_prod[0:64, :], lam_cols[0:64, 0:2], lam_cols[0:64, 2:4], ALU.mult).then_inc(lamp_ready, 1)
            V.tensor_scalar(sub_g, sub_col, 1.0 - LAMBDA_INIT, None, ALU.mult)
            dve.wait_ge(lam_ps, 1)

            def modulation(lo, hi):
                for j in range(2):
                    last = V.tensor_tensor(mod[:, lo:hi, j], accf[:, 1024 + 2 * lo:1024 + 2 * hi]
                                           .rearrange("p (m j) -> p m j", j=2)[:, :, j], ada_b[:, lo:hi], ALU.add)
                link(last)
            modulation(0, 16)
            for j in range(2):
                last = V.scalar_tensor_tensor(a_mix[:, j, :], mod[:, 8:16, j], 1.0, g_mix, ALU.add, ALU.mult)
            last.then_inc(mod_ready, 1)
            dve.wait_ge(mod_ready, 1)

            def norm(n, src, dst, gcol):
                dve.wait_ge(std_ready, n + 1)
                link(V.reciprocal(rstd[:, 0:T], std[:, 0:T]))
                for k in range(KT):
                    last = V.scalar_tensor_tensor(dst[:, k, :], src[:, k, :], gcol[:, k:k + 1], rstd[:, 0:T],
                                                  ALU.mult, ALU.mult)
                last.then_inc(h_scaled, 1)

            norm(0, cT, hcT, a_mix[:, 1, :])
            norm(1, xT, hT, a_mix[:, 0, :])
            dve.wait_ge(lame_ready, 1)
            link(V.tensor_tensor(neg_lam, lam_exp[:, 1:2], lam_exp[:, 0:1], ALU.subtract))
            link(V.tensor_scalar(neg_lam, neg_lam, -LAMBDA_INIT, None, ALU.add))
            V.tensor_copy(lam_prod[:, 0:1], neg_lam).then_inc(lam_ready, 1)

            for r in range(4):
                dve.wait_ge(rope_ps, r + 1)
                dve.wait_ge(rope_cos, r + 1)
                tmp = ropea[:, r % 2, :, :]
                link(V.tensor_tensor(tmp, accf[:, r * 512:(r + 1) * 512].rearrange("p (k t) -> p k t", k=2),
                                     sinT.rearrange("p (o t) -> p o t", o=1).to_broadcast([P, 2, T]), ALU.mult))
                dst = qT[:, 2 * r:2 * r + 2, :] if r < 2 else kT[:, 2 * r - 4:2 * r - 2, CTX:CTX + T]
                V.tensor_tensor(dst, tmp, ropeb[:, r % 2, :, :], ALU.add).then_inc(rope_done, 1)

            def maxima(s):
                dve.wait_ge(sc_ps, s + 1)
                link(V.tensor_reduce(out=nmax[:, s, :], in_=wk[:, 2 * (s % 2):2 * (s % 2) + 2, :], op=ALU.max, axis=AX_X))
                V.tensor_scalar(nbias[:, s, :], nmax[:, s, :], -(HD1 ** -0.5), None, ALU.mult).then_inc(max_ready, 1)

            def combine(s):
                dve.wait_ge(exp_ready, s + 1)
                if s >= 2:
                    dve.wait_ge(at_ps, s - 1)
                link(V.reciprocal(rsum[:, s, :], sums[:, s, :]))
                link(V.tensor_tensor(rsum[:, s, 1:2], rsum[:, s, 1:2], neg_lam, ALU.mult))
                link(V.tensor_scalar(prob[:, s % 2, 1, :], prob[:, s % 2, 1, :], rsum[:, s, 1:2], None, ALU.mult))
                V.scalar_tensor_tensor(attn[:, s % 2, :], prob[:, s % 2, 0, :], rsum[:, s, 0:1], prob[:, s % 2, 1, :],
                                       ALU.mult, ALU.add).then_inc(attn_ready, 1)
            maxima(0)
            for s in range(8):
                if s + 1 < 8:
                    maxima(s + 1)
                combine(s)
            dve.wait_ge(unit_done, U_OUT)
            modulation(16, 48)
            dve.wait_ge(sub_std, 1)
            link(V.reciprocal(rstdh[:, :], stdh[:, :]))
            for h in range(HEADS1):
                last = V.scalar_tensor_tensor(mixT[:, h, :], heads_o[:, h, :], sub_g, rstdh[:, h * T:(h + 1) * T],
                                              ALU.mult, ALU.mult)
            last.then_inc(sub_done, 1)
            V.scalar_tensor_tensor(a_ffn, mod[:, 32:40, 0], 1.0, g_ffn, ALU.add, ALU.mult).then_inc(mod_ready, 1)
            dve.wait_ge(mod_ready, 2)
            for a in range(4):
                dve.wait_ge(unit_done, U_OUT + a + 1)
                for m in (2 * a, 2 * a + 1):
                    last = V.scalar_tensor_tensor(xT[:, m, :], acc[:, m, :], mod[:, 16 + m, 0:1], xT[:, m, :],
                                                  ALU.mult, ALU.add)
            last.then_inc(resid_ready, 1)
            norm(2, xT, hT, a_ffn)

            dve.wait_ge(rt_sb, 1)
            for t in range(TT):
                e0 = 80 * t
                gmax, gneg, gsum = rt[:, 344 + t:345 + t], rt[:, 336 + t:337 + t], rt[:, 338 + t:339 + t]
                eneg, e2 = rt[:, 340 + t:341 + t], rt[:, 342 + t:343 + t]
                first = rt[:, 348 + t:349 + t]
                pick = rt[:, 352 + 4 * t:356 + 4 * t]
                off = rt[:, 360 + 4 * t:364 + 4 * t]
                t8 = rt[:, 320 + 8 * t:328 + 8 * t]
                link(V.tensor_reduce(out=gmax, in_=lg[:, t, 0:4], op=ALU.max, axis=AX_X))
                V.tensor_scalar(gneg, gmax, -1.0, None, ALU.mult)
                link(V.scalar_tensor_tensor(pick, lg[:, t, 0:4], gmax, groups[:, 0:4], ALU.is_equal, ALU.mult))
                link(V.tensor_reduce(out=first, in_=pick, op=ALU.min, axis=AX_X))
                link(V.tensor_scalar(pick, groups[:, 0:4], first, None, ALU.is_equal))
                link(V.tensor_scalar(off, pick, 1.0e30, -1.0e30, ALU.mult, ALU.add))
                V.memset(rt[:, e0 + 32:e0 + 40], -2.0e30)
                for gr in range(4):
                    last = V.tensor_scalar(rt[:, e0 + 8 * gr:e0 + 8 * gr + 8], lg[:, t, 4 + 8 * gr:12 + 8 * gr],
                                           pick[:, gr:gr + 1], off[:, gr:gr + 1], ALU.mult, ALU.add)
                link(last)
                link(V.max(t8, rt[:, e0:e0 + 32]))
                last = V.tensor_scalar(eneg, t8[:, 0:1], -1.0, None, ALU.mult)
                if t == TT - 1:
                    last.then_inc(rt_max, 1)
            dve.wait_ge(rt_exp, 1)
            for t in range(TT):
                e0 = 80 * t
                t8 = rt[:, 320 + 8 * t:328 + 8 * t]
                gsum, e2 = rt[:, 338 + t:339 + t], rt[:, 342 + t:343 + t]
                link(V.memset(t8[:, 2:8], -2.0e30))
                link(V.match_replace(out=rt[:, e0:e0 + 40], in_to_replace=t8, in_values=rt[:, e0:e0 + 40], imm_value=3.0e30))
                link(V.tensor_scalar(rt[:, e0:e0 + 32], rt[:, e0:e0 + 32], 2.0e30, None, ALU.is_ge))
                link(V.scalar_tensor_tensor(e2, e2, 1.0, gsum, ALU.add, ALU.mult))
                link(V.reciprocal(e2, e2))
                last = V.scalar_tensor_tensor(rt[:, 256 + 32 * t:288 + 32 * t], rt[:, e0 + 40:e0 + 72], e2,
                                              rt[:, e0:e0 + 32], ALU.mult, ALU.mult)
            last.then_inc(rt_g, 1)

            def swiglu(u0, c0, n, weighted):
                def hidden(ch, i):
                    def at(v):
                        return v if i is None else i * LOOP + v
                    dve.wait_ge(silw_ready if weighted else silu_ready, at(c0 + ch + 1))
                    u = gate_unit(u0, ch) + 1
                    dve.wait_ge(unit_done, u + 1 if i is None else i * (3 * LOOP) + (u + 1))
                    if ch >= 2:
                        d = down_unit(u0, ch - 2, n)
                        dve.wait_ge(unit_done, d + 1 if i is None else i * (3 * LOOP) + (d + 1))
                    V.tensor_tensor(hid[:, ch % 2, :, :], (silw if weighted else sil)[:, ch % 2, :, :],
                                    wk[:, 2 * (ch % 2) + 1, :].rearrange("p (m t) -> p m t", m=2),
                                    ALU.mult).then_inc(hidden_ready, 1)
                hidden(0, None)
                hidden(1, None)
                turns, rest = swiglu_steps(n)
                with dve.Fori(0, turns) as i:
                    for j in range(LOOP):
                        hidden(2 + j, i)
                for s in rest:
                    hidden(s, None)
                dve.wait_ge(unit_done, u0 + 3 * n)
            swiglu(U_MOE, C_MOE, MOEC, True)
            for m in range(KT):
                last = V.scalar_tensor_tensor(xT[:, m, :], acc[:, m, :], mod[:, 40 + m, 0:1], xT[:, m, :],
                                              ALU.mult, ALU.add)
            last.then_inc(resid_ready, 1)
            norm(3, xT, xT, g_fin)
            dve.wait_ge(h_scaled, 4)
            norm(4, xT, hT, norm2[:, 0:8])

            def feed(n):
                swiglu(U_F[n], C_F[n], FFC, False)
                V.scalar_tensor_tensor(xT[:, :, :].rearrange("p k t -> p (k t)"), accf, 0.5,
                                       xT[:, :, :].rearrange("p k t -> p (k t)"),
                                       ALU.mult, ALU.add).then_inc(resid_ready, 1)
            feed(0)

            norm(5, xT, hT, norm2[:, 8:16])
            link(V.memset(score.rearrange("p t k -> p (t k)"), 0.0))
            g0 = 20
            r = 0
            for t in range(TT):
                for pair in range(2):
                    for odd in range(2):
                        dve.wait_ge(grp_out, g0 + 5 + r)
                        for j in range(2):
                            h = 4 * pair + 2 * j + odd
                            ins = V.scalar_tensor_tensor(score[:, t, :], relb[:, r % 2, j * T:(j + 1) * T],
                                                         wiA[:, t, h:h + 1], score[:, t, :], ALU.mult, ALU.add)
                            if j == 0:
                                link(ins)
                        ins.then_inc(rel_used, 1)
                        r += 1
                        dve.wait_ge(rel_used, r)
            link(V.tensor_tensor(score, score, causal, ALU.add))
            for q in range(TOPK // 8):
                for t in range(TT):
                    last = V.max(top8[:, t, :], score[:, t, :])
                link(last)
                for t in range(TT):
                    last = V.match_replace(out=score[:, t, :], in_to_replace=top8[:, t, :], in_values=score[:, t, :],
                                           imm_value=TAKEN)
                link(last)
            link(V.tensor_scalar(amask, score, 2.0 * FAR, FAR, ALU.is_gt, ALU.mult))
            V.tensor_tensor(amask, amask, causal, ALU.min).then_inc(mask_ready, 1)
            dve.wait_ge(mask_ready, 1)

            def a_maxima(h):
                dve.wait_ge(a_ps, h + 1)
                if h >= 2:
                    dve.wait_ge(a_exp, h - 1)
                link(V.tensor_tensor(lgA[:, h % 2, :, :], wk[:, h % 2, :].rearrange("p (t k) -> p t k", t=2), amask,
                                     ALU.add))
                link(V.tensor_reduce(out=stA[:, 32 + 2 * h:34 + 2 * h], in_=lgA[:, h % 2, :, :], op=ALU.max, axis=AX_X))
                V.tensor_scalar(stA[:, 2 * h:2 * h + 2], stA[:, 32 + 2 * h:34 + 2 * h], -1.0, None,
                                ALU.mult).then_inc(a_max, 1)

            def a_normal(h):
                dve.wait_ge(a_exp, h + 1)
                link(V.reciprocal(stA[:, 48 + 2 * h:50 + 2 * h], stA[:, 16 + 2 * h:18 + 2 * h]))
                for t in range(TT):
                    last = V.tensor_scalar(prA[:, h % 2, t, :], prA[:, h % 2, t, :],
                                           stA[:, 48 + 2 * h + t:49 + 2 * h + t], None, ALU.mult)
                last.then_inc(a_norm, 1)
            a_maxima(0)
            for h in range(HEADS2):
                if h + 1 < HEADS2:
                    a_maxima(h + 1)
                a_normal(h)
            for a in range(4):
                dve.wait_ge(unit_done, U_AOUT + a + 1)
                last = V.tensor_tensor(xT[:, 2 * a:2 * a + 2, :], acc[:, 2 * a:2 * a + 2, :],
                                       xT[:, 2 * a:2 * a + 2, :], ALU.add)
            last.then_inc(resid_ready, 1)
            norm(6, xT, hT, norm2[:, 16:24])
            feed(1)
            norm(7, xT, hT, norm2[:, 24:32])
            feed(2)

            norm(8, xT, hT, norm2[:, 32:40])
            dve.wait_ge(w1_ready, 1)
            for f in range(BT):
                V.scalar_tensor_tensor(affB[:, f, :], wsum[:, f // 3, :], lnb_cols[:, f:f + 1], bspb[:, f // 3, :],
                                       ALU.mult, ALU.add)
            dve.wait_ge(grp_out, 43 + 12)
            link(V.tensor_reduce(out=stB[:, 24:26], in_=stB[:, 0:24].rearrange("p (t a) -> p t a", t=2),
                                 op=ALU.add, axis=AX_X))
            V.tensor_scalar(stB[:, 26:28], stB[:, 24:26], -1.0 / BH, None, ALU.mult).then_inc(ln_mean, 1)
            dve.wait_ge(ln_var, 4)
            V.tensor_reduce(out=stB[:, 32:34], in_=stB[:, 28:32].rearrange("p (t a) -> p t a", t=2),
                            op=ALU.add, axis=AX_X).then_inc(ln_mean, 1)
            dve.wait_ge(ln_std, 1)
            link(V.reciprocal(stB[:, 36:38], stB[:, 34:36]))
            for t in range(TT):
                V.tensor_scalar(vB[:, t, :], vB[:, t, :], stB[:, 26 + t:27 + t], stB[:, 36 + t:37 + t],
                                ALU.add, ALU.mult).then_inc(ln_ready, 1)
            dve.wait_ge(grp_out, 43 + 24)
            for q in range(BT // 2):
                dve.wait_ge(sp_ps, q + 1)
                for j in range(2):
                    f = 2 * q + j
                    y = spb[:, j, :, :]
                    last = V.scalar_tensor_tensor(
                        y, wk[:, q % 4, j * T:(j + 1) * T].rearrange("p (t k) -> p t k", t=2), lng_cols[:, f:f + 1],
                        affB[:, f, :].rearrange("p (o t) -> p o t", o=1).to_broadcast([P, 2, P]), ALU.mult, ALU.add)
                link(last)
                last = V.tensor_tensor(uB[:, 2 * q:2 * q + 2, :], uB[:, 2 * q:2 * q + 2, :],
                                       spb[:, :, :, :].rearrange("p j t k -> p j (t k)"), ALU.mult)
                last.then_inc(sp_done, 1)
                dve.wait_ge(sp_done, q + 1)
            dve.wait_ge(unit_done, U_BOUT + 12)
            V.tensor_tensor(xT[:, :, :], acc[:, :, :], xT[:, :, :], ALU.add).then_inc(resid_ready, 1)
            norm(9, xT, hT, norm2[:, 40:48])
            feed(3)
            norm(10, xT, hT, g_fin2)
    return nc


_INS = ["x", "c", "ctx", "c_ctx", "w_ada", "b_ada", "g_mix_norm", "g_ffn_norm", "w_in", "lambda_q1", "lambda_k1",
        "lambda_q2", "lambda_k2", "g_subln", "w_fourier", "w_out", "w_router_group", "b_router_group",
        "w_router_expert", "b_router_expert", "w_gate", "w_up", "w_down", "g_final", "norm_g_2", "final_g_2",
        "ffn_w_in_2", "ffn_w_out_2", "rel_table_2", "a_w_in_2", "a_w_out_2", "b_w_in_2", "b_b_in_2", "b_ln_g_2",
        "b_ln_b_2", "b_w_sp_2", "b_b_sp_2", "b_w_out_2"]


def kernel(**inputs):
    import numpy as _np
    import concourse.bacc as _bacc
    from concourse import mybir as _mybir
    from concourse.bass_utils import run_bass_kernel_spmd as _run

    nc = _bacc.Bacc("TRN2", target_bir_lowering=False, num_devices=1, dynamic_dma_scratch_size=1024)
    arrays, args = {}, {}
    for name in _INS:
        a = _np.ascontiguousarray(inputs[name])
        arrays[f"in_{name}_dram"] = a
        args[name] = nc.dram_tensor(f"in_{name}_dram", a.shape, _mybir.dt.from_np(a.dtype),
                                    kind="ExternalInput").ap()
    table = constants()
    arrays["in_consts_dram"] = table
    args["consts"] = nc.dram_tensor("in_consts_dram", table.shape, _mybir.dt.float32, kind="ExternalInput").ap()
    out = nc.dram_tensor("out_0_dram", (1, T, D), _mybir.dt.float32, kind="ExternalOutput").ap()
    build(nc, out=out, **args)
    r = _run(nc, [arrays], core_ids=[0])
    return r.results[0]["out_0_dram"]
```

```python
import math
from contextlib import ExitStack

import numpy as np

import concourse.bass as bass
from concourse import mybir

ALU = mybir.AluOpType
ACT = mybir.ActivationFunctionType
F32 = mybir.dt.float32
F32R = mybir.dt.float32r
AX_X = mybir.AxisListType.X

P = 128
D = 1024
KT = D // P
T = 256
TT = T // P
CTX = 256
EPS = 1e-6
UW = 256
RING = 4
SPLIT = 3
TURN = 12
HEADS1, HD1 = 4, 64
NE, DE = 32, 512
SLOTS = 128
TAKES = SLOTS
FF = 2816
FFC = FF // UW
HEADS2 = 8
TOPK = 64
BH = 3072
BT = BH // P
BGROUPS = 8
LAMBDA_INIT = 0.8 - 0.6 * math.exp(-0.3 * 0)
FAR = -1.0e38
TAKEN = -3.0e38

SPLIT_ARENA = 4352

CONSTS = {}
_at = 0
for _name, _w in (("ident", P), ("ones", P), ("rot", P), ("flip", P), ("cos", T), ("sin", T),
                  ("dft_cos", TT * T), ("dft_sin", TT * T), ("dft_ccos", P), ("dft_csin", P),
                  ("causal", TT * T), ("buckets", 512), ("groups", 8),
                  ("before", P), ("slots", SLOTS)):
    CONSTS[_name] = (_at, _at + _w)
    _at += _w
NCONST = _at

U_ADA1 = 0
U_IN = U_ADA1 + 8
U_ADA2 = U_IN + 8
U_OUT = U_ADA2 + 16
U_MOE = U_OUT + 4
U_F = [U_MOE + 6 * NE]
U_A = U_F[0] + 3 * FFC
U_AOUT = U_A + 15
U_F.append(U_AOUT + 4)
U_F.append(U_F[1] + 3 * FFC)
U_B = U_F[2] + 3 * FFC
U_BOUT = U_B + 24
U_F.append(U_BOUT + 12)
C_F = [i * FFC for i in range(4)]
C_H = [0, FFC, 2 * FFC, 3 * FFC + 12]
C_HB = 3 * FFC
LOOP = 4
N_UNITS = U_F[3] + 3 * FFC


def gate_unit(u0, ch):
    return u0 if ch == 0 else u0 + 2 + 3 * (ch - 1)


def down_unit(u0, ch, n):
    return u0 + 4 + 3 * ch if ch < n - 1 else u0 + 3 * n - 1


def split_of(u):
    if U_IN <= u < U_ADA2:
        return u - U_IN
    return u - U_OUT + 8 if u >= U_OUT else None


def unit_of(v):
    return v + U_IN if v < 8 else v - 8 + U_OUT


def constants():
    c = np.zeros((P, NCONST), np.float64)

    def put(name, a):
        lo, _ = CONSTS[name]
        c[:a.shape[0], lo:lo + a.shape[1]] = a

    p = np.arange(P)
    put("ident", np.eye(P))
    put("ones", np.ones((P, P)))
    put("flip", np.eye(P)[::-1])
    rot = np.zeros((P, P))
    for i in range(P):
        if i % 32 < 16:
            rot[i + 16, i] = -1.0
        else:
            rot[i - 16, i] = 1.0
    put("rot", rot)
    tok = np.arange(T)
    inv = (np.float32(10000.0) ** (-np.arange(0, 32, 2, dtype=np.float32) / np.float32(32))).astype(np.float32)
    pos = np.stack([tok // 64, tok % 64]).astype(np.float32)
    ang = (pos[(p % 64) // 32] * inv[(p % 32) % 16][:, None]).astype(np.float32)
    put("cos", np.cos(ang.astype(np.float64)))
    put("sin", np.sin(ang.astype(np.float64)))
    n = np.outer(tok, tok) % T
    cn, sn = np.cos(2 * np.pi * n / T), np.sin(2 * np.pi * n / T)
    for t in range(TT):
        lo = CONSTS["dft_cos"][0] + t * T
        c[:, lo:lo + T] = cn[t * P:(t + 1) * P]
        lo = CONSTS["dft_sin"][0] + t * T
        c[:, lo:lo + T] = sn[t * P:(t + 1) * P]
    m = np.outer(p, p) % P
    put("dft_ccos", np.cos(2 * np.pi * m / P) / math.sqrt(T * P))
    put("dft_csin", -np.sin(2 * np.pi * m / P) / math.sqrt(T * P))
    for t in range(TT):
        lo = CONSTS["causal"][0] + t * T
        c[:, lo:lo + T] = np.where(tok[None, :] <= (t * P + p)[:, None], 0.0, FAR)
    dist = np.maximum(T - 1 - np.arange(512), 0)
    large = 16 + (np.log(np.maximum(dist, 1).astype(np.float32) / np.float32(16)) / np.float32(math.log(2048 / 16))
                  * np.float32(16)).astype(np.int32)
    bucket = np.where(dist < 16, dist, np.minimum(large, 31))
    put("buckets", (np.arange(32)[:, None] == bucket[None, :]).astype(np.float64))
    put("groups", np.tile(np.arange(8)[None, :] - 99.0, (P, 1)))
    put("before", np.triu(np.ones((P, P)), 1))
    put("slots", np.tile(np.where(np.arange(SLOTS) < TAKES, np.arange(SLOTS), -7)[None, :], (P, 1)))
    return c.astype(np.float32)


def build(nc, x, c, ctx, c_ctx, w_ada, b_ada, g_mix_norm, g_ffn_norm, w_in, lambda_q1, lambda_k1,
          lambda_q2, lambda_k2, g_subln, w_fourier, w_out, w_router_group, b_router_group,
          w_router_expert, b_router_expert, w_gate, w_up, w_down, g_final, norm_g_2, final_g_2,
          ffn_w_in_2, ffn_w_out_2, rel_table_2, a_w_in_2, a_w_out_2, b_w_in_2, b_b_in_2, b_ln_g_2,
          b_ln_b_2, b_w_sp_2, b_b_sp_2, b_w_out_2, consts, out):
    stack = ExitStack()
    with stack:
        def sb(name, shape, dt=F32):
            return stack.enter_context(nc.sbuf_tensor(name, shape, dt))

        def sem(name):
            return stack.enter_context(nc.semaphore(name))

        ring = sb("ring", [P, RING, KT * UW])
        xT = sb("xT", [P, KT, T])
        scr = sb("scr", [P, KT * T])
        hT = scr[:, :].rearrange("p (k t) -> p k t", k=KT)
        w_hi, w_lo = sb("w_hi", [P, SPLIT, KT * UW], F32R), sb("w_lo", [P, SPLIT, KT * UW], F32R)
        h_hi, h_lo = sb("h_hi", [P, KT, T], F32R), sb("h_lo", [P, KT, T], F32R)
        hid_hi, hid_lo = sb("hid_hi", [P, 2, 2, T], F32R), sb("hid_lo", [P, 2, 2, T], F32R)
        gated = sb("gated", [P, 6 * 512])
        con = sb("con", [P, NCONST])
        cols = sb("cols", [P, 2 * P])
        small = sb("small", [P, 352])
        arena_at = nc.sbuf_base
        arena = sb("arena", [P, 18432])
        split_arena = nc.alloc_sbuf_tensor_at("split_arena", [P, SPLIT_ARENA], F32R, offset=arena_at)
        acc = stack.enter_context(nc.psum_tensor("acc", [P, KT, T], F32))
        wk = stack.enter_context(nc.psum_tensor("wk", [P, 4, 512], F32))
        accf = acc[:, :, :].rearrange("p k t -> p (k t)")

        def const(name):
            lo, hi = CONSTS[name]
            return con[:, lo:hi]

        ident, ones, rot, flip = const("ident"), const("ones"), const("rot"), const("flip")
        cosT, sinT = const("cos"), const("sin")
        dft_cos = const("dft_cos").rearrange("p (t n) -> p t n", t=TT)
        dft_sin = const("dft_sin").rearrange("p (t n) -> p t n", t=TT)
        dft_ccos, dft_csin = const("dft_ccos"), const("dft_csin")
        causal = const("causal").rearrange("p (t n) -> p t n", t=TT)
        buckets = const("buckets")
        groups = const("groups")
        before, slots = const("before"), const("slots")

        used = [0]

        def area(n, at=None):
            if at is None:
                at = used[0]
                used[0] += n
            assert at + n <= 18432, (at, n)
            return arena[:, at:at + n]

        rows1 = scr[:, 0:P]
        rows2 = scr[:, P:2 * P]
        rows3 = scr[:, 2 * P:2 * P + 64]
        ada_b = cols[:, 0:48]
        g_mix = cols[:, 48:56]
        g_ffn = cols[:, 56:64]
        g_fin = cols[:, 64:72]
        norm2 = cols[:, 72:120]
        g_fin2 = cols[:, 120:128]
        c_cols = cols[:, 128:144]
        bu_cols = cols[:, 144:168]
        lng_cols = cols[:, 168:192]
        lnb_cols = cols[:, 192:216]
        sub_col = cols[:, 216:217]
        lam_cols = cols[:, 217:221]
        NR2 = 16 + 24 + 24 + 24 + 1
        s_at = [0]

        def sm(n):
            a = small[:, s_at[0]:s_at[0] + n]
            s_at[0] += n
            assert s_at[0] <= 352
            return a

        csil = sm(16).rearrange("p (k j) -> p k j", j=2)
        mod = sm(96).rearrange("p (m j) -> p m j", j=2)
        a_mix = sm(16).rearrange("p (j k) -> p j k", j=2)
        a_ffn = sm(8)
        eps_col = sm(1)
        lam_prod = sm(2)
        lam_exp = sm(2)
        neg_lam = sm(1)
        sub_g = sm(1)
        std = sb("std", [P, T])
        rstd = sb("rstd", [P, T])

        weights_in = [sem(f"weights_in{i}") for i in range(RING)]
        unit_done = sem("unit_done")
        consts_in, rows_in, x_in, ctx_in = sem("consts_in"), sem("rows_in"), sem("x_in"), sem("ctx_in")
        side_in = sem("side_in")
        dve_step, act_step = sem("dve_step"), sem("act_step")
        const_set = sem("const_set")
        vec_ps, cols_ready, csil_ready = sem("vec_ps"), sem("cols_ready"), sem("csil_ready")
        reldist_sb, reldist_out = sem("reldist_sb"), sem("reldist_out")
        x_ps, ctx_ps, x_ready, ctx_ready = sem("x_ps"), sem("ctx_ps"), sem("x_ready"), sem("ctx_ready")
        lamp_ready, lam_ps, lame_ready, lam_ready = (sem("lamp_ready"), sem("lam_ps"), sem("lame_ready"),
                                                     sem("lam_ready"))
        mod_ready = sem("mod_ready")
        sq_ready, ss_ready, std_ready = sem("sq_ready"), sem("ss_ready"), sem("std_ready")
        h_scaled, h_shifted = sem("h_scaled"), sem("h_shifted")
        w_hi_ready, w_lo_ready, h_hi_ready, h_lo_ready = (sem("w_hi_ready"), sem("w_lo_ready"), sem("h_hi_ready"),
                                                          sem("h_lo_ready"))
        hid_hi_ready, hid_lo_ready = sem("hid_hi_ready"), sem("hid_lo_ready")
        mix_hi_ready, mix_lo_ready = sem("mix_hi_ready"), sem("mix_lo_ready")
        grp_ps, grp_out = sem("grp_ps"), sem("grp_out")
        rope_ps, rope_cos, rope_done = sem("rope_ps"), sem("rope_cos"), sem("rope_done")
        sc_ps, max_ready, exp_ready, attn_ready = (sem("sc_ps"), sem("max_ready"), sem("exp_ready"),
                                                   sem("attn_ready"))
        at_ps, at_ready, pv_ps, pv_ready = sem("at_ps"), sem("at_ready"), sem("pv_ps"), sem("pv_ready")
        sub_sq, sub_ss, sub_std, sub_done = sem("sub_sq"), sem("sub_ss"), sem("sub_std"), sem("sub_done")
        resid_ready = sem("resid_ready")
        rt_ps, rt_sb, rt_max, rt_exp, rt_g = sem("rt_ps"), sem("rt_sb"), sem("rt_max"), sem("rt_exp"), sem("rt_g")
        gt_ps, gt_sb, gt_out, gates_in = sem("gt_ps"), sem("gt_sb"), sem("gt_out"), sem("gates_in")
        silu_ready, hidden_ready, tail_in = sem("silu_ready"), sem("hidden_ready"), sem("tail_in")
        h2_ps, h2_ready, rank_ps, rank_ready = sem("h2_ps"), sem("h2_ready"), sem("rank_ps"), sem("rank_ready")
        h2_hi_ready, gates_split, pick_ready = sem("h2_hi_ready"), sem("gates_split"), sem("pick_ready")
        xg_hi_ps, xg_lo_ps, xg_hi_ready, xg_lo_ready = (sem("xg_hi_ps"), sem("xg_lo_ps"), sem("xg_hi_ready"),
                                                        sem("xg_lo_ready"))
        ex_silu, ex_hidden, turned_ps = sem("ex_silu"), sem("ex_hidden"), sem("turned_ps")
        turned_hi_ready, turned_lo_ready = sem("turned_hi_ready"), sem("turned_lo_ready")
        y0_ps, y_hi_ready, y_lo_ready = sem("y0_ps"), sem("y_hi_ready"), sem("y_lo_ready")
        spread_ps, spread_ready, spread_done = sem("spread_ps"), sem("spread_ready"), sem("spread_done")
        fb_in, fb_up, fb_silu, fb_mul, fb_hidden, fb_down = (sem("fb_in"), sem("fb_up"), sem("fb_silu"),
                                                             sem("fb_mul"), sem("fb_hidden"), sem("fb_down"))
        bias_in = sem("bias_in")
        rel_ready, rel_used, mask_ready = sem("rel_ready"), sem("rel_used"), sem("mask_ready")
        a_ps, a_max, a_exp, a_norm = sem("a_ps"), sem("a_max"), sem("a_exp"), sem("a_norm")
        apt_ps, apt_ready, apv_ps, apv_ready = (sem("apt_ps"), sem("apt_ready"), sem("apv_ps"),
                                                sem("apv_ready"))
        wsp_in, wsp_masked, wsp_ps, wsp_ready = (sem("wsp_in"), sem("wsp_masked"), sem("wsp_ps"),
                                                 sem("wsp_ready"))
        w1_ps, w1_ready, binrow_in = sem("w1_ps"), sem("w1_ready"), sem("binrow_in")
        ln_mean, ln_var, ln_std, ln_ready = sem("ln_mean"), sem("ln_var"), sem("ln_std"), sem("ln_ready")
        sp_ps, sp_done = sem("sp_ps"), sem("sp_done")
        fin_ps, fin_sb, out_done = sem("fin_ps"), sem("fin_sb"), sem("out_done")

        reldist_dram = nc.dram_tensor("reldist_dram", (HEADS2, 512), F32, kind="Internal").ap()
        gates_dram = nc.dram_tensor("gates_dram", (NE, T), F32, kind="Internal").ap()

        base1 = area(8192)
        x_rows, c_rows = base1[:, 0:2048], base1[:, 2048:4096]
        cT = base1[:, 4096:6144].rearrange("p (k t) -> p k t", k=KT)
        hcT = base1[:, 6144:8192].rearrange("p (k t) -> p k t", k=KT)
        x_rows = x_rows.rearrange("p (a d) -> p a d", a=TT)
        c_rows = c_rows.rearrange("p (a d) -> p a d", a=TT)
        prob = base1[:, 0:2048].rearrange("p (b m k) -> p b m k", b=2, m=2)
        attn = base1[:, 2048:3072].rearrange("p (b k) -> p b k", b=2)
        attnT = base1[:, 3072:5120].rearrange("p (b k t) -> p b k t", b=2, k=4)
        heads_o = base1[:, 5120:6144].rearrange("p (h t) -> p h t", h=4)
        dft_sb = base1[:, 6144:8192].rearrange("p (g a n) -> p g a n", g=4, a=2)
        mixT = area(2048).rearrange("p (k t) -> p k t", k=KT)
        raw = mixT
        qT = area(1024).rearrange("p (k t) -> p k t", k=4)
        kT = area(2048).rearrange("p (k t) -> p k t", k=4)
        vv = area(2048).rearrange("p (k f) -> p k f", k=4)
        ff = area(1024).rearrange("p (k f) -> p k f", k=2)
        frT = area(1024).rearrange("p (g n) -> p g n", g=4)
        wfo = area(512).rearrange("p (g n) -> p g n", g=4)
        wrt = area(8 * 36).rearrange("p (k n) -> p k n", k=KT)
        brt = area(36)
        gates = arena[:, 0:NE * T].rearrange("p (e t) -> p e t", e=NE)
        lg = arena[:, 8192:8264].rearrange("p (t n) -> p t n", t=2)
        rt = arena[:, 8264:8264 + 512]
        gT = arena[:, 8800:9056]
        fb_w = arena[:, 11648:17792].rearrange("p (w n) -> p w n", w=3)
        r_gate = rt[:, 256:320].rearrange("p (t e) -> p e t", t=TT)
        used[0] = 0

        def split_area(n):
            area(n)
            assert used[0] <= SPLIT_ARENA
            return split_arena[:, used[0] - n:used[0]]
        ex_hi, ex_lo = (split_area(4 * SLOTS).rearrange("p (f s) -> p f s", f=4) for _ in range(2))
        y_hi, y_lo = split_area(D), split_area(D)
        spread = split_area(2 * T).rearrange("p (b t) -> p b t", b=2)
        pick_at = split_area(4 * SLOTS).rearrange("p (b t s) -> p b t s", b=2, t=TT)
        ident_r = split_area(P)
        gate_parts = split_area(2 * NE * TT).rearrange("p (h e t) -> p h e t", h=2, e=NE)
        used[0] = SPLIT_ARENA
        ex_sil, ex_rows = area(DE), area(DE)
        assert used[0] <= NE * T
        slot_gate = sb("slot_gate", [P, 2])
        gate_pick = sb("gate_pick", [P, 2, TT, 2], F32R)
        h2_hi, h2_lo = (h[:, :, :].rearrange("p k t -> p (k t)").rearrange("p (t d) -> p t d", t=TT)
                        for h in (h_hi, h_lo))
        xg_hi, xg_lo = (h[:, :, :, :].rearrange("p a b t -> p (a b t)").rearrange("p (k s) -> p k s", k=KT)
                        for h in (hid_hi, hid_lo))
        rank = gated[:, 2816:2880].rearrange("p (t e) -> p t e", t=TT)
        r_rank = gated[:, 2816:2880].rearrange("p (t e) -> p e t", t=TT)
        over = gated[:, 2880:2944].rearrange("p (t e) -> p t e", t=TT)
        most = gated[:, 2944:2945]
        fb_sil, fb_prod, fb_hid = (gated[:, 512 * q:512 * q + 512].rearrange("p (m t) -> p m t", m=2)
                                   for q in range(3))
        flag = stack.enter_context(nc.sbuf_tensor("flag", [P, 1], mybir.dt.int32))
        used[0] = 0
        qA = area(2048).rearrange("p (k t) -> p k t", k=8)
        kA = area(2048).rearrange("p (k t) -> p k t", k=8)
        vA = area(2048).rearrange("p (k f) -> p k f", k=2)
        qiA = area(1024).rearrange("p (k t) -> p k t", k=4)
        kiA = area(256)
        wiA = area(16).rearrange("p (t h) -> p t h", t=2)
        bias = area(3072).rearrange("p (h j) -> p h j", h=8)
        score = area(512).rearrange("p (t k) -> p t k", t=2)
        amask = area(512).rearrange("p (t k) -> p t k", t=2)
        relb = area(1024).rearrange("p (b k) -> p b k", b=2)
        lgA = area(1024).rearrange("p (b t k) -> p b t k", b=2, t=2)
        prA = area(1024).rearrange("p (b t k) -> p b t k", b=2, t=2)
        ptA = area(1024).rearrange("p (b k t) -> p b k t", b=2, k=2)
        mixA = area(2048).rearrange("p (k t) -> p k t", k=8)
        top8 = area(16).rearrange("p (t k) -> p t k", t=2)
        stA = area(64)
        used[0] = 0
        uB = area(6144).rearrange("p (k t) -> p k t", k=BT)
        vB = area(6144).rearrange("p (t f) -> p t f", t=2)
        wspT = area(1024).rearrange("p (g t) -> p g t", g=8)
        bspb = area(1024).rearrange("p (g t) -> p g t", g=8)
        wsum = area(1024).rearrange("p (g t) -> p g t", g=8)
        wsp = area(1024).rearrange("p (g t) -> p g t", g=8)
        binrow = arena[0:1, 15360:15360 + BH]
        stB = sm(64)
        affB = gated[:, 0:BT * P].rearrange("p (k t) -> p k t", k=BT)
        sqB = scr
        sil = gated[:, 0:1024].rearrange("p (b m t) -> p b m t", b=2, m=2)
        hid = gated[:, 1024:2048].rearrange("p (b m t) -> p b m t", b=2, m=2)

        spb = scr[:, 0:512].rearrange("p (j t k) -> p j t k", j=2, t=2)
        ropea = scr[:, 0:1024].rearrange("p (b k t) -> p b k t", b=2, k=2)
        ropeb = scr[:, 1024:2048].rearrange("p (b k t) -> p b k t", b=2, k=2)
        stdh, rstdh = gated[:, 0:1024], gated[:, 1024:2048]
        nmax, nbias, sums, rsum = (sm(16).rearrange("p (s m) -> p s m", m=2) for _ in range(4))
        reltab = sb("reltab", [32, HEADS2])
        reldist = scr[0:HEADS2, 512:1024]

        rows2d = lambda v: v.rearrange("(r q) -> r q", q=P)
        ROWS = [(rows1[0:48, :], rows2d(b_ada[0])), (rows1[48:56, :], rows2d(g_mix_norm[0])),
                (rows1[56:64, :], rows2d(g_ffn_norm[0])), (rows1[64:72, :], rows2d(g_final)),
                (rows1[72:120, :], norm_g_2.rearrange("l n (r q) -> (l n r) q", q=P)),
                (rows1[120:128, :], rows2d(final_g_2)),
                (rows2[0:8, :], rows2d(c[0])), (rows2[8:16, :], rows2d(c_ctx)),
                (rows2[16:40, :], rows2d(b_b_in_2[0, 0:BH])), (rows2[40:64, :], rows2d(b_ln_g_2[0])),
                (rows2[64:88, :], rows2d(b_ln_b_2[0])), (rows2[88:89, :], g_subln),
                (rows3[0:1, :], lambda_q1), (rows3[1:2, :], lambda_q2),
                (rows3[2:3, :], lambda_k1), (rows3[3:4, :], lambda_k2), (reltab[:, :], rel_table_2)]
        N_ROWS = len(ROWS)
        SIDE = [(wfo, w_fourier[0].rearrange("g c d -> c g d")),
                (wrt[:, :, 0:4], w_router_group[0].rearrange("(k p) n -> p k n", p=P)),
                (wrt[:, :, 4:36], w_router_expert[0].rearrange("(k p) n -> p k n", p=P)),
                (brt[0:1, 0:4], b_router_group), (brt[0:1, 4:36], b_router_expert)]
        N_SIDE = len(SIDE)

        ada_v = w_ada[0].rearrange("(k p) (u f) -> u p k f", p=P, f=UW)
        in_v = w_in[0].rearrange("(k p) (u f) -> u p k f", p=P, f=UW)
        out_v = w_out[0].rearrange("(k p) (u f) -> u p k f", p=P, f=UW)
        gate_v = w_gate[0].rearrange("e (k p) (u f) -> u e p k f", p=P, f=UW)
        up_v = w_up[0].rearrange("e (k p) (u f) -> u e p k f", p=P, f=UW)
        down_v = w_down[0].rearrange("e (u k p) f -> u e p k f", p=P, k=2)
        ffin_v = [ffn_w_in_2[i // 2, i % 2].rearrange("(k p) (u f) -> u p k f", p=P, f=UW) for i in range(4)]
        ffout_v = [ffn_w_out_2[i // 2, i % 2].rearrange("(u k p) f -> u p k f", p=P, k=2) for i in range(4)]
        aout_v = a_w_out_2[0].rearrange("(k p) (u f) -> u p k f", p=P, f=UW)
        ain_v = a_w_in_2[0].rearrange("(k p) f -> p k f", p=P)
        bin_v = b_w_in_2[0].rearrange("(k p) (u f) -> u p k f", p=P, f=UW)
        bout_v = b_w_out_2[0].rearrange("(u k p) f -> u p k f", p=P, k=2)
        A_UNITS = [3072, 3328, 3584] + [UW * u for u in range(12)]

        def slot_cols(u, w=UW):
            return ring[:, u % RING, 0:KT * w].rearrange("p (k f) -> p k f", k=KT)

        def slot_rows(u):
            return ring[:, u % RING, :].rearrange("p (k f) -> p k f", k=2)

        fin = arena[:, 0:2048]

        def halves(hi, v, w=UW, rows=False):
            a = hi[:, v % SPLIT, :]
            return a.rearrange("p (k f) -> p k f", k=2) if rows else a[:, 0:KT * w].rearrange("p (k f) -> p k f", k=KT)

        def landed(eng, u, i=None):
            n = 16 * (u // RING + 1)
            eng.wait_ge(weights_in[u % RING], n if i is None else i * (16 * TURN // RING) + n)

        TAIL = split_of(U_A + 2)

        def split_high(v, i=None):
            if v >= split_of(N_UNITS):
                return
            u, n = unit_of(v), KT * (136 if v == TAIL else UW)
            if v >= SPLIT:
                d = unit_of(v - SPLIT) + 1
                nc.scalar.wait_ge(unit_done, d if i is None else i * TURN + d)
            if v == TAIL:
                nc.scalar.wait_ge(tail_in, 16)
            landed(nc.scalar, u, i)
            nc.scalar.activation(w_hi[:, v % SPLIT, 0:n], ring[:, u % RING, 0:n], ACT.Copy).then_inc(w_hi_ready, 1)

        def split_low(v, i=None):
            if v >= split_of(N_UNITS):
                return
            u, n = unit_of(v), KT * (136 if v == TAIL else UW)
            nc.vector.wait_ge(w_hi_ready, v + 1 if i is None else i * TURN + (v + 1))
            nc.vector.tensor_tensor(w_lo[:, v % SPLIT, 0:n], ring[:, u % RING, 0:n],
                                    w_hi[:, v % SPLIT, 0:n].bitcast(F32), ALU.subtract).then_inc(w_lo_ready, 1)

        def after_feed(n):
            return split_of(U_F[n]) + 3 * FFC - 1 + SPLIT

        block = stack.enter_context(nc.Block())

        def experts(eng, step):
            step(0, None)
            step(1, None)
            with eng.Fori(0, (NE - 4) // 2) as i:
                step(2, i)
                step(3, i)
            step(NE - 2, None)
            step(NE - 1, None)

        def swiglu_steps(n):
            return (n - 2) // LOOP, list(range(2 + (n - 2) // LOOP * LOOP, n))

        @block.sync
        def _(sp):
            def vacant(u, i=None):
                p = u - RING
                if p < 0:
                    return
                v = split_of(p)
                if v is None or U_IN + 2 <= p < U_IN + 6:
                    sp.wait_ge(unit_done, p + 1 if i is None else i * TURN + (p + 1))
                if v is not None:
                    sp.wait_ge(w_lo_ready, v + 1 if i is None else i * TURN + (v + 1))

            def fetch(u, dst, src, i=None):
                vacant(u, i)
                sp.dma_start(dst, src).then_inc(weights_in[u % RING], 16)

            def swiglu_first(u0, gate, up):
                fetch(u0, slot_cols(u0), gate(0, 0, None))
                fetch(u0 + 1, slot_cols(u0 + 1), up(0, 0, None))
                fetch(u0 + 2, slot_cols(u0 + 2), gate(1, 1, None))

            def swiglu(u0, n, gate, up, down):
                def step(s, s_static, i):
                    u = u0 + 2 + 3 * (s_static - 1)
                    if s_static > 1 or i is not None:
                        fetch(u, slot_cols(u), gate(s_static, s, i), i)
                    fetch(u + 1, slot_cols(u + 1), up(s_static, s, i), i)
                    fetch(u + 2, slot_rows(u + 2), down(s_static - 1, s, i), i)
                step(1, 1, None)
                turns, rest = swiglu_steps(n)
                with sp.Fori(0, turns) as i:
                    for j in range(LOOP):
                        step(j, 2 + j, i)
                for s in rest:
                    step(s, s, None)
                u = u0 + 3 * n - 1
                fetch(u, slot_rows(u), down(n - 1, n, None))

            for a in range(8):
                fetch(U_ADA1 + a, slot_cols(U_ADA1 + a), ada_v[a])
            for a in range(8):
                fetch(U_IN + a, slot_cols(U_IN + a), in_v[a])
            for a in range(16):
                fetch(U_ADA2 + a, slot_cols(U_ADA2 + a), ada_v[8 + a])
            for a in range(4):
                fetch(U_OUT + a, slot_cols(U_OUT + a), out_v[a])

            def expert(e, i):
                u, at = U_MOE + 6 * e, (e if i is None else i * 2 + e)
                ii = i
                for half in range(2):
                    fetch(u + half, slot_cols(u + half), gate_v[half, at], ii)
                for half in range(2):
                    fetch(u + 2 + half, slot_cols(u + 2 + half), up_v[half, at], ii)
                for half in range(2):
                    fetch(u + 4 + half, slot_rows(u + 4 + half), down_v[half, at], ii)
            experts(sp, expert)

            def dense(view, off):
                def at(ch, _, i):
                    return view[off + ch if i is None else i * LOOP + (off + ch)]
                return at

            def feed_first(n):
                swiglu_first(U_F[n], dense(ffin_v[n], 0), dense(ffin_v[n], FFC))

            def feed(n):
                swiglu(U_F[n], FFC, dense(ffin_v[n], 0), dense(ffin_v[n], FFC), dense(ffout_v[n], 0))
            feed_first(0)
            sp.wait_ge(rank_ready, 1)
            with sp.If(sp.value_load(flag[0:1, 0:1], min_val=0, max_val=1)):
                sp.wait_ge(spread_done, NE)
                with sp.Fori(0, NE) as i:
                    for half in range(2):
                        sp.wait_ge(fb_down, i * 2 + (half + 1))
                        sp.dma_start(fb_w[:, 0, :].rearrange("p (k f) -> p k f", k=KT), gate_v[half, i]).then_inc(fb_in, 16)
                        sp.dma_start(fb_w[:, 1, :].rearrange("p (k f) -> p k f", k=KT), up_v[half, i]).then_inc(fb_in, 16)
                        sp.dma_start(fb_w[:, 2, :].rearrange("p (k f) -> p k f", k=2), down_v[half, i]).then_inc(fb_in, 16)

            feed(0)
            for a, lo in enumerate(A_UNITS):
                u = U_A + a
                if a == 2:
                    vacant(u)
                    tail = slot_cols(u, 136)
                    sp.dma_start(tail[:, :, 0:64], ain_v[:, :, lo:lo + 64]).then_inc(weights_in[u % RING], 16)
                    sp.dma_start(tail[:, :, 64:136], ain_v[:, :, lo:lo + 72]).then_inc(tail_in, 16)
                else:
                    fetch(u, slot_cols(u), ain_v[:, :, lo:lo + UW])
            for a in range(4):
                fetch(U_AOUT + a, slot_cols(U_AOUT + a), aout_v[a])
            feed_first(1)
            feed(1)
            feed_first(2)
            feed(2)
            for a in range(24):
                fetch(U_B + a, slot_cols(U_B + a), bin_v[(a + 12) % 24])
            for a in range(12):
                fetch(U_BOUT + a, slot_rows(U_BOUT + a), bout_v[a])
            feed_first(3)
            feed(3)
            for t in range(TT):
                sp.wait_ge(fin_sb, t + 1)
                sp.dma_start(out[0, t * P:(t + 1) * P, :], fin[:, t * D:(t + 1) * D]).then_inc(out_done, 16)
            sp.wait_ge(out_done, 16 * TT)

        @block.tensor
        def _(pe):
            mm = nc.tensor.matmul

            def arrived(u, i=None):
                landed(pe, u, i)

            def split(u, i=None):
                v = split_of(u)
                pe.wait_ge(w_lo_ready, v + 1 if i is None else i * TURN + (v + 1))
                return v

            def triple(dst, w, x, first, last):
                mm(dst, w[0], x[0], start=first, stop=False, skip_group_check=True)
                mm(dst, w[0], x[1], start=False, stop=False, skip_group_check=True)
                return mm(dst, w[1], x[0], start=False, stop=last, skip_group_check=True)

            def project3(dst, v, fresh=None):
                wh, wl = halves(w_hi, v), halves(w_lo, v)
                for k in range(KT):
                    if fresh is not None:
                        pe.wait_ge(h_lo_ready, fresh + k + 1)
                    for m in range(2):
                        f = slice(m * P, (m + 1) * P)
                        last = triple(dst[:, m * T:(m + 1) * T], (wh[:, k, f], wl[:, k, f]),
                                      (h_hi[:, k, :], h_lo[:, k, :]), k == 0 and m == 0, k == KT - 1)
                return last

            def project_rows3(dst, v, close_row=None, fresh=None):
                wh, wl = halves(w_hi, v), halves(w_lo, v)
                for t in range(TT):
                    r = slice(t * P, (t + 1) * P)
                    for k in range(KT):
                        if fresh is not None and t == 0:
                            pe.wait_ge(h_lo_ready, fresh + k + 1)
                        last = triple(dst[:, t * UW:(t + 1) * UW], (h_hi[:, k, r], h_lo[:, k, r]),
                                      (wh[:, k, :], wl[:, k, :]), k == 0, not close_row and k == KT - 1)
                    if close_row:
                        last = close_row(dst, t)
                return last

            def project(dst, w, src):
                for m in range(2):
                    for k in range(KT):
                        last = mm(dst[:, m * T:(m + 1) * T], w[:, k, m * P:(m + 1) * P], src[:, k, :],
                                  start=(k == 0), stop=(k == KT - 1))
                return last

            def project_rows(dst, w, src):
                for t in range(TT):
                    for k in range(KT):
                        last = mm(dst[:, t * UW:(t + 1) * UW], src[:, k, t * P:(t + 1) * P], w[:, k, :],
                                  start=(k == 0), stop=(k == KT - 1))
                return last

            def norm(n, bank):
                sq = scr[:, :].rearrange("p (k t) -> p k t", k=KT)
                for k in range(KT):
                    if k % 2 == 0:
                        pe.wait_ge(sq_ready, 4 * n + k // 2 + 1)
                    last = mm(wk[:, bank, 0:T], ones, sq[:, k, :], start=(k == 0), stop=(k == KT - 1))
                last.then_inc(ss_ready, 1)

            pe.wait_ge(consts_in, 16)
            pe.wait_ge(rows_in, 16 * N_ROWS)
            nc.tensor.transpose(wk[:, 0, 0:P], rows1, ident)
            nc.tensor.transpose(wk[:, 0, P:P + NR2], rows2[0:NR2, :], ident[0:NR2, 0:NR2])
            nc.tensor.transpose(wk[0:64, 0, 256:260], rows3[0:4, :], ident[0:4, 0:4])
            mm(wk[0:HEADS2, 1, :], reltab[:, :], buckets[0:32, :], start=True, stop=True).then_inc(vec_ps, 1)
            pe.wait_ge(x_in, 16)
            for t in range(TT):
                for k in range(KT):
                    last = nc.tensor.transpose(acc[:, k, t * P:(t + 1) * P], x_rows[:, t, k * P:(k + 1) * P], ident)
            last.then_inc(x_ps, 1)
            pe.wait_ge(ctx_in, 16)
            pe.wait_ge(cols_ready, 3)
            pe.wait_ge(reldist_sb, 1)
            wkf = wk[:, :, :].rearrange("p b (c t) -> p (b c) t", t=T)
            for t in range(TT):
                for k in range(KT):
                    last = nc.tensor.transpose(wkf[:, k, t * P:(t + 1) * P], c_rows[:, t, k * P:(k + 1) * P], ident)
            last.then_inc(ctx_ps, 1)

            def ada(u, m0):
                arrived(u)
                for m in range(2):
                    for k in range(KT):
                        last = mm(accf[:, 1024 + 2 * (m0 + m):1024 + 2 * (m0 + m) + 2],
                                  slot_cols(u)[:, k, m * P:(m + 1) * P], csil[:, k, :],
                                  start=(k == 0), stop=(k == KT - 1))
                return last.then_inc(unit_done, 1)

            pe.wait_ge(csil_ready, 1)
            pe.wait_ge(x_ready, 1)
            pe.wait_ge(ctx_ready, 1)
            for a in range(8):
                ada(U_ADA1 + a, 2 * a)
            pe.wait_ge(lamp_ready, 1)
            mm(wk[:, 2, 0:2], ones[0:64, :], lam_prod[0:64, :], start=True, stop=True).then_inc(lam_ps, 1)
            norm(0, 0)
            norm(1, 1)

            g = [0]

            def group(fill, ends_unit=False):
                n = g[0]
                if n >= 4:
                    pe.wait_ge(grp_out, n - 3)
                fill(wk[:, n % 4, :]).then_inc(unit_done if ends_unit else grp_ps, 1)
                g[0] += 1

            pe.wait_ge(h_shifted, 1)
            pe.wait_ge(std_ready, 2)
            pe.wait_ge(lam_ready, 1)

            for a in range(2):
                v = split(U_IN + a)
                group(lambda b: project3(b, v, fresh=None if a else 0), ends_unit=True)
            for a in range(2, 4):
                v, w = split(U_IN + a), slot_cols(U_IN + a)
                arrived(U_IN + a)
                group(lambda b: project3(b, v))
                group(lambda b: project(b, w, hcT), ends_unit=True)
            for a in range(4, 6):
                v, w = split(U_IN + a), slot_cols(U_IN + a)
                arrived(U_IN + a)
                group(lambda b: project_rows3(b, v))
                group(lambda b: project_rows(b, w, hcT), ends_unit=True)
            for a in range(6, 8):
                v = split(U_IN + a)
                group(lambda b: project_rows3(b, v), ends_unit=True)

            for r in range(4):
                if r == 0:
                    pe.wait_ge(mod_ready, 1)
                pe.wait_ge(grp_out, (1, 2, 3, 5)[r])
                mm(accf[:, r * 512:(r + 1) * 512], rot, raw[:, 2 * r:2 * r + 2, :].rearrange("p k t -> p (k t)"),
                   start=True, stop=True).then_inc(rope_ps, 1)

            def over_tokens(b, gr):
                for a, table in enumerate((dft_cos, dft_sin)):
                    for t in range(TT):
                        last = mm(b[:, a * T:(a + 1) * T], ff[:, t, gr * P:(gr + 1) * P], table[:, t, :],
                                  start=(t == 0), stop=(t == TT - 1))
                return last

            def over_channels(b, pair):
                for j in range(2):
                    gr = 2 * pair + j
                    mm(b[:, j * T:(j + 1) * T], dft_ccos, dft_sb[:, gr, 0, :], start=True, stop=False)
                    last = mm(b[:, j * T:(j + 1) * T], dft_csin, dft_sb[:, gr, 1, :], start=False, stop=True)
                return last

            def own_matrix(b, pair):
                for j in range(2):
                    gr = 2 * pair + j
                    last = mm(b[:, j * T:(j + 1) * T], wfo[:, gr, :], frT[:, gr, :], start=True, stop=True)
                return last

            pe.wait_ge(grp_out, 12)
            for gr in range(4):
                group(lambda b: over_tokens(b, gr))
            pe.wait_ge(grp_out, 16)
            for pair in range(2):
                group(lambda b: over_channels(b, pair))
            pe.wait_ge(grp_out, 18)
            pe.wait_ge(side_in, 16 * N_SIDE)
            for pair in range(2):
                group(lambda b: own_matrix(b, pair))

            pe.wait_ge(rope_done, 4)

            def scores(s):
                h, t = divmod(s, TT)
                if s < 2:
                    pe.wait_ge(grp_out, 20)
                else:
                    pe.wait_ge(exp_ready, s - 1)
                for m in range(2):
                    last = mm(wk[:, 2 * (s % 2) + m, :], qT[64 * m:64 * m + 64, h, t * P:(t + 1) * P],
                              kT[64 * m:64 * m + 64, h, :], start=True, stop=True)
                last.then_inc(sc_ps, 1)

            def turn(s):
                pe.wait_ge(attn_ready, s + 1)
                if s >= 2:
                    pe.wait_ge(at_ready, s - 1)
                for k in range(4):
                    last = nc.tensor.transpose(accf[:, (s % 2) * 512 + k * P:(s % 2) * 512 + (k + 1) * P],
                                               attn[:, s % 2, k * P:(k + 1) * P], ident)
                last.then_inc(at_ps, 1)

            def values(h):
                pe.wait_ge(at_ready, 2 * h + 2)
                if h >= 1:
                    pe.wait_ge(pv_ready, h)
                o = accf[:, 1536 + (h % 2) * T:1536 + (h % 2 + 1) * T]
                for k in range(4):
                    last = mm(o, vv[:, k, h * P:(h + 1) * P], attnT[:, h % 2, k, :], start=(k == 0), stop=(k == 3))
                last.then_inc(pv_ps, 1)

            scores(0)
            for s in range(8):
                if s + 1 < 8:
                    scores(s + 1)
                for a in (2 * s, 2 * s + 1):
                    last = ada(U_ADA2 + a, 16 + 2 * a)
                    if a == 15:
                        pass
                turn(s)
                if s % 2 == 1 and s >= 3:
                    values(s // 2 - 1)
            values(3)
            pe.wait_ge(sub_sq, 1)
            for j in range(2):
                last = mm(wk[:, j, :], ones, scr[:, j * 512:(j + 1) * 512], start=True, stop=True)
            last.then_inc(sub_ss, 1)

            pe.wait_ge(mix_lo_ready, 2)
            for a in range(4):
                last = project3(accf[:, a * 512:(a + 1) * 512], split(U_OUT + a))
                last.then_inc(unit_done, 1)
            norm(2, 0)

            pe.wait_ge(h_shifted, 2)
            pe.wait_ge(side_in, 16 * N_SIDE)
            for t in range(TT):
                o = wk[:, 1, 64 * t:64 * t + 36]
                for k in range(KT):
                    mm(o, hT[:, k, t * P:(t + 1) * P], wrt[:, k, :], start=(k == 0), stop=False)
                last = mm(o, ones[0:1, :], brt[0:1, :], start=False, stop=True)
            last.then_inc(rt_ps, 1)
            for t in range(TT):
                for k in range(KT):
                    last = nc.tensor.transpose(accf[:, t * D + k * P:t * D + (k + 1) * P],
                                               hT[:, k, t * P:(t + 1) * P], ident)
            last.then_inc(h2_ps, 1)
            pe.wait_ge(rt_g, 1)
            chosen = [rt[:, 80 * t:80 * t + NE] for t in range(TT)]
            mm(wk[:, 3, 0:NE], before, chosen[0], start=True, stop=True)
            mm(wk[:, 3, NE:2 * NE], ones, chosen[0], start=True, stop=False)
            mm(wk[:, 3, NE:2 * NE], before, chosen[1], start=False, stop=True)
            mm(wk[:, 3, 64:64 + NE], ones, chosen[0], start=True, stop=False)
            mm(wk[:, 3, 64:64 + NE], ones, chosen[1], start=False, stop=True).then_inc(rank_ps, 1)

            def gather(e, i, q):
                n = (lambda v: v if i is None else i * 4 + v)
                if q == 0:
                    pe.wait_ge(pick_ready, e + 1 if i is None else i * 2 + (e + 1))
                    if e:
                        pe.wait_ge(spread_ready, e if i is None else i * 2 + e)
                elif q == 2:
                    pe.wait_ge(xg_hi_ready, n(2 * e + 1))
                elif q == 3:
                    pe.wait_ge(xg_lo_ready, n(2 * e + 1))
                src = h2_lo if q % 2 else h2_hi
                for k in range(4 * (q // 2), 4 * (q // 2) + 4):
                    for t in range(TT):
                        last = mm(wk[:, q % 2, (k % 4) * SLOTS:(k % 4 + 1) * SLOTS], src[:, t, k * P:(k + 1) * P],
                                  pick_at[:, e % 2, t, :], start=(t == 0), stop=(t == TT - 1))
                last.then_inc(xg_lo_ps if q % 2 else xg_hi_ps, 1)

            def turn_pick(e, i):
                n = 2 * e + 2
                pe.wait_ge(xg_hi_ready, n if i is None else i * 4 + n)
                for t in range(TT):
                    mm(wk[:, 0, t * P:(t + 1) * P], pick_at[:, e % 2, t, :], ident_r, start=True, stop=True)
                for t in range(TT):
                    last = mm(wk[:, 0, T:T + 2], pick_at[:, e % 2, t, :], gate_pick[:, e % 2, t, :],
                              start=(t == 0), stop=(t == TT - 1))
                last.then_inc(spread_ps, 1)

            def scatter(e):
                for m in range(KT):
                    mm(acc[:, m, :], y_hi[:, m * P:(m + 1) * P], spread[:, e % 2, :], start=(e == 0 and m % 2 == 0),
                       stop=True, skip_group_check=True)
                    last = mm(acc[:, m, :], y_lo[:, m * P:(m + 1) * P], spread[:, e % 2, :], start=False,
                              stop=True, skip_group_check=True)
                last.then_inc(spread_done, 1)

            def expert(e, i):
                def at(v, n=1):
                    return v if i is None else i * (2 * n) + v
                u = U_MOE + 6 * e
                pe.wait_ge(xg_hi_ready, at(2 * e + 2, 2))
                pe.wait_ge(xg_lo_ready, at(2 * e + 2, 2))
                if e:
                    pe.wait_ge(y_lo_ready, at(2 * e - 1, 2))
                for j in range(4):
                    if j == 2 and e:
                        pe.wait_ge(y_lo_ready, at(2 * e, 2))
                    v = split(u + j, i)
                    wh, wl = halves(w_hi, v), halves(w_lo, v)
                    o = wk[:, 2 + j // 2, (j % 2) * UW:(j % 2 + 1) * UW]
                    for k in range(KT):
                        last = triple(o, (xg_hi[:, k, :], xg_lo[:, k, :]), (wh[:, k, :], wl[:, k, :]),
                                      k == 0, k == KT - 1)
                    last.then_inc(unit_done, 1)
                if e:
                    scatter(e - 1)
                if e < NE - 1:
                    gather(e + 1, i, 0)
                    gather(e + 1, i, 1)
                pe.wait_ge(ex_hidden, at(e + 1))
                for f in range(4):
                    last = nc.tensor.transpose(wk[:, 2, f * SLOTS:(f + 1) * SLOTS], ex_rows[:, f * P:(f + 1) * P], ident)
                last.then_inc(turned_ps, 1)
                if e < NE - 1:
                    gather(e + 1, i, 2)
                    gather(e + 1, i, 3)
                pe.wait_ge(turned_lo_ready, at(e + 1))
                for j in range(2):
                    v = split(u + 4 + j, i)
                    wh, wl = halves(w_hi, v, rows=True), halves(w_lo, v, rows=True)
                    for half in range(2):
                        c = slice(half * 512, (half + 1) * 512)
                        for f in range(2):
                            last = triple(wk[:, 2 + half, :], (ex_hi[:, 2 * j + f, :], ex_lo[:, 2 * j + f, :]),
                                          (wh[:, f, c], wl[:, f, c]), j == 0 and f == 0, j == 1 and f == 1)
                        if j and not half:
                            last.then_inc(y0_ps, 1)
                    last.then_inc(unit_done, 1)
                if e < NE - 1:
                    turn_pick(e + 1, i)
            pe.wait_ge(h2_ready, 1)
            pe.wait_ge(rank_ready, 1)
            for q in range(4):
                gather(0, None, q)
            turn_pick(0, None)
            experts(pe, expert)
            pe.wait_ge(y_lo_ready, 2 * NE)
            pe.wait_ge(spread_ready, NE)
            scatter(NE - 1)

            with pe.If(pe.value_load(flag[0:1, 0:1], min_val=0, max_val=1)):
                for t in range(TT):
                    last = nc.tensor.transpose(wk[0:NE, 2, t * P:(t + 1) * P], over[:, t, :], ident)
                    if t == 0:
                        last.then_inc(fb_down, 1)
                last.then_inc(gt_ps, 1)
                with pe.Fori(0, NE) as i:
                    for half in range(2):
                        n = i * 2 + (half + 1)
                        pe.wait_ge(fb_in, i * 96 + 48 * (half + 1))
                        for j in range(2):
                            last = project(wk[:, j, :], fb_w[:, j, :].rearrange("p (k f) -> p k f", k=KT), hT)
                        last.then_inc(fb_up, 1)
                        pe.wait_ge(fb_hidden, n)
                        w = fb_w[:, 2, :].rearrange("p (k f) -> p k f", k=2)
                        for k in range(2):
                            for m in range(KT):
                                last = mm(acc[:, m, :], w[:, k, m * P:(m + 1) * P], fb_hid[:, k, :],
                                          start=False, stop=True, skip_group_check=True)
                        last.then_inc(fb_down, 1)

            def down3(v, x, opens):
                wh, wl = halves(w_hi, v, rows=True), halves(w_lo, v, rows=True)
                for k in range(2):
                    for m in range(KT):
                        f = slice(m * P, (m + 1) * P)
                        last = triple(acc[:, m, :], (wh[:, k, f], wl[:, k, f]), (x[0][:, k, :], x[1][:, k, :]),
                                      opens and k == 0 and m % 2 == 0, True)
                return last

            def swiglu(u0, c0, ch0, n, fresh):
                def gate_up(u, ch, i):
                    for j in range(2):
                        v = split(u + j, i)
                        if j == 0:
                            if i is not None:
                                pe.wait_ge(hidden_ready, i * LOOP + (c0 + ch - 1))
                            elif ch >= 2:
                                pe.wait_ge(hidden_ready, c0 + ch - 1)
                        last = project3(wk[:, 2 * (ch % 2) + j, :], v, fresh if ch == 0 and j == 0 and i is None else None)
                        last.then_inc(unit_done, 1)

                def down(u, ch, i):
                    v = split(u, i)
                    n = ch0 + ch + 1
                    pe.wait_ge(hid_lo_ready, n if i is None else i * LOOP + n)
                    down3(v, (hid_hi[:, ch % 2, :, :], hid_lo[:, ch % 2, :, :]), ch == 0).then_inc(unit_done, 1)

                gate_up(u0, 0, None)

                def step(s, i):
                    u = u0 + 2 + 3 * (s - 1)
                    gate_up(u, s, i)
                    down(u + 2, s - 1, i)
                step(1, None)
                turns, rest = swiglu_steps(n)
                with pe.Fori(0, turns) as i:
                    for j in range(LOOP):
                        step(2 + j, i)
                for s in rest:
                    step(s, None)
                down(u0 + 3 * n - 1, n - 1, None)

            norm(3, 0)
            norm(4, 0)

            def feed(n, j):
                swiglu(U_F[n], C_F[n], C_H[n], FFC, KT * j)
            feed(0, 1)

            norm(5, 0)
            g0 = 20
            def aunit(a, rows=False, fresh=None):
                v = split(U_A + a)
                group(lambda b: project_rows3(b, v) if rows else project3(b, v, fresh), ends_unit=True)

            aunit(0, fresh=2 * KT)
            aunit(1)

            def tail(b):
                v = split(U_A + 2)
                wh, wl = halves(w_hi, v, 136), halves(w_lo, v, 136)
                for k in range(KT):
                    triple(b[:, 0:T], (wh[:, k, 0:P], wl[:, k, 0:P]), (h_hi[:, k, :], h_lo[:, k, :]),
                           k == 0, k == KT - 1)
                for t in range(TT):
                    r = slice(t * P, (t + 1) * P)
                    for k in range(KT):
                        last = triple(b[:, T + 8 * t:T + 8 * t + 8], (h_hi[:, k, r], h_lo[:, k, r]),
                                      (wh[:, k, P:P + 8], wl[:, k, P:P + 8]), k == 0, k == KT - 1)
                return last
            group(tail, ends_unit=True)
            aunit(3)

            def index_scores(b, t, pair, odd):
                for j in range(2):
                    h = 4 * pair + 2 * j + odd
                    last = mm(b[:, j * T:(j + 1) * T], qiA[64 * odd:64 * odd + 64, h // 2, t * P:(t + 1) * P],
                              kiA[64 * odd:64 * odd + 64, :], start=True, stop=True)
                return last
            pe.wait_ge(grp_out, g0 + 3)
            for t in range(TT):
                for pair in range(2):
                    for odd in range(2):
                        group(lambda b: index_scores(b, t, pair, odd))
            for a in range(4, 11):
                aunit(a)
            for a in range(11, 15):
                aunit(a, rows=True)

            def a_scores(h):
                if h < 2:
                    pe.wait_ge(grp_out, g0 + 23)
                else:
                    pe.wait_ge(a_max, h - 1)
                if h == 0:
                    pe.wait_ge(bias_in, 16)
                for t in range(TT):
                    o = wk[:, h % 2, t * T:(t + 1) * T]
                    mm(o, qA[:, h, t * P:(t + 1) * P], kA[:, h, :], start=True, stop=False)
                    last = mm(o, flip, bias[:, h, P * (1 - t):P * (1 - t) + T], start=False, stop=True)
                last.then_inc(a_ps, 1)

            def a_turn(h):
                pe.wait_ge(a_norm, h + 1)
                if h >= 2:
                    pe.wait_ge(apt_ready, h - 1)
                for k in range(2):
                    for t in range(TT):
                        last = nc.tensor.transpose(wk[:, 2 + h % 2, k * T + t * P:k * T + (t + 1) * P],
                                                   prA[:, h % 2, t, k * P:(k + 1) * P], ident)
                last.then_inc(apt_ps, 1)

            def a_values(h):
                pe.wait_ge(apt_ready, h + 1)
                if h >= 2:
                    pe.wait_ge(apv_ready, h - 1)
                o = accf[:, (h % 2) * 512:(h % 2) * 512 + T]
                for k in range(2):
                    last = mm(o, vA[:, k, h * P:(h + 1) * P], ptA[:, h % 2, k, :], start=(k == 0), stop=(k == 1))
                last.then_inc(apv_ps, 1)

            a_scores(0)
            for h in range(HEADS2):
                if h + 1 < HEADS2:
                    a_scores(h + 1)
                a_turn(h)
                if h >= 1:
                    a_values(h - 1)
            a_values(HEADS2 - 1)
            pe.wait_ge(mix_lo_ready, 2 + HEADS2)
            for a in range(4):
                last = project3(accf[:, a * 512:(a + 1) * 512], split(U_AOUT + a))
                last.then_inc(unit_done, 1)

            norm(6, 0)
            feed(1, 3)
            norm(7, 0)
            feed(2, 4)

            pe.wait_ge(wsp_masked, 1)
            for gr in range(BGROUPS):
                last = nc.tensor.transpose(wkf[:, 4 + gr // 2, (gr % 2) * P:(gr % 2 + 1) * P], wsp[:, gr, :], ident)
            last.then_inc(wsp_ps, 1)
            norm(8, 0)
            pe.wait_ge(std_ready, 9)
            pe.wait_ge(wsp_ready, 1)
            for j in range(2):
                last = mm(wk[:, j, :], ones, wspT[:, 4 * j:4 * j + 4, :].rearrange("p g t -> p (g t)"),
                          start=True, stop=True)
            last.then_inc(w1_ps, 1)
            pe.wait_ge(w1_ready, 1)
            pe.wait_ge(binrow_in, 16)
            gb = g[0]
            for a in range(12):
                v = split(U_B + a)

                def close_row(b, t):
                    return mm(b[:, t * UW:(t + 1) * UW], ones[0:1, :], binrow[0:1, a * UW:(a + 1) * UW],
                              start=False, stop=True, skip_group_check=True)
                group(lambda b: project_rows3(b, v, close_row, None if a else 5 * KT), ends_unit=True)
            for a in range(12, 24):
                v = split(U_B + a)
                group(lambda b: project3(b, v), ends_unit=True)
            pe.wait_ge(ln_ready, 2)
            pe.wait_ge(grp_out, g[0])

            def spatial(q):
                if q >= 4:
                    pe.wait_ge(sp_done, q - 3)
                for j in range(2):
                    f = 2 * q + j
                    for t in range(TT):
                        last = mm(wk[:, q % 4, j * T + t * P:j * T + (t + 1) * P], vB[:, t, f * P:(f + 1) * P],
                                  wspT[:, f // 3, :], start=True, stop=True)
                last.then_inc(sp_ps, 1)
            for q in range(4):
                spatial(q)
            for a in range(12):
                v = split(U_BOUT + a)
                pe.wait_ge(hid_lo_ready, C_HB + a + 1)
                down3(v, (hid_hi[:, a % 2, :, :], hid_lo[:, a % 2, :, :]), a == 0).then_inc(unit_done, 1)
                if a + 4 < 12:
                    spatial(a + 4)

            norm(9, 0)
            feed(3, 6)
            norm(10, 0)
            pe.wait_ge(h_scaled, 11 * KT)
            for t in range(TT):
                for k in range(KT):
                    last = nc.tensor.transpose(accf[:, t * D + k * P:t * D + (k + 1) * P],
                                               hT[:, k, t * P:(t + 1) * P], ident)
                last.then_inc(fin_ps, 1)

        @block.scalar
        def _(act):
            chain = [0]

            def link(ins):
                chain[0] += 1
                ins.then_inc(act_step, 1)
                act.wait_ge(act_step, chain[0])

            A = nc.scalar.activation
            act.dma_start(con[:, :], consts).then_inc(consts_in, 16)
            for dst, src in ROWS:
                act.dma_start(dst, src).then_inc(rows_in, 16)
            act.dma_start(x_rows, x[0].rearrange("(t p) d -> p t d", p=P)).then_inc(x_in, 16)
            act.dma_start(c_rows, ctx[0].rearrange("(t p) d -> p t d", p=P)).then_inc(ctx_in, 16)
            for dst, src in SIDE:
                act.dma_start(dst, src).then_inc(side_in, 16)

            act.wait_ge(vec_ps, 1)
            A(cols[:, 0:P], wk[:, 0, 0:P], ACT.Copy).then_inc(cols_ready, 1)
            A(cols[:, P:P + NR2], wk[:, 0, P:P + NR2], ACT.Copy).then_inc(cols_ready, 1)
            A(lam_cols[0:64, :], wk[0:64, 0, 256:260], ACT.Copy).then_inc(cols_ready, 1)
            A(reldist[:, :], wk[0:HEADS2, 1, :], ACT.Copy).then_inc(reldist_sb, 1)
            act.wait_ge(reldist_sb, 1)
            act.dma_start(reldist_dram, reldist[:, :]).then_inc(reldist_out, 16)
            act.wait_ge(cols_ready, 3)
            A(csil, c_cols.rearrange("p (j k) -> p k j", j=2), ACT.Silu).then_inc(csil_ready, 1)
            act.wait_ge(ctx_ps, 1)
            A(cT.rearrange("p k t -> p (k t)"), wk[:, :, :].rearrange("p b n -> p (b n)"), ACT.Copy).then_inc(ctx_ready, 1)
            act.wait_ge(ctx_ready, 1)

            def square(n, src, c, after=None):
                if after is not None:
                    act.wait_ge(after[0], after[1] + after[2] * (c + 1))
                A(scr[:, 2 * c * T:(2 * c + 2) * T], src[:, 2 * c:2 * c + 2, :].rearrange("p k t -> p (k t)"),
                  ACT.Square).then_inc(sq_ready, 1)

            def root(n, bank):
                act.wait_ge(ss_ready, n + 1)
                A(std[:, 0:T], wk[:, bank, 0:T], ACT.Sqrt, bias=eps_col, scale=1.0 / D).then_inc(std_ready, 1)

            def norm(n, src, bank, after=None, last_split=None):
                for c in range(4):
                    square(n, src, c, after)
                if last_split is not None:
                    split_high(last_split)
                root(n, bank)

            def shift(n, dst, j, m0):
                for k in range(KT):
                    act.wait_ge(h_scaled, n * KT + k + 1)
                    if n == 1:
                        A(h_hi[:, k, :], dst[:, k, :], ACT.Identity, bias=mod[:, m0 + k, j:j + 1])
                    last = A(dst[:, k, :], dst[:, k, :], ACT.Identity, bias=mod[:, m0 + k, j:j + 1])
                    if n == 1:
                        last.then_inc(h_hi_ready, 1)
                if n != 1:
                    last.then_inc(h_shifted, 1)

            def split_norm(n):
                for k in range(KT):
                    act.wait_ge(h_scaled, n * KT + k + 1)
                    A(h_hi[:, k, :], hT[:, k, :], ACT.Copy).then_inc(h_hi_ready, 1)

            act.wait_ge(const_set, 1)
            act.wait_ge(reldist_out, 16)
            norm(0, cT, 0)
            act.wait_ge(h_scaled, KT)
            act.wait_ge(x_ready, 1)
            norm(1, xT, 1)
            act.wait_ge(mod_ready, 1)
            for v in range(SPLIT):
                split_high(v)
            shift(0, hcT, 1, 0)
            shift(1, hT, 0, 0)
            act.wait_ge(lam_ps, 1)
            A(lam_exp, wk[:, 2, 0:2], ACT.Exp).then_inc(lame_ready, 1)

            g, loose = [0], [0]

            def bank(unit=None):
                if unit is None:
                    loose[0] += 1
                    act.wait_ge(grp_ps, loose[0])
                else:
                    act.wait_ge(unit_done, unit + 1)
                g[0] += 1
                return wk[:, (g[0] - 1) % 4, :]

            def take(dst, unit=None, two=False, scale=1.0):
                b = bank(unit)
                A(dst, b.rearrange("p (k t) -> p k t", k=2) if two else b, ACT.Copy, scale=scale).then_inc(grp_out, 1)

            def half(a, n=2):
                return a.rearrange("p k t -> p (k t)") if len(a.shape) == 3 else a
            take(half(raw[:, 0:2, :]), U_IN)
            split_high(3)
            take(half(raw[:, 2:4, :]), U_IN + 1)
            split_high(4)
            for j in range(2):
                take(half(raw[:, 4 + 2 * j:6 + 2 * j, :]))
                take(kT[:, 2 * j:2 * j + 2, 0:CTX], U_IN + 2 + j, two=True)
                split_high(5 + j)
            for j in range(2):
                take(vv[:, 2:4, j * UW:(j + 1) * UW], two=True)
                take(vv[:, 0:2, j * UW:(j + 1) * UW], U_IN + 4 + j, two=True)
                if j == 0:
                    split_high(7)
            for j in range(2):
                take(ff[:, :, j * UW:(j + 1) * UW], U_IN + 6 + j, two=True)
            for gr in range(4):
                take(dft_sb[:, gr, :, :].rearrange("p a n -> p (a n)"))
            for pair in range(2):
                take(half(frT[:, 2 * pair:2 * pair + 2, :]))
            act.wait_ge(rope_done, 4)
            for pair in range(2):
                b = bank()
                A(half(mixT[:, 4 + 2 * pair:6 + 2 * pair, :]), b, ACT.Copy)
                A(half(h_hi[:, 4 + 2 * pair:6 + 2 * pair, :]), b, ACT.Copy).then_inc(grp_out, 1)

            def exps(s):
                act.wait_ge(max_ready, s + 1)
                if s >= 2:
                    act.wait_ge(attn_ready, s - 1)
                for m in range(2):
                    last = A(prob[:, s % 2, m, :], wk[:, 2 * (s % 2) + m, :], ACT.Exp, bias=nbias[:, s, m:m + 1],
                             scale=HD1 ** -0.5, accum_out=sums[:, s, m:m + 1])
                last.then_inc(exp_ready, 1)

            def turned(s):
                h, t = divmod(s, TT)
                act.wait_ge(at_ps, s + 1)
                if h >= 2:
                    act.wait_ge(pv_ps, h - 1)
                A(attnT[:, h % 2, :, t * P:(t + 1) * P],
                  accf[:, (s % 2) * 512:(s % 2) * 512 + 512].rearrange("p (k t) -> p k t", k=4),
                  ACT.Copy).then_inc(at_ready, 1)

            def head_out(h):
                act.wait_ge(pv_ps, h + 1)
                A(heads_o[:, h, :], accf[:, 1536 + (h % 2) * T:1536 + (h % 2 + 1) * T], ACT.Copy).then_inc(pv_ready, 1)

            exps(0)
            for s in range(8):
                if s + 1 < 8:
                    exps(s + 1)
                turned(s)
                if s % 2 == 1 and s >= 3:
                    head_out(s // 2 - 1)
            head_out(3)
            act.wait_ge(pv_ready, 4)
            A(scr[:, 0:1024], heads_o.rearrange("p h t -> p (h t)"), ACT.Square).then_inc(sub_sq, 1)
            act.wait_ge(sub_ss, 1)
            A(stdh[:, :], wk[:, 0:2, :].rearrange("p b n -> p (b n)"), ACT.Sqrt, bias=eps_col,
              scale=1.0 / P).then_inc(sub_std, 1)

            for v in range(8, 11):
                split_high(v)
            act.wait_ge(sub_done, 1)
            A(h_hi[:, 0:4, :], mixT[:, 0:4, :], ACT.Copy).then_inc(mix_hi_ready, 1)
            split_high(11)

            norm(2, xT, 0, (resid_ready, 0, 1))
            act.wait_ge(mod_ready, 2)
            shift(2, hT, 0, 24)
            act.wait_ge(rt_ps, 1)
            A(lg, wk[:, 1, 0:128].rearrange("p (t n) -> p t n", t=2)[:, :, 0:36], ACT.Copy).then_inc(rt_sb, 1)
            act.wait_ge(h2_ps, 1)
            A(h2_hi.rearrange("p t d -> p (t d)"), accf, ACT.Copy).then_inc(h2_hi_ready, 1)
            for v in range(12, 12 + SPLIT):
                split_high(v)
            act.wait_ge(rt_max, 1)
            for t in range(TT):
                A(rt[:, 400 + 4 * t:404 + 4 * t], lg[:, t, 0:4], ACT.Exp, bias=rt[:, 336 + t:337 + t],
                  accum_out=rt[:, 338 + t:339 + t])
                A(rt[:, 80 * t + 40:80 * t + 72], rt[:, 80 * t:80 * t + 32], ACT.Exp, bias=rt[:, 340 + t:341 + t])
                last = A(rt[:, 342 + t:343 + t], rt[:, 321 + 8 * t:322 + 8 * t], ACT.Exp, bias=rt[:, 340 + t:341 + t])
            last.then_inc(rt_exp, 1)
            def gathered(e, i, half):
                n = 2 * e + half + 1
                act.wait_ge(xg_hi_ps, n if i is None else i * 4 + n)
                A(xg_hi[:, 4 * half:4 * half + 4, :].rearrange("p k s -> p (k s)"), wk[:, 0, :],
                  ACT.Copy).then_inc(xg_hi_ready, 1)

            def expert(e, i):
                def at(v, n=1):
                    return v if i is None else i * (2 * n) + v
                u = U_MOE + 6 * e
                v = split_of(u) + SPLIT
                split_high(v, i)
                act.wait_ge(unit_done, at(u + 2, 6))
                A(ex_sil, wk[:, 2, :], ACT.Silu).then_inc(ex_silu, 1)
                split_high(v + 1, i)
                split_high(v + 2, i)
                split_high(v + 3, i)
                if e < NE - 1:
                    gathered(e + 1, i, 0)
                act.wait_ge(turned_ps, at(e + 1))
                A(ex_hi.rearrange("p f s -> p (f s)"), wk[:, 2, :], ACT.Copy).then_inc(turned_hi_ready, 1)
                if e < NE - 1:
                    gathered(e + 1, i, 1)
                split_high(v + 4, i)
                act.wait_ge(y0_ps, at(e + 1))
                A(y_hi[:, 0:512], wk[:, 2, :], ACT.Copy).then_inc(y_hi_ready, 1)
                act.wait_ge(unit_done, at(u + 6, 6))
                A(y_hi[:, 512:1024], wk[:, 3, :], ACT.Copy).then_inc(y_hi_ready, 1)
                split_high(v + 5, i)
            gathered(0, None, 0)
            gathered(0, None, 1)
            experts(act, expert)

            act.wait_ge(rank_ready, 1)
            with act.If(act.value_load(flag[0:1, 0:1], min_val=0, max_val=1)):
                act.wait_ge(gt_ps, 1)
                A(gT[0:NE, :], wk[0:NE, 2, 0:T], ACT.Copy).then_inc(gt_sb, 1)
                act.wait_ge(gt_sb, 1)
                act.dma_start(gates_dram, gT[0:NE, :]).then_inc(gt_out, 16)
                act.wait_ge(gt_out, 16)
                for q in range(4):
                    act.dma_start(gates[:, 8 * q:8 * q + 8, :],
                                  gates_dram[8 * q:8 * q + 8, :].rearrange("(o e) t -> o e t", o=1)
                                  .to_broadcast([P, 8, T])).then_inc(gates_in, 16)
                with act.Fori(0, NE) as i:
                    for hf in range(2):
                        act.wait_ge(fb_up, i * 2 + (hf + 1))
                        A(fb_sil.rearrange("p m t -> p (m t)"), wk[:, 0, :], ACT.Silu).then_inc(fb_silu, 1)

            def swiglu(u0, c0, n):
                v0 = split_of(u0)

                def silu(ch, i):
                    def at(v):
                        return v if i is None else i * LOOP + v
                    u = gate_unit(u0, ch)
                    act.wait_ge(unit_done, u + 1 if i is None else i * (3 * LOOP) + (u + 1))
                    if ch >= 2:
                        act.wait_ge(hidden_ready, at(c0 + ch - 1))
                    A(sil[:, ch % 2, :, :].rearrange("p m t -> p (m t)"), wk[:, 2 * (ch % 2), :],
                      ACT.Silu).then_inc(silu_ready, 1)

                def high(ch, i):
                    act.wait_ge(hidden_ready, c0 + ch + 1 if i is None else i * LOOP + (c0 + ch + 1))
                    A(hid_hi[:, ch % 2, :, :], hid[:, ch % 2, :, :], ACT.Copy).then_inc(hid_hi_ready, 1)

                def step(ch, i):
                    v = v0 + (0 if ch == 0 else 3 * ch - 1)
                    silu(ch, i)
                    split_high(v + SPLIT, i)
                    split_high(v + 1 + SPLIT, i)
                    high(ch, i)
                    if ch:
                        split_high(v + 2 + SPLIT, i)
                step(0, None)
                step(1, None)
                turns, rest = swiglu_steps(n)
                with act.Fori(0, turns) as i:
                    for j in range(LOOP):
                        step(2 + j, i)
                for s in rest:
                    step(s, None)

            norm(3, xT, 0, (resid_ready, 4, 1))
            norm(4, xT, 0, (h_scaled, 3 * KT, 2))
            split_norm(4)
            swiglu(U_F[0], C_F[0], FFC)

            norm(5, xT, 0, (resid_ready, 8, 1), after_feed(0))
            split_norm(5)
            VA = split_of(U_A) + SPLIT
            act.wait_ge(reldist_out, 16)
            act.dma_start(bias, bass.AP(reldist_dram.tensor, 0, [[1, P], [512, HEADS2], [1, 384]])).then_inc(bias_in, 16)
            take(half(qiA[:, 0:2, :]), U_A)
            split_high(VA)
            take(half(qiA[:, 2:4, :]), U_A + 1)
            split_high(VA + 1)
            b = bank(U_A + 2)
            A(kiA, b[:, 0:T], ACT.Copy)
            A(wiA, b[:, T:T + 16].rearrange("p (t h) -> p t h", t=2), ACT.Copy, scale=8 ** -0.5).then_inc(grp_out, 1)
            split_high(VA + 2)
            take(half(qA[:, 0:2, :]), U_A + 3, scale=P ** -0.5)
            split_high(VA + 3)
            for r in range(8):
                if r >= 2:
                    act.wait_ge(rel_used, r - 1)
                A(relb[:, r % 2, :], bank(), ACT.Relu, scale=64 ** -0.5).then_inc(grp_out, 1)
            for a in range(1, 4):
                take(half(qA[:, 2 * a:2 * a + 2, :]), U_A + 3 + a, scale=P ** -0.5)
                split_high(VA + 3 + a)
            for a in range(4):
                take(half(kA[:, 2 * a:2 * a + 2, :]), U_A + 7 + a)
                split_high(VA + 7 + a)
            for a in range(4):
                take(vA[:, :, a * UW:(a + 1) * UW], U_A + 11 + a, two=True)
                split_high(VA + 11 + a)

            def a_exps(h):
                act.wait_ge(a_max, h + 1)
                if h >= 2:
                    act.wait_ge(apt_ps, h - 1)
                for t in range(TT):
                    last = A(prA[:, h % 2, t, :], lgA[:, h % 2, t, :], ACT.Exp, bias=stA[:, 2 * h + t:2 * h + t + 1],
                             accum_out=stA[:, 16 + 2 * h + t:17 + 2 * h + t])
                last.then_inc(a_exp, 1)

            def a_turned(h):
                act.wait_ge(apt_ps, h + 1)
                if h >= 2:
                    act.wait_ge(apv_ps, h - 1)
                A(ptA[:, h % 2, :, :].rearrange("p k t -> p (k t)"), wk[:, 2 + h % 2, :], ACT.Copy).then_inc(apt_ready, 1)

            def a_out(h):
                act.wait_ge(apv_ps, h + 1)
                o = accf[:, (h % 2) * 512:(h % 2) * 512 + T]
                A(mixA[:, h, :], o, ACT.Copy)
                A(h_hi[:, h, :], o, ACT.Copy).then_inc(apv_ready, 1)

            a_exps(0)
            for h in range(HEADS2):
                if h + 1 < HEADS2:
                    a_exps(h + 1)
                a_turned(h)
                if h >= 1:
                    a_out(h - 1)
            a_out(HEADS2 - 1)
            for a in range(4):
                if a < 3:
                    split_high(VA + 15 + a)
                square(6, xT, a, (resid_ready, 12, 1))
            split_high(VA + 18)
            root(6, 0)
            split_norm(6)
            swiglu(U_F[1], C_F[1], FFC)
            act.wait_ge(resid_ready, 20)
            act.dma_start(wsp, b_w_sp_2[0].rearrange("g t s -> t g s")).then_inc(wsp_in, 16)
            act.dma_start(bspb, b_b_sp_2[0].rearrange("(o g) t -> o g t", o=1).to_broadcast([P, BGROUPS, P])).then_inc(wsp_in, 16)
            norm(7, xT, 0, None, after_feed(1))
            split_norm(7)
            swiglu(U_F[2], C_F[2], FFC)

            act.wait_ge(wsp_ps, 1)
            A(wspT.rearrange("p g t -> p (g t)"), wk[:, 2:4, :].rearrange("p b n -> p (b n)"), ACT.Copy).then_inc(wsp_ready, 1)
            act.dma_start(binrow, b_b_in_2[:, BH:2 * BH]).then_inc(binrow_in, 16)
            norm(8, xT, 0, (resid_ready, 20, 1), after_feed(2))
            split_norm(8)
            VB = split_of(U_B) + SPLIT
            act.wait_ge(w1_ps, 1)
            A(wsum.rearrange("p g t -> p (g t)"), wk[:, 0:2, :].rearrange("p b n -> p (b n)"), ACT.Copy).then_inc(w1_ready, 1)
            for a in range(12):
                b = bank(U_B + a)
                for t in range(TT):
                    last = A(vB[:, t, a * UW:(a + 1) * UW], b[:, t * UW:(t + 1) * UW], ACT.Gelu_apprx_tanh,
                             accum_out=stB[:, 12 * t + a:12 * t + a + 1])
                last.then_inc(grp_out, 1)
                split_high(VB + a)
            for a in range(12):
                b = bank(U_B + 12 + a)
                for m in range(2):
                    last = A(uB[:, 2 * a + m, :], b[:, m * T:(m + 1) * T], ACT.Gelu_apprx_tanh,
                             bias=bu_cols[:, 2 * a + m:2 * a + m + 1])
                last.then_inc(grp_out, 1)
                split_high(VB + 12 + a)
                if a == 0:
                    act.wait_ge(ln_mean, 1)
                if a in (0, 2, 4, 6):
                    q = a // 2
                    t, hf = divmod(q, 2)
                    if q:
                        act.wait_ge(ln_var, q)
                    A(sqB[:, 0:BH // 2], vB[:, t, hf * (BH // 2):(hf + 1) * (BH // 2)], ACT.Square,
                      bias=stB[:, 26 + t:27 + t], accum_out=stB[:, 28 + q:29 + q]).then_inc(ln_var, 1)
            act.wait_ge(ln_mean, 2)
            A(stB[:, 34:36], stB[:, 32:34], ACT.Sqrt, bias=eps_col, scale=1.0 / BH).then_inc(ln_std, 1)

            def pair_high(q):
                act.wait_ge(sp_done, q + 1)
                if q >= 2:
                    act.wait_ge(unit_done, U_BOUT + q - 1)
                A(hid_hi[:, q % 2, :, :], uB[:, 2 * q:2 * q + 2, :], ACT.Copy).then_inc(hid_hi_ready, 1)
            pair_high(0)
            pair_high(1)
            for a in range(12):
                if a < 11:
                    split_high(VB + 24 + a)
                if a + 2 < 12:
                    pair_high(a + 2)
            norm(9, xT, 0, (resid_ready, 24, 1), VB + 24 + 11)
            split_norm(9)
            swiglu(U_F[3], C_F[3], FFC)
            norm(10, xT, 0, (resid_ready, 28, 1))
            act.wait_ge(fin_ps, 1)
            A(fin[:, 0:D], accf[:, 0:D], ACT.Copy).then_inc(fin_sb, 1)
            act.wait_ge(fin_ps, 2)
            A(fin[:, D:2 * D], accf[:, D:2 * D], ACT.Copy).then_inc(fin_sb, 1)

        @block.gpsimd
        def _(pool):
            def low(dst, src, hi, ready):
                nc.gpsimd.tensor_tensor(dst, src, hi.bitcast(F32), ALU.subtract).then_inc(ready, 1)

            def split_norm(j):
                for k in range(KT):
                    pool.wait_ge(h_hi_ready, KT * j + k + 1)
                    low(h_lo[:, k, :], hT[:, k, :], h_hi[:, k, :], h_lo_ready)

            def hidden(ch0, n):
                def one(ch, i):
                    pool.wait_ge(hid_hi_ready, ch0 + ch + 1 if i is None else i * LOOP + (ch0 + ch + 1))
                    low(hid_lo[:, ch % 2, :, :], hid[:, ch % 2, :, :], hid_hi[:, ch % 2, :, :], hid_lo_ready)
                one(0, None)
                one(1, None)
                turns, rest = swiglu_steps(n)
                with pool.Fori(0, turns) as i:
                    for j in range(LOOP):
                        one(2 + j, i)
                for s in rest:
                    one(s, None)

            split_norm(0)
            for r in range(4):
                pool.wait_ge(grp_out, (1, 2, 3, 5)[r])
                if r == 0:
                    pool.wait_ge(ss_ready, 2)
                if r >= 2:
                    pool.wait_ge(rope_done, r - 1)
                nc.gpsimd.tensor_tensor(ropeb[:, r % 2, :, :], raw[:, 2 * r:2 * r + 2, :],
                                        cosT.rearrange("p (o t) -> p o t", o=1).to_broadcast([P, 2, T]),
                                        ALU.mult).then_inc(rope_cos, 1)

            pool.wait_ge(grp_out, 20)
            low(h_lo[:, 4:8, :], mixT[:, 4:8, :], h_hi[:, 4:8, :], mix_lo_ready)
            pool.wait_ge(mix_hi_ready, 1)
            low(h_lo[:, 0:4, :], mixT[:, 0:4, :], h_hi[:, 0:4, :], mix_lo_ready)
            split_norm(1)
            hidden(C_H[0], FFC)
            split_norm(2)
            for h in range(HEADS2):
                pool.wait_ge(apv_ready, h + 1)
                low(h_lo[:, h, :], mixA[:, h, :], h_hi[:, h, :], mix_lo_ready)
            split_norm(3)
            hidden(C_H[1], FFC)
            split_norm(4)

            pool.wait_ge(wsp_in, 32)
            nc.gpsimd.affine_select(out=wsp, in_=wsp, compare_op=ALU.is_ge, fill=0.0, base=0,
                                    pattern=[[0, BGROUPS], [-1, P]], channel_multiplier=1).then_inc(wsp_masked, 1)
            hidden(C_H[2], FFC)
            split_norm(5)
            for q in range(BT // 2):
                pool.wait_ge(hid_hi_ready, C_HB + q + 1)
                low(hid_lo[:, q % 2, :, :], uB[:, 2 * q:2 * q + 2, :], hid_hi[:, q % 2, :, :], hid_lo_ready)
            split_norm(6)
            hidden(C_H[3], FFC)

        @block.vector
        def _(dve):
            chain = [0]

            def link(ins):
                chain[0] += 1
                ins.then_inc(dve_step, 1)
                dve.wait_ge(dve_step, chain[0])

            V = nc.vector
            V.memset(eps_col, EPS).then_inc(const_set, 1)
            dve.wait_ge(x_ps, 1)
            V.tensor_copy(xT[:, :, :], acc[:, :, :]).then_inc(x_ready, 1)
            dve.wait_ge(cols_ready, 3)
            V.tensor_tensor(lam_prod[0:64, :], lam_cols[0:64, 0:2], lam_cols[0:64, 2:4], ALU.mult).then_inc(lamp_ready, 1)
            V.tensor_scalar(sub_g, sub_col, 1.0 - LAMBDA_INIT, None, ALU.mult)
            dve.wait_ge(lam_ps, 1)

            def modulation(lo, hi):
                for j in range(2):
                    last = V.tensor_tensor(mod[:, lo:hi, j], accf[:, 1024 + 2 * lo:1024 + 2 * hi]
                                           .rearrange("p (m j) -> p m j", j=2)[:, :, j], ada_b[:, lo:hi], ALU.add)
                link(last)
            modulation(0, 16)
            for j in range(2):
                last = V.scalar_tensor_tensor(a_mix[:, j, :], mod[:, 8:16, j], 1.0, g_mix, ALU.add, ALU.mult)
            last.then_inc(mod_ready, 1)
            dve.wait_ge(mod_ready, 1)

            def norm(n, src, dst, gcol):
                dve.wait_ge(std_ready, n + 1)
                link(V.reciprocal(rstd[:, 0:T], std[:, 0:T]))
                for k in range(KT):
                    V.scalar_tensor_tensor(dst[:, k, :], src[:, k, :], gcol[:, k:k + 1], rstd[:, 0:T],
                                           ALU.mult, ALU.mult).then_inc(h_scaled, 1)

            norm(0, cT, hcT, a_mix[:, 1, :])
            norm(1, xT, hT, a_mix[:, 0, :])
            for v in range(SPLIT):
                split_low(v)
            dve.wait_ge(lame_ready, 1)
            link(V.tensor_tensor(neg_lam, lam_exp[:, 1:2], lam_exp[:, 0:1], ALU.subtract))
            link(V.tensor_scalar(neg_lam, neg_lam, -LAMBDA_INIT, None, ALU.add))
            V.tensor_copy(lam_prod[:, 0:1], neg_lam).then_inc(lam_ready, 1)

            for v in range(SPLIT, 8):
                split_low(v)

            for r in range(4):
                dve.wait_ge(rope_ps, r + 1)
                dve.wait_ge(rope_cos, r + 1)
                tmp = ropea[:, r % 2, :, :]
                link(V.tensor_tensor(tmp, accf[:, r * 512:(r + 1) * 512].rearrange("p (k t) -> p k t", k=2),
                                     sinT.rearrange("p (o t) -> p o t", o=1).to_broadcast([P, 2, T]), ALU.mult))
                dst = qT[:, 2 * r:2 * r + 2, :] if r < 2 else kT[:, 2 * r - 4:2 * r - 2, CTX:CTX + T]
                V.tensor_tensor(dst, tmp, ropeb[:, r % 2, :, :], ALU.add).then_inc(rope_done, 1)

            def maxima(s):
                dve.wait_ge(sc_ps, s + 1)
                link(V.tensor_reduce(out=nmax[:, s, :], in_=wk[:, 2 * (s % 2):2 * (s % 2) + 2, :], op=ALU.max, axis=AX_X))
                V.tensor_scalar(nbias[:, s, :], nmax[:, s, :], -(HD1 ** -0.5), None, ALU.mult).then_inc(max_ready, 1)

            def combine(s):
                dve.wait_ge(exp_ready, s + 1)
                if s >= 2:
                    dve.wait_ge(at_ps, s - 1)
                link(V.reciprocal(rsum[:, s, :], sums[:, s, :]))
                link(V.tensor_tensor(rsum[:, s, 1:2], rsum[:, s, 1:2], neg_lam, ALU.mult))
                link(V.tensor_scalar(prob[:, s % 2, 1, :], prob[:, s % 2, 1, :], rsum[:, s, 1:2], None, ALU.mult))
                V.scalar_tensor_tensor(attn[:, s % 2, :], prob[:, s % 2, 0, :], rsum[:, s, 0:1], prob[:, s % 2, 1, :],
                                       ALU.mult, ALU.add).then_inc(attn_ready, 1)
            maxima(0)
            for s in range(8):
                if s + 1 < 8:
                    maxima(s + 1)
                combine(s)
            dve.wait_ge(unit_done, U_OUT)
            modulation(16, 48)
            for v in range(8, 11):
                split_low(v)
            dve.wait_ge(sub_std, 1)
            link(V.reciprocal(rstdh[:, :], stdh[:, :]))
            for h in range(HEADS1):
                last = V.scalar_tensor_tensor(mixT[:, h, :], heads_o[:, h, :], sub_g, rstdh[:, h * T:(h + 1) * T],
                                              ALU.mult, ALU.mult)
            last.then_inc(sub_done, 1)
            V.scalar_tensor_tensor(a_ffn, mod[:, 32:40, 0], 1.0, g_ffn, ALU.add, ALU.mult).then_inc(mod_ready, 1)
            dve.wait_ge(mod_ready, 2)
            for a in range(4):
                dve.wait_ge(unit_done, U_OUT + a + 1)
                for m in (2 * a, 2 * a + 1):
                    last = V.scalar_tensor_tensor(xT[:, m, :], acc[:, m, :], mod[:, 16 + m, 0:1], xT[:, m, :],
                                                  ALU.mult, ALU.add)
                last.then_inc(resid_ready, 1)
                if a == 0:
                    split_low(11)
            norm(2, xT, hT, a_ffn)
            dve.wait_ge(rt_sb, 1)

            dve.wait_ge(rt_sb, 1)
            for t in range(TT):
                e0 = 80 * t
                gmax, gneg, gsum = rt[:, 344 + t:345 + t], rt[:, 336 + t:337 + t], rt[:, 338 + t:339 + t]
                eneg, e2 = rt[:, 340 + t:341 + t], rt[:, 342 + t:343 + t]
                first = rt[:, 348 + t:349 + t]
                pick = rt[:, 352 + 4 * t:356 + 4 * t]
                off = rt[:, 360 + 4 * t:364 + 4 * t]
                t8 = rt[:, 320 + 8 * t:328 + 8 * t]
                link(V.tensor_reduce(out=gmax, in_=lg[:, t, 0:4], op=ALU.max, axis=AX_X))
                V.tensor_scalar(gneg, gmax, -1.0, None, ALU.mult)
                link(V.scalar_tensor_tensor(pick, lg[:, t, 0:4], gmax, groups[:, 0:4], ALU.is_equal, ALU.mult))
                link(V.tensor_reduce(out=first, in_=pick, op=ALU.min, axis=AX_X))
                link(V.tensor_scalar(pick, groups[:, 0:4], first, None, ALU.is_equal))
                link(V.tensor_scalar(off, pick, 1.0e30, -1.0e30, ALU.mult, ALU.add))
                V.memset(rt[:, e0 + 32:e0 + 40], -2.0e30)
                for gr in range(4):
                    last = V.tensor_scalar(rt[:, e0 + 8 * gr:e0 + 8 * gr + 8], lg[:, t, 4 + 8 * gr:12 + 8 * gr],
                                           pick[:, gr:gr + 1], off[:, gr:gr + 1], ALU.mult, ALU.add)
                link(last)
                link(V.max(t8, rt[:, e0:e0 + 32]))
                last = V.tensor_scalar(eneg, t8[:, 0:1], -1.0, None, ALU.mult)
                if t == TT - 1:
                    last.then_inc(rt_max, 1)
            dve.wait_ge(rt_exp, 1)
            for t in range(TT):
                e0 = 80 * t
                t8 = rt[:, 320 + 8 * t:328 + 8 * t]
                gsum, e2 = rt[:, 338 + t:339 + t], rt[:, 342 + t:343 + t]
                link(V.memset(t8[:, 2:8], -2.0e30))
                link(V.match_replace(out=rt[:, e0:e0 + 40], in_to_replace=t8, in_values=rt[:, e0:e0 + 40], imm_value=3.0e30))
                link(V.tensor_scalar(rt[:, e0:e0 + 32], rt[:, e0:e0 + 32], 2.0e30, None, ALU.is_ge))
                link(V.scalar_tensor_tensor(e2, e2, 1.0, gsum, ALU.add, ALU.mult))
                link(V.reciprocal(e2, e2))
                last = V.scalar_tensor_tensor(rt[:, 256 + 32 * t:288 + 32 * t], rt[:, e0 + 40:e0 + 72], e2,
                                              rt[:, e0:e0 + 32], ALU.mult, ALU.mult)
            last.then_inc(rt_g, 1)
            dve.wait_ge(rt_g, 1)
            link(V.tensor_copy(gate_parts[:, 0, :, :], r_gate))
            V.tensor_tensor(gate_parts[:, 1, :, :], r_gate, gate_parts[:, 0, :, :].bitcast(F32),
                            ALU.subtract).then_inc(gates_split, 1)
            V.tensor_copy(ident_r, ident)
            dve.wait_ge(h2_hi_ready, 1)
            V.tensor_tensor(h2_lo.rearrange("p t d -> p (t d)"), accf,
                            h2_hi.rearrange("p t d -> p (t d)").bitcast(F32), ALU.subtract).then_inc(h2_ready, 1)
            dve.wait_ge(rank_ps, 1)
            for t in range(TT):
                last = V.scalar_tensor_tensor(rank[:, t, :], wk[:, 3, NE * t:NE * (t + 1)], 1.0, rt[:, 80 * t:80 * t + NE],
                                              ALU.add, ALU.mult)
            link(last)
            link(V.tensor_scalar(rank, rank, -1.0, None, ALU.add))
            V.scalar_tensor_tensor(over, rank, float(TAKES), rt[:, 256:320].rearrange("p (t e) -> p t e", t=TT),
                                   ALU.is_ge, ALU.mult)
            link(V.tensor_reduce(out=most, in_=wk[:, 3, 64:64 + NE], op=ALU.max, axis=AX_X))
            V.tensor_scalar(flag[:, :], most, float(TAKES), None, ALU.is_gt).then_inc(rank_ready, 1)

            def choose(e, i):
                at = e if i is None else i * 2 + e
                for t in range(TT):
                    V.tensor_scalar(pick_at[:, e % 2, t, :], slots, r_rank[:, at, t:t + 1], None, ALU.is_equal)
                V.tensor_copy(gate_pick[:, e % 2, :, :].rearrange("p t h -> p h t"),
                              gate_parts[:, :, at, :]).then_inc(pick_ready, 1)

            def gathered(e, i, half):
                n = 2 * e + half + 1
                dve.wait_ge(xg_lo_ps, n if i is None else i * 4 + n)
                V.tensor_copy(xg_lo[:, 4 * half:4 * half + 4, :].rearrange("p k s -> p (k s)"),
                              wk[:, 1, :]).then_inc(xg_lo_ready, 1)

            def turned_pick(e, i):
                dve.wait_ge(spread_ps, e + 1 if i is None else i * 2 + (e + 1))
                V.tensor_copy(spread[:, e % 2, :], wk[:, 0, 0:T])
                V.tensor_reduce(out=slot_gate[:, e % 2:e % 2 + 1], in_=wk[:, 0, T:T + 2], op=ALU.add,
                                axis=AX_X).then_inc(spread_ready, 1)

            def results(e, i, half):
                n = 2 * e + half + 1
                dve.wait_ge(y_hi_ready, n if i is None else i * 4 + n)
                c = slice(half * 512, (half + 1) * 512)
                V.tensor_tensor(y_lo[:, c], wk[:, 2 + half, :], y_hi[:, c].bitcast(F32),
                                ALU.subtract).then_inc(y_lo_ready, 1)

            def expert(e, i):
                def at(v, n=1):
                    return v if i is None else i * (2 * n) + v
                u = U_MOE + 6 * e
                v = split_of(u) + SPLIT
                if e < NE - 1:
                    choose(e + 1, i)
                for a in range(3):
                    split_low(v + a, i)
                dve.wait_ge(ex_silu, at(e + 1))
                dve.wait_ge(unit_done, at(u + 4, 6))
                dve.wait_ge(spread_ready, at(e + 1))
                V.scalar_tensor_tensor(ex_rows, wk[:, 3, :], slot_gate[:, e % 2:e % 2 + 1], ex_sil, ALU.mult,
                                       ALU.mult).then_inc(ex_hidden, 1)
                if e < NE - 1:
                    gathered(e + 1, i, 0)
                dve.wait_ge(turned_hi_ready, at(e + 1))
                V.tensor_tensor(ex_lo.rearrange("p f s -> p (f s)"), wk[:, 2, :],
                                ex_hi.rearrange("p f s -> p (f s)").bitcast(F32),
                                ALU.subtract).then_inc(turned_lo_ready, 1)
                if e < NE - 1:
                    gathered(e + 1, i, 1)
                split_low(v + 3, i)
                results(e, i, 0)
                results(e, i, 1)
                split_low(v + 4, i)
                if e < NE - 1:
                    turned_pick(e + 1, i)
                split_low(v + 5, i)
            dve.wait_ge(rank_ready, 1)
            dve.wait_ge(gates_split, 1)
            choose(0, None)
            for v in range(12, 12 + SPLIT):
                split_low(v)
            for half in range(2):
                gathered(0, None, half)
            turned_pick(0, None)
            experts(dve, expert)
            dve.wait_ge(spread_done, NE)
            with dve.If(dve.value_load(flag[0:1, 0:1], min_val=0, max_val=1)):
                dve.wait_ge(gates_in, 64)
                with dve.Fori(0, NE) as i:
                    for half in range(2):
                        n = i * 2 + (half + 1)
                        dve.wait_ge(fb_silu, n)
                        V.tensor_tensor(fb_prod, fb_sil, wk[:, 1, :].rearrange("p (m t) -> p m t", m=2),
                                        ALU.mult).then_inc(fb_mul, 1)
                        dve.wait_ge(fb_mul, n)
                        for m in range(2):
                            last = V.tensor_tensor(fb_hid[:, m, :], fb_prod[:, m, :], gates[:, i, :], ALU.mult)
                        last.then_inc(fb_hidden, 1)
                dve.wait_ge(fb_down, 2 * NE + 1)

            def swiglu(u0, c0, ch0, n):
                v0 = split_of(u0)

                def hidden(ch, i):
                    def at(v):
                        return v if i is None else i * LOOP + v
                    dve.wait_ge(silu_ready, at(c0 + ch + 1))
                    u = gate_unit(u0, ch) + 1
                    dve.wait_ge(unit_done, u + 1 if i is None else i * (3 * LOOP) + (u + 1))
                    if ch >= 2:
                        dve.wait_ge(hid_lo_ready, at(ch0 + ch - 1))
                    V.tensor_tensor(hid[:, ch % 2, :, :], sil[:, ch % 2, :, :],
                                    wk[:, 2 * (ch % 2) + 1, :].rearrange("p (m t) -> p m t", m=2),
                                    ALU.mult).then_inc(hidden_ready, 1)

                def step(ch, i):
                    v = v0 + (0 if ch == 0 else 3 * ch - 1)
                    split_low(v + SPLIT, i)
                    hidden(ch, i)
                    split_low(v + 1 + SPLIT, i)
                    if ch:
                        split_low(v + 2 + SPLIT, i)
                step(0, None)
                step(1, None)
                turns, rest = swiglu_steps(n)
                with dve.Fori(0, turns) as i:
                    for j in range(LOOP):
                        step(2 + j, i)
                for s in rest:
                    step(s, None)
                dve.wait_ge(unit_done, u0 + 3 * n)
            for m in range(KT):
                last = V.scalar_tensor_tensor(xT[:, m, :], acc[:, m, :], mod[:, 40 + m, 0:1], xT[:, m, :],
                                              ALU.mult, ALU.add)
                if m % 2:
                    last.then_inc(resid_ready, 1)
            norm(3, xT, xT, g_fin)
            dve.wait_ge(h_scaled, 4 * KT)
            norm(4, xT, hT, norm2[:, 0:8])

            def feed(n):
                swiglu(U_F[n], C_F[n], C_H[n], FFC)
                for m in range(0, KT, 2):
                    V.scalar_tensor_tensor(xT[:, m:m + 2, :], acc[:, m:m + 2, :], 0.5, xT[:, m:m + 2, :],
                                           ALU.mult, ALU.add).then_inc(resid_ready, 1)
            feed(0)

            norm(5, xT, hT, norm2[:, 8:16])
            split_low(after_feed(0))
            VA = split_of(U_A) + SPLIT
            for a in range(4):
                split_low(VA + a)
            link(V.memset(score.rearrange("p t k -> p (t k)"), 0.0))
            g0 = 20
            r = 0
            for t in range(TT):
                for pair in range(2):
                    for odd in range(2):
                        dve.wait_ge(grp_out, g0 + 5 + r)
                        for j in range(2):
                            h = 4 * pair + 2 * j + odd
                            ins = V.scalar_tensor_tensor(score[:, t, :], relb[:, r % 2, j * T:(j + 1) * T],
                                                         wiA[:, t, h:h + 1], score[:, t, :], ALU.mult, ALU.add)
                            if j == 0:
                                link(ins)
                        ins.then_inc(rel_used, 1)
                        r += 1
                        dve.wait_ge(rel_used, r)
            link(V.tensor_tensor(score, score, causal, ALU.add))
            for q in range(TOPK // 8):
                split_low(VA + 4 + q)
                for t in range(TT):
                    last = V.max(top8[:, t, :], score[:, t, :])
                link(last)
                for t in range(TT):
                    last = V.match_replace(out=score[:, t, :], in_to_replace=top8[:, t, :], in_values=score[:, t, :],
                                           imm_value=TAKEN)
                link(last)
            link(V.tensor_scalar(amask, score, 2.0 * FAR, FAR, ALU.is_gt, ALU.mult))
            V.tensor_tensor(amask, amask, causal, ALU.min).then_inc(mask_ready, 1)
            for a in range(12, 15):
                split_low(VA + a)
            dve.wait_ge(mask_ready, 1)

            def a_maxima(h):
                dve.wait_ge(a_ps, h + 1)
                if h >= 2:
                    dve.wait_ge(a_exp, h - 1)
                link(V.tensor_tensor(lgA[:, h % 2, :, :], wk[:, h % 2, :].rearrange("p (t k) -> p t k", t=2), amask,
                                     ALU.add))
                link(V.tensor_reduce(out=stA[:, 32 + 2 * h:34 + 2 * h], in_=lgA[:, h % 2, :, :], op=ALU.max, axis=AX_X))
                V.tensor_scalar(stA[:, 2 * h:2 * h + 2], stA[:, 32 + 2 * h:34 + 2 * h], -1.0, None,
                                ALU.mult).then_inc(a_max, 1)

            def a_normal(h):
                dve.wait_ge(a_exp, h + 1)
                link(V.reciprocal(stA[:, 48 + 2 * h:50 + 2 * h], stA[:, 16 + 2 * h:18 + 2 * h]))
                for t in range(TT):
                    last = V.tensor_scalar(prA[:, h % 2, t, :], prA[:, h % 2, t, :],
                                           stA[:, 48 + 2 * h + t:49 + 2 * h + t], None, ALU.mult)
                last.then_inc(a_norm, 1)
            a_maxima(0)
            for h in range(HEADS2):
                if h + 1 < HEADS2:
                    a_maxima(h + 1)
                a_normal(h)
            for a in range(4):
                dve.wait_ge(unit_done, U_AOUT + a + 1)
                last = V.tensor_tensor(xT[:, 2 * a:2 * a + 2, :], acc[:, 2 * a:2 * a + 2, :],
                                       xT[:, 2 * a:2 * a + 2, :], ALU.add)
                last.then_inc(resid_ready, 1)
                if a < 3:
                    split_low(VA + 15 + a)
            norm(6, xT, hT, norm2[:, 16:24])
            split_low(VA + 18)
            feed(1)
            norm(7, xT, hT, norm2[:, 24:32])
            split_low(after_feed(1))
            feed(2)

            norm(8, xT, hT, norm2[:, 32:40])
            split_low(after_feed(2))
            dve.wait_ge(w1_ready, 1)
            VB = split_of(U_B) + SPLIT
            for a in range(12):
                split_low(VB + a)
                for f in (2 * a, 2 * a + 1):
                    V.scalar_tensor_tensor(affB[:, f, :], wsum[:, f // 3, :], lnb_cols[:, f:f + 1], bspb[:, f // 3, :],
                                           ALU.mult, ALU.add)
            dve.wait_ge(grp_out, 43 + 12)
            link(V.tensor_reduce(out=stB[:, 24:26], in_=stB[:, 0:24].rearrange("p (t a) -> p t a", t=2),
                                 op=ALU.add, axis=AX_X))
            V.tensor_scalar(stB[:, 26:28], stB[:, 24:26], -1.0 / BH, None, ALU.mult).then_inc(ln_mean, 1)
            for a in range(12, 21):
                split_low(VB + a)
            dve.wait_ge(ln_var, 4)
            V.tensor_reduce(out=stB[:, 32:34], in_=stB[:, 28:32].rearrange("p (t a) -> p t a", t=2),
                            op=ALU.add, axis=AX_X).then_inc(ln_mean, 1)
            split_low(VB + 21)
            split_low(VB + 22)
            split_low(VB + 23)
            dve.wait_ge(ln_std, 1)
            link(V.reciprocal(stB[:, 36:38], stB[:, 34:36]))
            for t in range(TT):
                V.tensor_scalar(vB[:, t, :], vB[:, t, :], stB[:, 26 + t:27 + t], stB[:, 36 + t:37 + t],
                                ALU.add, ALU.mult).then_inc(ln_ready, 1)
            dve.wait_ge(grp_out, 43 + 24)

            def spatial(q):
                dve.wait_ge(sp_ps, q + 1)
                for j in range(2):
                    f = 2 * q + j
                    y = spb[:, j, :, :]
                    last = V.scalar_tensor_tensor(
                        y, wk[:, q % 4, j * T:(j + 1) * T].rearrange("p (t k) -> p t k", t=2), lng_cols[:, f:f + 1],
                        affB[:, f, :].rearrange("p (o t) -> p o t", o=1).to_broadcast([P, 2, P]), ALU.mult, ALU.add)
                link(last)
                V.tensor_tensor(uB[:, 2 * q:2 * q + 2, :], uB[:, 2 * q:2 * q + 2, :],
                                spb[:, :, :, :].rearrange("p j t k -> p j (t k)"), ALU.mult).then_inc(sp_done, 1)
                dve.wait_ge(sp_done, q + 1)
            spatial(0)
            spatial(1)
            for a in range(12):
                if a < 11:
                    split_low(VB + 24 + a)
                if a + 2 < 12:
                    spatial(a + 2)
            dve.wait_ge(unit_done, U_BOUT + 12)
            for m in range(0, KT, 2):
                V.tensor_tensor(xT[:, m:m + 2, :], acc[:, m:m + 2, :], xT[:, m:m + 2, :],
                                ALU.add).then_inc(resid_ready, 1)
            norm(9, xT, hT, norm2[:, 40:48])
            split_low(VB + 24 + 11)
            feed(3)
            norm(10, xT, hT, g_fin2)
    return nc


_INS = ["x", "c", "ctx", "c_ctx", "w_ada", "b_ada", "g_mix_norm", "g_ffn_norm", "w_in", "lambda_q1", "lambda_k1",
        "lambda_q2", "lambda_k2", "g_subln", "w_fourier", "w_out", "w_router_group", "b_router_group",
        "w_router_expert", "b_router_expert", "w_gate", "w_up", "w_down", "g_final", "norm_g_2", "final_g_2",
        "ffn_w_in_2", "ffn_w_out_2", "rel_table_2", "a_w_in_2", "a_w_out_2", "b_w_in_2", "b_b_in_2", "b_ln_g_2",
        "b_ln_b_2", "b_w_sp_2", "b_b_sp_2", "b_w_out_2"]


def kernel(**inputs):
    import numpy as _np
    import concourse.bacc as _bacc
    from concourse import mybir as _mybir
    from concourse.bass_utils import run_bass_kernel_spmd as _run

    nc = _bacc.Bacc("TRN2", target_bir_lowering=False, num_devices=1, dynamic_dma_scratch_size=1024)
    arrays, args = {}, {}
    for name in _INS:
        a = _np.ascontiguousarray(inputs[name])
        arrays[f"in_{name}_dram"] = a
        args[name] = nc.dram_tensor(f"in_{name}_dram", a.shape, _mybir.dt.from_np(a.dtype),
                                    kind="ExternalInput").ap()
    table = constants()
    arrays["in_consts_dram"] = table
    args["consts"] = nc.dram_tensor("in_consts_dram", table.shape, _mybir.dt.float32, kind="ExternalInput").ap()
    out = nc.dram_tensor("out_0_dram", (1, T, D), _mybir.dt.float32, kind="ExternalOutput").ap()
    build(nc, out=out, **args)
    r = _run(nc, [arrays], core_ids=[0])
    return r.results[0]["out_0_dram"]
```
